# Optimizing a Trainium2 kernel written in Bass

```python
import jax
import jax.numpy as jnp
from jax import lax
import numpy as np

D_MODEL = 1024
BATCH = 1
SEQ = 512
DEPTH = 2

GRID_W = 64
CTX_LEN = 256
D_MIX = D_MODEL
D_MLSTM = D_MIX // 2
N_HEADS = 4
HEAD_DIM = D_MLSTM // N_HEADS
D_CONV = D_MIX - D_MLSTM
CONV_WIDTH = 31
D_FF = 2816
CHUNK = 64
N_MOD = 9
EPS = 1e-6
FGATE_BIAS_LO = 3.0
FGATE_BIAS_HI = 6.0
GATE_W_SCALE = 0.1

Q0 = 0
K0 = Q0 + D_MLSTM
V0 = K0 + D_MLSTM
O0 = V0 + D_MLSTM
G0 = O0 + D_MLSTM
U0 = G0 + 4 * N_HEADS
D_IN = U0 + 2 * D_CONV

kernel_name = 'hybrid_mlstm_conformer_macaron_dit'

def rmsnorm(x, g):
    xf = x.astype(jnp.float32)
    y = xf * lax.rsqrt(jnp.mean(jnp.square(xf), axis=-1, keepdims=True) + EPS)
    return (y * g.astype(jnp.float32)).astype(x.dtype)

def layernorm(x, g, b):
    xf = x.astype(jnp.float32)
    mu = jnp.mean(xf, axis=-1, keepdims=True)
    var = jnp.mean(jnp.square(xf - mu), axis=-1, keepdims=True)
    y = (xf - mu) * lax.rsqrt(var + EPS)
    return (y * g.astype(jnp.float32) + b.astype(jnp.float32)).astype(x.dtype)

def modulate(h, shift, scale):
    return h * (1.0 + scale) + shift

def swiglu(h, w_up, w_down):
    g, u = jnp.split(h @ w_up, 2, axis=-1)
    return (jax.nn.silu(g) * u) @ w_down

def mixer_project(u, w_in, b_in):
    p = u @ w_in + b_in
    B_, S_, _ = p.shape

    def heads(a):
        return a.reshape(B_, S_, N_HEADS, HEAD_DIM).transpose(0, 2, 1, 3).astype(jnp.float32)

    q = heads(p[..., Q0:K0]) * (HEAD_DIM ** -0.5)
    k = heads(p[..., K0:V0])
    v = heads(p[..., V0:O0])
    o = p[..., O0:G0]
    gates = p[..., G0:U0].astype(jnp.float32).reshape(B_, S_, 4, N_HEADS).transpose(2, 0, 3, 1)
    glu = p[..., U0:]
    return q, k, v, o, gates, glu

def init_state(b):
    return (jnp.zeros((b, N_HEADS, HEAD_DIM, HEAD_DIM), jnp.float32),
            jnp.zeros((b, N_HEADS, HEAD_DIM), jnp.float32),
            jnp.zeros((b, N_HEADS), jnp.float32))

def mlstm_scan(q, k, v, log_i, log_f, state):
    B_, H_, S_, Dh = q.shape
    nc = S_ // CHUNK

    def to_chunks(a):
        return jnp.moveaxis(a.reshape((B_, H_, nc, CHUNK) + a.shape[3:]), 2, 0)

    xs = (to_chunks(q), to_chunks(k), to_chunks(v), to_chunks(log_i), to_chunks(log_f))
    lower = jnp.tril(jnp.ones((CHUNK, CHUNK), dtype=bool))

    def step(carry, inp):
        C, n, m = carry
        qc, kc, vc, li, lf = inp
        b = jnp.cumsum(lf, axis=-1)
        dmat = b[..., :, None] - b[..., None, :] + li[..., None, :]
        dmat = jnp.where(lower, dmat, -jnp.inf)
        a = b + m[..., None]
        m_t = jnp.maximum(a, jnp.max(dmat, axis=-1))
        w = jnp.exp(dmat - m_t[..., None])
        inter = jnp.exp(a - m_t)
        s = jnp.einsum('bhtd,bhsd->bhts', qc, kc) * w
        num = jnp.einsum('bhts,bhse->bhte', s, vc) + inter[..., None] * jnp.einsum('bhtd,bhde->bhte', qc, C)
        den = jnp.sum(s, axis=-1) + inter * jnp.einsum('bhtd,bhd->bht', qc, n)
        den = jnp.maximum(jnp.abs(den), jnp.exp(-m_t))
        h = num / den[..., None]
        b_last = b[..., -1]
        g = b_last[..., None] - b + li
        m_new = jnp.maximum(b_last + m, jnp.max(g, axis=-1))
        wk = jnp.exp(g - m_new[..., None])
        decay = jnp.exp(b_last + m - m_new)
        C_new = decay[..., None, None] * C + jnp.einsum('bhs,bhsd,bhse->bhde', wk, kc, vc)
        n_new = decay[..., None] * n + jnp.einsum('bhs,bhsd->bhd', wk, kc)
        return (C_new, n_new, m_new), h

    state, hs = lax.scan(step, state, xs)
    h = jnp.moveaxis(hs, 0, 2).reshape(B_, H_, S_, Dh)
    return h, state

def mlstm_bidir(q, k, v, gates, init_fwd, init_bwd):
    li_f = gates[0]
    lf_f = jax.nn.log_sigmoid(gates[1])
    li_b = gates[2]
    lf_b = jax.nn.log_sigmoid(gates[3])
    h_f, st_f = mlstm_scan(q, k, v, li_f, lf_f, init_fwd)

    def flip(a):
        return jnp.flip(a, axis=2)

    h_b, st_b = mlstm_scan(flip(q), flip(k), flip(v), flip(li_b), flip(lf_b), init_bwd)
    return h_f + flip(h_b), st_f, st_b

def mlstm_out(h, o, g):
    B_, H_, S_, Dh = h.shape
    hn = h * lax.rsqrt(jnp.mean(jnp.square(h), axis=-1, keepdims=True) + EPS)
    hn = hn.transpose(0, 2, 1, 3).reshape(B_, S_, H_ * Dh) * g.astype(jnp.float32)
    return hn.astype(o.dtype) * jax.nn.sigmoid(o)

def conv_latent(z, w, b):
    B_, S_, Dc = z.shape
    rows = S_ // GRID_W
    half = Dc // 2
    z = z.reshape(B_, rows, GRID_W, Dc)
    dn = ('NHWC', 'HWIO', 'NHWC')
    zh = lax.conv_general_dilated(z[..., :half], w[:, :half].reshape(1, CONV_WIDTH, 1, half),
                                  (1, 1), 'SAME', dimension_numbers=dn, feature_group_count=half)
    zv = lax.conv_general_dilated(z[..., half:], w[:, half:].reshape(CONV_WIDTH, 1, 1, Dc - half),
                                  (1, 1), 'SAME', dimension_numbers=dn, feature_group_count=Dc - half)
    return jnp.concatenate([zh, zv], axis=-1).reshape(B_, S_, Dc) + b

def conv_context(z, w, b):
    Dc = z.shape[-1]
    y = lax.conv_general_dilated(z, w.reshape(CONV_WIDTH, 1, Dc), (1,), 'SAME',
                                 dimension_numbers=('NWC', 'WIO', 'NWC'), feature_group_count=Dc)
    return y + b

def head_group_mix(h, o, glu, conv_fn, mlstm_g, conv_w, conv_b, cn_g, cn_b, w_out):
    y_m = mlstm_out(h, o, mlstm_g)
    a, gl = jnp.split(glu, 2, axis=-1)
    z = conv_fn(a * jax.nn.sigmoid(gl), conv_w, conv_b)
    y_c = jax.nn.silu(layernorm(z, cn_g, cn_b))
    return jnp.concatenate([y_m, y_c], axis=-1) @ w_out

def setup_inputs(seed: int = 0) -> dict:
    key = jax.random.key(seed)
    ks = jax.random.split(key, 22)

    def nrm(k, shape, s):
        return jax.random.normal(k, shape, jnp.float32) * s

    def gain(k, shape):
        return 1.0 + nrm(k, shape, 0.02)

    D = D_MODEL
    f_bias = jnp.linspace(FGATE_BIAS_LO, FGATE_BIAS_HI, N_HEADS, dtype=jnp.float32)
    w_in = nrm(ks[10], (DEPTH, D, D_IN), D ** -0.5)
    w_in = w_in.at[:, :, G0:U0].multiply(GATE_W_SCALE)
    b_in = nrm(ks[11], (DEPTH, D_IN), 0.02)
    b_in = b_in.at[:, G0 + N_HEADS:G0 + 2 * N_HEADS].add(f_bias)
    b_in = b_in.at[:, G0 + 3 * N_HEADS:G0 + 4 * N_HEADS].add(f_bias)
    return {
        'x': nrm(ks[0], (BATCH, SEQ, D), 1.0),
        'c': nrm(ks[1], (BATCH, D), 1.0),
        'ctx': nrm(ks[2], (BATCH, CTX_LEN, D), 1.0),
        'c_ctx': nrm(ks[3], (D,), 1.0),
        'w_mod': nrm(ks[4], (DEPTH, D, N_MOD * D), 0.5 * D ** -0.5),
        'b_mod': nrm(ks[5], (DEPTH, N_MOD * D), 0.02),
        'norm_ffn1': gain(ks[6], (DEPTH, D)),
        'ffn1_up': nrm(ks[7], (DEPTH, D, 2 * D_FF), D ** -0.5),
        'ffn1_down': nrm(ks[8], (DEPTH, D_FF, D), D_FF ** -0.5),
        'norm_mix': gain(ks[9], (DEPTH, D)),
        'w_in': w_in,
        'b_in': b_in,
        'mlstm_norm': gain(ks[12], (DEPTH, D_MLSTM)),
        'conv_w': nrm(ks[13], (DEPTH, CONV_WIDTH, D_CONV), CONV_WIDTH ** -0.5),
        'conv_b': nrm(ks[14], (DEPTH, D_CONV), 0.02),
        'conv_norm_g': gain(ks[15], (DEPTH, D_CONV)),
        'conv_norm_b': nrm(ks[16], (DEPTH, D_CONV), 0.02),
        'w_out': nrm(ks[17], (DEPTH, D_MIX, D), D_MIX ** -0.5),
        'norm_ffn2': gain(ks[18], (DEPTH, D)),
        'ffn2_up': nrm(ks[19], (DEPTH, D, 2 * D_FF), D ** -0.5),
        'ffn2_down': nrm(ks[20], (DEPTH, D_FF, D), D_FF ** -0.5),
        'norm_final': gain(ks[21], (D,)),
    }

def reference(x, c, ctx, c_ctx, w_mod, b_mod, norm_ffn1, ffn1_up, ffn1_down, norm_mix, w_in, b_in,
              mlstm_norm, conv_w, conv_b, conv_norm_g, conv_norm_b, w_out, norm_ffn2, ffn2_up,
              ffn2_down, norm_final):
    B_ = x.shape[0]
    D = x.shape[-1]
    xc = ctx
    sc = jax.nn.silu(c)
    scc = jax.nn.silu(c_ctx)
    for l in range(DEPTH):
        last = l == DEPTH - 1
        mod = (sc @ w_mod[l] + b_mod[l]).reshape(B_, 1, N_MOD, D)
        mod_c = (scc @ w_mod[l] + b_mod[l]).reshape(1, 1, N_MOD, D)
        m = [mod[:, :, j] for j in range(N_MOD)]
        mc = [mod_c[:, :, j] for j in range(N_MOD)]

        x = x + 0.5 * m[2] * swiglu(modulate(rmsnorm(x, norm_ffn1[l]), m[0], m[1]), ffn1_up[l], ffn1_down[l])
        xc = xc + 0.5 * mc[2] * swiglu(modulate(rmsnorm(xc, norm_ffn1[l]), mc[0], mc[1]), ffn1_up[l], ffn1_down[l])

        u = modulate(rmsnorm(x, norm_mix[l]), m[3], m[4])
        uc = modulate(rmsnorm(xc, norm_mix[l]), mc[3], mc[4])
        q, k, v, o, gates, glu = mixer_project(u, w_in[l], b_in[l])
        qc, kc, vc, oc, gatesc, gluc = mixer_project(uc, w_in[l], b_in[l])
        zero = init_state(B_)
        hc, st_f, st_b = mlstm_bidir(qc, kc, vc, gatesc, zero, zero)
        h, _, _ = mlstm_bidir(q, k, v, gates, st_f, st_b)
        y = head_group_mix(h, o, glu, conv_latent, mlstm_norm[l], conv_w[l], conv_b[l],
                           conv_norm_g[l], conv_norm_b[l], w_out[l])
        x = x + m[5] * y
        if not last:
            yc = head_group_mix(hc, oc, gluc, conv_context, mlstm_norm[l], conv_w[l], conv_b[l],
                                conv_norm_g[l], conv_norm_b[l], w_out[l])
            xc = xc + mc[5] * yc

        x = x + 0.5 * m[8] * swiglu(modulate(rmsnorm(x, norm_ffn2[l]), m[6], m[7]), ffn2_up[l], ffn2_down[l])
        if not last:
            xc = xc + 0.5 * mc[8] * swiglu(modulate(rmsnorm(xc, norm_ffn2[l]), mc[6], mc[7]), ffn2_up[l], ffn2_down[l])
    return rmsnorm(x, norm_final)


_drawn_inputs = setup_inputs


def setup_inputs(seed=0):
    import zlib

    import numpy as np

    out = dict(_drawn_inputs(seed))
    spreads = {}
    factors = {'norm_ffn1': 8.0,
     'norm_mix': 19.415,
     'mlstm_norm': 64.0,
     'conv_b': 35.16,
     'conv_norm_g': 64.0,
     'conv_norm_b': 64.0,
     'norm_ffn2': 8.0,
     'norm_final': 7.595}
    for name, (base, spread) in spreads.items():
        noise = np.random.default_rng([zlib.crc32(name.encode()), seed]).standard_normal(out[name].shape)
        drawn = base * np.exp(spread * noise) if base else spread * noise
        out[name] = jnp.asarray(drawn.astype(out[name].dtype))
    for name, factor in factors.items():
        out[name] = (out[name] * factor).astype(out[name].dtype)
    return out
```

```python
import concourse.bass as bass
from concourse import mybir
from contextlib import ExitStack

F32 = mybir.dt.float32
F32R = mybir.dt.float32r
ALU = mybir.AluOpType
ACT = mybir.ActivationFunctionType
AX = mybir.AxisListType

P = 128
EPS = 1e-6
GRID_W = 64


def mixer_dit_kernel(nc, x, c, ctx_in, c_ctx, w_mod, b_mod, norm_ffn1, ffn1_up, ffn1_down, norm_mix, w_in, b_in,
                     mlstm_norm, conv_w, conv_b, conv_norm_g, conv_norm_b, w_out, norm_ffn2, ffn2_up, ffn2_down,
                     norm_final, out):
    _, NX, D = x.shape
    NC = ctx_in.shape[1]
    T = NX + NC
    DEPTH = w_mod.shape[0]
    KD = D // P
    NM = w_mod.shape[2] // P
    FF = ffn1_down.shape[1]
    KF = FF // P // 2
    DM = mlstm_norm.shape[1]
    H = DM // P
    KC = conv_norm_g.shape[1] // P
    TAPS = conv_w.shape[1]
    G0 = 4 * DM
    U0 = G0 + 4 * H
    TX, TT = NX // P, T // P
    NCH = TT
    CCH = NC // P
    E1 = P + 1
    ROWS = 32 + H
    GR = 96 + H
    R_CS, R_WK, R_INTER, R_EM, R_DEC = range(5)
    assert D == 2 * DM and H == 4 and KC == 4 and T == 768 and FF % (2 * P) == 0

    phases = []

    def add_phase(name, l, k, pairs, width, **more):
        before = sum(q["pairs"] for q in phases)
        phases.append(dict(name=name, l=l, k=k, pairs=pairs, w=width, p0=before, **more))

    for l in range(DEPTH):
        last = l == DEPTH - 1
        WL = NX if last else T
        for half in range(2):
            add_phase("up", l, KD, KF, T, up=ffn1_up, half=half)
            add_phase("down", l, KF, KD // 2, T, down=ffn1_down, half=half, gate=0, norm=3 * l + 1 if half else None)
        add_phase("glu", l, KD, KC, WL)
        add_phase("q", l, KD, H // 2, WL)
        add_phase("kv", l, KD, H, T)
        add_phase("o", l, KD, H // 2, WL)
        add_phase("out", l, KD, KD // 2, WL, gate=1, norm=3 * l + 2)
        for half in range(2):
            add_phase("up", l, KD, KF, WL, up=ffn2_up, half=half)
            add_phase("down", l, KF, KD // 2, WL, down=ffn2_down, half=half, gate=2, norm=3 * l + 3 if half else None)
    PAIRS = sum(q["pairs"] for q in phases)
    for n, q in enumerate(phases):
        q["next"] = phases[n + 1] if n + 1 < len(phases) else None
        q["ups"] = sum(1 for r in phases[:n] if r["name"] == "up")

    def phase(name, l, nth=0):
        return [q for q in phases if q["name"] == name and q["l"] == l][nth]

    def width_of_norm(r):
        return NX if r >= 3 * (DEPTH - 1) + 2 else T

    def split_of(l, what):
        return 4 * l + {"ffn1": 0, "mix": 1, "y": 2, "ffn2": 3}[what]

    norm_place = {}
    for l in range(DEPTH):
        norm_place[3 * l], norm_place[3 * l + 1], norm_place[3 * l + 2] = (
            split_of(l, "ffn1"), split_of(l, "mix"), split_of(l, "ffn2"))

    def tile_of(d, ch):
        return (TX + ch if ch < CCH else ch - CCH) if d == 0 else TT - 1 - ch

    steps = [(2 * ch + d, d, ch, tile_of(d, ch)) for ch in range(NCH) for d in range(2)]

    def gives(l, step):
        return l < DEPTH - 1 or step[2] >= CCH

    def outs_before(l, n):
        return sum(gives(m, s) for m in range(l) for s in steps) + sum(gives(l, s) for s in steps[:n])

    def keeps(step):
        return step[2] < NCH - 1

    def kept(l, step):
        return keeps(step)

    def inters(l, step):
        return gives(l, step) and step[2] > 0

    def count(pred, l, n):
        return sum(pred(m, s) for m in range(l) for s in steps) + sum(pred(l, s) for s in steps[:n])

    with ExitStack() as stack:
        SB0 = 16512
        place = [SB0]

        def region(size):
            at = place[0]
            place[0] += (size + 31) // 32 * 32
            assert place[0] <= 229344, place[0]
            return at

        def at(name, shape, offset, dt=F32):
            return nc.alloc_sbuf_tensor_at(name, shape, dt, offset=offset)

        def sem(name):
            return stack.enter_context(nc.semaphore(name))

        r_x = region(KD * T * 4)
        r_h = region(2 * KD * T * 4)
        r_a = region(2 * KF * T * 4)
        UNIT = max(KD, KF) * P
        xres = at("xres", [P, KD, T], r_x)
        h_hi = at("h_hi", [P, KD, T], r_h, F32R)
        h_lo = at("h_lo", [P, KD, T], r_h + KD * T * 4, F32R)
        a_hi = at("a_hi", [P, KF, T], r_a, F32R)
        a_lo = at("a_lo", [P, KF, T], r_a + KF * T * 4, F32R)
        raw = [at(f"raw{s}", [P, UNIT], region(UNIT * 4)) for s in range(2)]
        w_hi = [at(f"w_hi{s}", [P, UNIT], region(UNIT * 4), F32R) for s in range(2)]
        w_lo = [at(f"w_lo{s}", [P, UNIT], region(UNIT * 4), F32R) for s in range(2)]
        r_m = region(KC * T * 4)
        tmp = at("tmp", [P, 4, T], region(4 * T * 4))
        ssum = at("ssum", [P, T], region(T * 4))
        ident = at("ident", [P, P], region(P * 4))
        ones = at("ones", [P, P], region(P * 4))
        sel = at("sel", [ROWS, 2, H, P], region(2 * H * P * 4))
        tab_a = at("tab_a", [P, DEPTH, P], region(DEPTH * P * 4))
        tab_b = at("tab_b", [P, DEPTH, TAPS * KC], region(DEPTH * TAPS * KC * 4))
        NCR = DEPTH * 2 * KC + 3 * KD
        tab_c = at("tab_c", [P, NCR], region(NCR * 4))
        coef = at("coef", [P, DEPTH, 3, 2, KD], region(DEPTH * 3 * 2 * KD * 4))
        shift = at("shift", [P, DEPTH, 3, 2, KD], region(DEPTH * 3 * 2 * KD * 4))
        gate = at("gate", [P, DEPTH, 3, 2, KD], region(DEPTH * 3 * 2 * KD * 4))
        silu_c = at("silu_c", [P, KD, 2], region(KD * 2 * 4))
        bq = at("bq", [P, DEPTH, H], region(DEPTH * H * 4))
        gbias = at("gbias", [P, DEPTH], region(DEPTH * 4))
        stat = at("stat", [P, 3, TT * H], region(3 * TT * H * 4))
        eps = at("eps", [P, 1], region(4))
        rsm = at("rsm", [ROWS, 3, NCH], region(3 * NCH * 4))
        qkvo = at("qkvo", [P, 4 * H, T], r_a)
        kt = at("kt", [P, TT, DM], r_a + 2 * H * T * 4)
        z = at("z", [P, KC, T], r_a + 4 * H * T * 4)
        r_left = r_a + (4 * H + KC) * T * 4
        r1_row = at("r1_row", [ROWS, NCH, P], r_left)
        col = at("col", [P, 5, NCH, 2, H], r_left + T * 4)
        rt = at("rt", [ROWS, 9, T], r_a)
        rq = at("rq", [ROWS, 5, NCH, P], r_a + 9 * T * 4)
        yc = at("yc", [P, KC, T], r_m)
        mraw = [at(f"mraw{s}", [P, KD, P], r_m + s * KD * P * 4) for s in range(2)]
        gw = at("gw", [P, KD, GR], r_m)
        gw_hi = at("gw_hi", [P, KD, GR], r_m + KD * GR * 4, F32R)
        gw_lo = at("gw_lo", [P, KD, GR], r_m + 2 * KD * GR * 4, F32R)
        gw16 = at("gw16", [P, KD, 4 * H], r_m + 3 * KD * GR * 4)
        HE = (H * E1 * 4 + 31) // 32 * 32
        vw = [at(f"vw{s}", [P, H, E1], r_h + s * HE) for s in range(2)]
        sw = [at(f"sw{s}", [P, H, P], r_h + 2 * HE + s * H * P * 4) for s in range(2)]
        r_h1 = r_h + KC * T * 4
        hm = at("hm", [P, TT, DM], r_h1)
        r_h2 = r_h + KD * T * 4
        vt = at("vt", [P, TT, H, E1], r_h2)
        state = [at(f"state{d}", [P, H, E1], r_h2 + (TT + d) * HE) for d in range(2)]
        isb = [at(f"isb{s}", [P, H, E1], r_h2 + (TT + 2 + s) * HE) for s in range(2)]
        r_h4 = r_h2 + (TT + 4) * HE
        ew = [at("ew0", [P, H, P], r_h + 2 * HE + 2 * H * P * 4), at("ew1", [P, H, P], r_h4)]
        assert r_h4 + H * P * 4 <= r_a
        tok = at("tok", [P, TT, D], r_a)
        tabs = at("tabs", [P, 2 * DEPTH + 1, P], r_a + TT * D * 4)
        otok = at("otok", [P, TX, D], r_a)
        tot = tmp[:, 0, 0:H * E1].rearrange("p (h e) -> p h e", h=H)

        ps = stack.enter_context(nc.psum_tensor("ps", [P, 8, 512], F32))

        def slot_ps(s, w):
            return ps[:, 2 * s:2 * s + 2, :].rearrange("p b n -> p (b n)")[:, 0:w]

        wide = ps[:, 5:7, :].rearrange("p b n -> p (b n)")

        def groups(w):
            return [(0, NX)] + ([(NX, T)] if w > NX else [])

        def pair_banks(b):
            return ps[:, b:b + 2, 0:2 * E1]

        def head_ps(b, h):
            return ps[:, b + h // 2, h % 2 * E1:h % 2 * E1 + E1]

        def flat2(t):
            return t.rearrange("p (b h) e -> p b (h e)", b=2)

        def chunk(t, j, w):
            if isinstance(j, int):
                return t[:, j, 0:w]
            return t[:, bass.ds(j, 1), 0:w].rearrange("p k n -> p (k n)")

        def column(t, j):
            return t[:, j:j + 1] if isinstance(j, int) else t[:, bass.ds(j, 1)]

        in_loaded = sem("in_loaded")
        tab_loaded = sem("tab_loaded")
        bias_cleared = sem("bias_cleared")
        const_ready = sem("const_ready")
        const_cleared = sem("const_cleared")
        tab_turned = sem("tab_turned")
        tab_read = sem("tab_read")
        silu_ready = sem("silu_ready")
        mod_loaded = [sem(f"mod_loaded{s}") for s in range(2)]
        mod_used = sem("mod_used")
        x_turned = sem("x_turned")
        x_copied = sem("x_copied")
        raw_loaded = [sem(f"raw_loaded{s}") for s in range(2)]
        hi_ready = sem("hi_ready")
        lo_ready = sem("lo_ready")
        unit_done = sem("unit_done")
        slot_read = [sem(f"slot_read{s}") for s in range(2)]
        a_hi_ready = sem("a_hi_ready")
        a_lo_ready = sem("a_lo_ready")
        sq_ready = sem("sq_ready")
        ss_added = sem("ss_added")
        ss_summed = sem("ss_summed")
        root_ready = sem("root_ready")
        diag_ready = sem("diag_ready")
        wide_ready = sem("wide_ready")
        normed = sem("normed")
        hf_ready = sem("hf_ready")
        h_hi_ready = sem("h_hi_ready")
        h_lo_ready = sem("h_lo_ready")
        dve_self = sem("dve_self")
        gw_loaded = sem("gw_loaded")
        gw_cleared = sem("gw_cleared")
        gw_ready = sem("gw_ready")
        gw_hi_ready = sem("gw_hi_ready")
        gw_lo_ready = sem("gw_lo_ready")
        gates_ready = sem("gates_ready")
        rows_dve = sem("rows_dve")
        rows_act = sem("rows_act")
        cols_turned = sem("cols_turned")
        cols_ready = sem("cols_ready")
        conv_step = sem("conv_step")
        yc_totalled = sem("yc_totalled")
        yc_dev = sem("yc_dev")
        yc_sq = sem("yc_sq")
        yc_summed = sem("yc_summed")
        yc_norm = sem("yc_norm")
        yc_act = sem("yc_act")
        vk_turned = sem("vk_turned")
        vk_read = sem("vk_read")
        ones_ready = sem("ones_ready")
        s_ready = sem("s_ready")
        b_ready = sem("b_ready")
        e_ready = sem("e_ready")
        mask_ready = sem("mask_ready")
        sw_ready = sem("sw_ready")
        vw_ready = sem("vw_ready")
        n_ready = sem("n_ready")
        i_ready = sem("i_ready")
        isb_ready = sem("isb_ready")
        dc_ready = sem("dc_ready")
        state_ready = sem("state_ready")
        tot_ready = sem("tot_ready")
        hm_squared = sem("hm_squared")
        hm_root = sem("hm_root")
        hm_scaled = sem("hm_scaled")
        hm_turned = sem("hm_turned")
        ym_ready = sem("ym_ready")
        o_turned = sem("o_turned")
        out_read = sem("out_read")
        stored = sem("stored")

        A_N1 = NM
        A_NM, A_N2, A_MG = A_N1 + KD, A_N1 + 2 * KD, A_N1 + 3 * KD
        A_CB, A_CG, A_CN, A_BIN = A_MG + H, A_MG + H + KC, A_MG + H + 2 * KC, A_MG + H + 3 * KC
        assert A_BIN + 4 * H == P
        C_FIN = DEPTH * 2 * KC
        C_C = C_FIN + KD
        TAB_DMAS = DEPTH * 10 + DEPTH + 3 + DEPTH * 4
        GATE_ROWS = (0, 64, 32, 96)

        def as_rows(v):
            return v.rearrange("(r f) -> r f", f=P)

        def weights_of(q, i, s):
            l, name = q["l"], q["name"]
            if name == "up":
                w, at_col = q["up"][l], i * P + (s * FF + q["half"] * KF * P)
            elif name == "down":
                w, at_col = q["down"][l][q["half"] * KF * P:(q["half"] + 1) * KF * P], i * (2 * P) + s * P
            elif name == "glu":
                w, at_col = w_in[l], i * P + (U0 + s * KC * P)
            elif name == "out":
                w, at_col = w_out[l], i * (2 * P) + s * P
            else:
                w, at_col = w_in[l], i * (2 * P) + ({"q": 0, "kv": DM, "o": 3 * DM}[name] + s * P)
            return w.rearrange("(k p) n -> p k n", p=P)[:, :, bass.ds(at_col, P)]

        def chain_of_norm(r):
            return 5 * (r // 3) + (0, 1, 4)[r % 3]

        def chain_of_conv(l, which):
            return 5 * l + 2 + which

        def roots_before(chain):
            return chain - sum(chain_of_conv(l, 0) < chain for l in range(DEPTH))

        def run_pairs(engine, q, pair):
            n = q["pairs"]
            pair(0, q["p0"], q["k"])
            if n > 2:
                with engine.Fori(1, n - 1) as i:
                    pair(i, i + q["p0"], q["k"])
            pair(n - 1, q["p0"] + n - 1, q["next"]["k"] if q["next"] else 0)

        block = stack.enter_context(nc.Block())

        @block.sync
        def _(sp):
            sp.dma_start(tok[:, 0:TX, :], x[0].rearrange("(t p) d -> p t d", p=P)).then_inc(in_loaded, 16)
            sp.dma_start(tok[:, TX:TT, :], ctx_in[0].rearrange("(t p) d -> p t d", p=P)).then_inc(in_loaded, 16)

            for l in range(DEPTH):
                wm = w_mod[l].rearrange("(k p) n -> p k n", p=P)
                for s in range(2):
                    if l:
                        sp.wait_ge(mod_used, NM * l + s - 1)
                    sp.dma_start(mraw[s][:], wm[:, :, s * P:(s + 1) * P]).then_inc(mod_loaded[s], 16)
                with sp.Fori(1, NM // 2) as i:
                    for s in range(2):
                        sp.wait_ge(mod_used, i * 2 + (NM * l + s - 1))
                        sp.dma_start(mraw[s][:], wm[:, :, bass.ds(i * (2 * P) + s * P, P)]).then_inc(mod_loaded[s], 16)

            def load(q, i, s):
                sp.dma_start(raw[s][:, 0:q["k"] * P].rearrange("p (k n) -> p k n", n=P),
                             weights_of(q, i, s)).then_inc(raw_loaded[s], 16)

            for q in phases:
                first = 0
                if q["p0"] == 0:
                    load(q, 0, 0)
                    load(q, 0, 1)
                    first = 1
                if q["name"] == "down" and q["gate"] == 0 and q["half"] == 1:
                    sp.wait_ge(unit_done, 2 * phase("up", q["l"])["p0"] + 1)
                    sp.dma_start(gw16[:], w_in[q["l"]].rearrange("(k p) n -> p k n", p=P)[:, :, G0:U0]).then_inc(gw_loaded, 16)
                with sp.Fori(first, q["pairs"]) as i:
                    for s in range(2):
                        sp.wait_ge(lo_ready, i * 2 + (2 * q["p0"] + s - 1))
                        load(q, i, s)

            sp.wait_ge(out_read, KD)
            for t in range(TX):
                sp.dma_start(out[0, t * P:(t + 1) * P, :], otok[:, t, :]).then_inc(stored, 16)
            sp.wait_ge(stored, 16 * TX)

        @block.gpsimd
        def _(pool):
            pool.memset(gbias[:], 0.0).then_inc(bias_cleared, 1)
            pool.wait_ge(bias_cleared, 1)
            for l in range(DEPTH):
                for j, row in enumerate(GATE_ROWS):
                    pool.dma_start(gbias[row:row + H, l:l + 1],
                                   b_in[l, G0 + j * H:G0 + (j + 1) * H].rearrange("(h o) -> h o", o=1)).then_inc(tab_loaded, 16)
                r = 0
                for v in (b_mod[l], norm_ffn1[l], norm_mix[l], norm_ffn2[l], mlstm_norm[l], conv_b[l],
                          conv_norm_g[l], conv_norm_b[l], b_in[l, 0:G0]):
                    n = v.shape[0] // P
                    pool.dma_start(tabs[r:r + n, l, :], as_rows(v)).then_inc(tab_loaded, 16)
                    r += n
                pool.dma_start(tabs[0:TAPS * KC, DEPTH + l, :],
                               conv_w[l].rearrange("t (c f) -> (t c) f", f=P)).then_inc(tab_loaded, 16)
                pool.dma_start(tabs[l * 2 * KC:(l + 1) * 2 * KC, 2 * DEPTH, :],
                               as_rows(b_in[l, U0:U0 + 2 * KC * P])).then_inc(tab_loaded, 16)
            for v, r in ((norm_final, C_FIN), (c[0], C_C), (c_ctx, C_C + KD)):
                pool.dma_start(tabs[r:r + KD, 2 * DEPTH, :], as_rows(v)).then_inc(tab_loaded, 16)

            pool.memset(ident[:], 0.0).then_inc(const_cleared, 1)
            pool.memset(sel[:], 0.0).then_inc(const_cleared, 1)
            pool.memset(ones[:], 1.0).then_inc(const_ready, 1)
            pool.memset(eps[:], EPS).then_inc(const_ready, 1)
            pool.wait_ge(const_cleared, 2)
            pool.affine_select(out=ident[:], in_=ident[:], compare_op=ALU.not_equal, fill=1.0, base=0,
                               pattern=[[-1, P]], channel_multiplier=1).then_inc(const_ready, 1)
            pool.affine_select(out=sel[:], in_=sel[:], compare_op=ALU.not_equal, fill=1.0, base=0,
                               pattern=[[-32, 2], [-1, H], [0, P]], channel_multiplier=1).then_inc(const_ready, 1)

            def split_low(k, p, s):
                pool.wait_ge(hi_ready, p * 2 + (s + 1))
                pool.tensor_tensor(w_lo[s][:, 0:k * P], raw[s][:, 0:k * P], w_hi[s][:, 0:k * P].bitcast(F32),
                                   ALU.subtract).then_inc(lo_ready, 1)

            def add_square(r, j, s, w, first):
                pool.wait_ge(sq_ready, j + (KD * r + 1))
                if first:
                    if r:
                        pool.wait_ge(ss_summed, chain_of_norm(r))
                    pool.tensor_copy(ssum[:, 0:w], tmp[:, 2 + s, 0:w]).then_inc(ss_added, 1)
                else:
                    pool.wait_ge(ss_added, j + KD * r)
                    pool.tensor_tensor(ssum[:, 0:w], ssum[:, 0:w], tmp[:, 2 + s, 0:w], ALU.add).then_inc(ss_added, 1)

            def norm_low(r):
                w, n = width_of_norm(r), KD * norm_place[r]
                with pool.Fori(0, KD // 2) as i:
                    for s in range(2):
                        pool.wait_ge(h_hi_ready, i * 2 + (n + s + 1))
                        j = i * 2 + s
                        pool.tensor_tensor(chunk(h_lo, j, w), tmp[:, 2 + s, 0:w], chunk(h_hi, j, w).bitcast(F32),
                                           ALU.subtract).then_inc(h_lo_ready, 1)

            def gate_weights(l):
                pool.wait_ge(gw_loaded, 16 * (l + 1))
                pool.memset(gw[:], 0.0).then_inc(gw_cleared, 1)
                pool.wait_ge(gw_cleared, l + 1)
                for j, row in enumerate(GATE_ROWS):
                    pool.tensor_copy(gw[:, :, row:row + H], gw16[:, :, j * H:(j + 1) * H]).then_inc(gw_ready, 1)
                pool.wait_ge(gw_hi_ready, l + 1)
                pool.tensor_tensor(gw_lo[:], gw[:], gw_hi[:].bitcast(F32), ALU.subtract).then_inc(gw_lo_ready, 1)

            def scan_steps(l):
                pool.wait_ge(vk_turned, 2 * TT * l + 1)
                pool.memset(vt[:, :, :, P:E1], 1.0).then_inc(ones_ready, 1)
                for st in steps:
                    n, d, ch, t = st
                    if keeps(st):
                        if n == 0:
                            pool.wait_ge(vk_read, 2 * TT * l + TT)
                            pool.wait_ge(ones_ready, l + 1)
                            pool.wait_ge(cols_ready, l + 1)
                        if n >= 2:
                            pool.wait_ge(dc_ready, count(kept, l, n - 1))
                        pool.tensor_tensor(vw[n % 2][:], vt[:, t, :, :],
                                           col[:, R_WK, ch, d, :].rearrange("p (h o) -> p h o", o=1).to_broadcast([P, H, E1]),
                                           ALU.mult).then_inc(vw_ready, 1)
                    if gives(l, st):
                        pool.wait_ge(e_ready, outs_before(l, n) + 1)
                        sign = 1 if d == 0 else -1
                        pool.affine_select(out=ew[n % 2][:], in_=ew[n % 2][:], compare_op=ALU.is_ge, fill=0.0, base=0,
                                           pattern=[[0, H], [sign, P]], channel_multiplier=-sign).then_inc(mask_ready, 1)

            def conv_squares(l, w):
                for k in range(KC):
                    pool.wait_ge(yc_sq, KC * l + k + 1)
                    if k == 0:
                        pool.wait_ge(ss_summed, chain_of_conv(l, 0) + 1)
                        pool.tensor_copy(ssum[:, 0:w], tmp[:, 2, 0:w]).then_inc(yc_summed, 1)
                    else:
                        pool.wait_ge(yc_summed, KC * l + k)
                        pool.tensor_tensor(ssum[:, 0:w], ssum[:, 0:w], tmp[:, 2 + k % 2, 0:w], ALU.add).then_inc(yc_summed, 1)

            def mixer_low(l, w):
                n = KD * split_of(l, "y")
                for k in range(KD):
                    pool.wait_ge(h_hi_ready, n + k + 1)
                    src = tmp[:, 2 + k % 2, 0:w] if k < H else yc[:, k - H, 0:w]
                    pool.tensor_tensor(h_lo[:, k, 0:w], src, h_hi[:, k, 0:w].bitcast(F32), ALU.subtract).then_inc(h_lo_ready, 1)

            split_low(KD, 0, 0)
            split_low(KD, 0, 1)
            for j in range(KD):
                add_square(0, j, j % 2, T, j == 0)
            for q in phases:
                l, w, name = q["l"], q["w"], q["name"]
                if name == "up" and q["half"] == 0:
                    norm_low(3 * l + (0 if q["up"] is ffn1_up else 2))
                if name == "glu":
                    gate_weights(l)
                    norm_low(3 * l + 1)
                if name == "out":
                    conv_squares(l, w)
                    scan_steps(l)
                    mixer_low(l, w)

                def pair(i, p, k_next, q=q, w=w):
                    if k_next:
                        split_low(k_next, p + 1, 0)
                        split_low(k_next, p + 1, 1)
                    if q.get("norm"):
                        for s in range(2):
                            add_square(q["norm"], i * 2 + s, s, w, isinstance(i, int) and i == 0 and s == 0)

                run_pairs(pool, q, pair)

        @block.scalar
        def _(act):
            def split_high(k, p, s):
                act.wait_ge(raw_loaded[s], p * 16 + 16)
                if not isinstance(p, int) or p > 0:
                    act.wait_ge(unit_done, p * 2 + (s - 1))
                act.activation(w_hi[s][:, 0:k * P], raw[s][:, 0:k * P], ACT.Copy).then_inc(hi_ready, 1)

            def square(r, j, s, w):
                if not (isinstance(j, int) and j < 2):
                    act.wait_ge(ss_added, j + (KD * r - 1))
                act.activation(tmp[:, 2 + s, 0:w], chunk(xres, j, w), ACT.Square).then_inc(sq_ready, 1)

            def root(chain, w, scale):
                act.wait_ge(ss_summed, chain + 1)
                act.activation(stat[:, 0, 0:w // P], ps[:, 4, 0:w // P], ACT.Sqrt, scale=scale,
                               bias=eps[:]).then_inc(root_ready, 1)

            def norm_high(r):
                w, n = width_of_norm(r), KD * norm_place[r]
                with act.Fori(0, KD // 2) as i:
                    for s in range(2):
                        act.wait_ge(hf_ready, i * 2 + (KD * r + s + 1))
                        act.activation(chunk(h_hi, i * 2 + s, w), tmp[:, 2 + s, 0:w], ACT.Copy).then_inc(h_hi_ready, 1)

            def gate_rows(l):
                act.wait_ge(rows_dve, 3 * l + 1)
                act.activation(rt[:, 6, :], rt[:, 5, :], ACT.Exp, scale=-1.0).then_inc(rows_act, 1)
                act.wait_ge(rows_act, 3 * l + 1)
                act.activation(rt[:, 5, :], rt[:, 6, :], ACT.Ln, bias=ones[0:ROWS, 0:1]).then_inc(rows_act, 1)
                act.wait_ge(rows_dve, 3 * l + 2)
                for r, src, scale in ((R_WK, rt[:, 1, :], 1.0), (R_INTER, rt[:, 5, :], 1.0), (R_EM, rt[:, 4, :], -1.0),
                                      (R_DEC, None, 1.0)):
                    if src is None:
                        src = rsm[:, 2, :].rearrange("r (c o) -> r c o", o=1).to_broadcast([ROWS, NCH, P])
                    else:
                        src = src.rearrange("r (c n) -> r c n", n=P)
                    act.activation(rq[0:32, r, :, :], src[0:32], ACT.Exp, scale=scale)
                    last = act.activation(rq[32:ROWS, r, :, ::-1], src[32:ROWS], ACT.Exp, scale=scale)
                last.then_inc(rows_act, 1)

            def turned_values(l):
                for i in range(2 * TT):
                    act.wait_ge(vk_turned, 2 * TT * l + i + 1)
                    bank = ps[:, 4 + i % 4, :]
                    if i < TT:
                        act.activation(vt[:, i, :, 0:P], bank.rearrange("p (h e) -> p h e", h=H), ACT.Copy).then_inc(vk_read, 1)
                    else:
                        act.activation(kt[:, i - TT, :], bank, ACT.Copy).then_inc(vk_read, 1)

            def conv_norm(l, w):
                for k in range(KC):
                    act.wait_ge(yc_dev, KC * l + k + 1)
                    if k >= 2:
                        act.wait_ge(yc_summed, KC * l + k - 1)
                    act.activation(tmp[:, 2 + k % 2, 0:w], yc[:, k, 0:w], ACT.Square).then_inc(yc_sq, 1)
                root(chain_of_conv(l, 1), w, 1.0 / (KC * P))
                for k in range(KC):
                    act.wait_ge(yc_norm, KC * l + k + 1)
                    act.activation(yc[:, k, 0:w], yc[:, k, 0:w], ACT.Silu, scale=tab_a[:, l, A_CG + k:A_CG + k + 1],
                                   bias=tab_a[:, l, A_CN + k:A_CN + k + 1]).then_inc(yc_act, 1)

            def scan_steps(l):
                def weights(st):
                    n, d, ch, t = st
                    o = outs_before(l, n)
                    act.wait_ge(b_ready, o + 1)
                    if o >= 2:
                        act.wait_ge(sw_ready, o - 1)
                    for h in range(H):
                        last = act.activation(ew[n % 2][:, h, :], ps[:, 1, h * P:(h + 1) * P], ACT.Exp,
                                              bias=col[:, R_CS, ch, d, h:h + 1])
                    last.then_inc(e_ready, 1)

                act.wait_ge(cols_ready, l + 1)
                if gives(l, steps[0]):
                    weights(steps[0])
                for st in steps:
                    n, d, ch, t = st
                    if n + 1 < len(steps) and gives(l, steps[n + 1]):
                        weights(steps[n + 1])
                    if inters(l, st):
                        act.wait_ge(i_ready, count(inters, l, n) + 1)
                        if outs_before(l, n) >= 2:
                            act.wait_ge(tot_ready, outs_before(l, n) - 1)
                        for h in range(H):
                            last = act.activation(isb[n % 2][:, h, :], head_ps(4, h), ACT.Copy,
                                                  scale=col[:, R_INTER, ch, d, h:h + 1])
                        last.then_inc(isb_ready, 1)

            def mixer_high(l, w):
                act.wait_ge(hm_squared, l + 1)
                m = w // P * H
                act.activation(stat[:, 0, 0:m], stat[:, 1, 0:m], ACT.Sqrt, scale=1.0 / P, bias=eps[:]).then_inc(hm_root, 1)
                for k in range(KD):
                    if k < H:
                        act.wait_ge(ym_ready, H * l + k + 1)
                        src = tmp[:, 2 + k % 2, 0:w]
                    else:
                        act.wait_ge(hm_turned, H * (l + 1))
                        act.wait_ge(yc_act, KC * (l + 1))
                        src = yc[:, k - H, 0:w]
                    act.activation(h_hi[:, k, 0:w], src, ACT.Copy).then_inc(h_hi_ready, 1)

            act.wait_ge(const_ready, 4)
            act.wait_ge(tab_read, 1)
            act.activation(silu_c[:], tab_c[:, C_C:C_C + 2 * KD].rearrange("p (o k) -> p k o", o=2), ACT.Silu).then_inc(silu_ready, 1)
            split_high(KD, 0, 0)
            split_high(KD, 0, 1)
            for j in range(KD):
                act.wait_ge(x_copied, j + 1)
                square(0, j, j % 2, T)

            for q in phases:
                l, w, name = q["l"], q["w"], q["name"]
                if name == "up" and q["half"] == 0:
                    r = 3 * l + (0 if q["up"] is ffn1_up else 2)
                    root(chain_of_norm(r), w, 1.0 / D)
                    norm_high(r)
                if name == "glu":
                    act.wait_ge(gw_ready, 4 * (l + 1))
                    act.activation(gw_hi[:], gw[:], ACT.Copy).then_inc(gw_hi_ready, 1)
                    root(chain_of_norm(3 * l + 1), T, 1.0 / D)
                    norm_high(3 * l + 1)
                    gate_rows(l)
                if name == "out":
                    turned_values(l)
                    conv_norm(l, w)
                    scan_steps(l)
                    mixer_high(l, w)

                def evacuate(i, s, q=q, l=l, w=w, name=name):
                    if name == "q":
                        func, scale, bias, to = ACT.Identity, float(P) ** -0.5, column(bq[:, l, :], i * 2 + s), i * 2 + s
                    elif name == "kv":
                        func, scale, bias, to = ACT.Identity, 1.0, column(tab_a[:, l, :], i * 2 + (A_BIN + H + s)), i * 2 + (H + s)
                    else:
                        func, scale, bias, to = ACT.Sigmoid, 1.0, column(tab_a[:, l, :], i * 2 + (A_BIN + 3 * H + s)), i * 2 + (3 * H + s)
                    act.activation(chunk(qkvo, to, w), slot_ps(s, w), func, scale=scale, bias=bias).then_inc(slot_read[s], 1)

                def pair(i, p, k_next, q=q, l=l, w=w, name=name, evacuate=evacuate):
                    act.wait_ge(unit_done, p * 2 + 1)
                    if name == "up":
                        act.activation(tmp[:, 0, 0:w], slot_ps(0, w), ACT.Silu).then_inc(slot_read[0], 1)
                    if name in ("q", "kv", "o"):
                        evacuate(i, 0)
                    if k_next:
                        split_high(k_next, p + 1, 0)
                    act.wait_ge(unit_done, p * 2 + 2)
                    if name == "glu":
                        if not isinstance(i, int) or i > 0:
                            act.wait_ge(slot_read[0], p)
                        act.activation(tmp[:, 0, 0:w], slot_ps(1, w), ACT.Sigmoid,
                                       bias=column(tab_c, i + (l * 2 * KC + KC))).then_inc(slot_read[1], 1)
                    if name in ("q", "kv", "o"):
                        evacuate(i, 1)
                    if k_next:
                        split_high(k_next, p + 1, 1)
                    if name == "up":
                        act.wait_ge(slot_read[1], p + 1)
                        act.activation(chunk(a_hi, i, w), tmp[:, 1, 0:w], ACT.Copy).then_inc(a_hi_ready, 1)
                    if q.get("norm"):
                        for s in range(2):
                            act.wait_ge(slot_read[s], p + 1)
                            square(q["norm"], i * 2 + s, s, w)

                run_pairs(act, q, pair)

            root(chain_of_norm(3 * DEPTH), NX, 1.0 / D)
            for k in range(KD):
                act.wait_ge(o_turned, k + 1)
                act.activation(otok[:, :, k * P:(k + 1) * P], ps[:, 2 * (k % 2), :].rearrange("p (t f) -> p t f", t=TX),
                               ACT.Copy).then_inc(out_read, 1)

        @block.vector
        def _(dve):
            self_count = [0]

            def settle(ins):
                self_count[0] += 1
                ins.then_inc(dve_self, 1)
                dve.wait_ge(dve_self, self_count[0])

            def diagonals(chain, w):
                for t in range(w // P):
                    last = dve.tensor_scalar(tmp[:, 0, t * P:(t + 1) * P], ident[:], stat[:, 1, t:t + 1], None, ALU.mult)
                last.then_inc(diag_ready, 1)
                dve.wait_ge(wide_ready, chain + 1)

            def reciprocals(chain, w):
                dve.wait_ge(root_ready, roots_before(chain) + 1)
                settle(dve.reciprocal(stat[:, 1, 0:w // P], stat[:, 0, 0:w // P]))
                diagonals(chain, w)

            def norm(r):
                w = width_of_norm(r)
                l, which = divmod(r, 3)
                reciprocals(chain_of_norm(r), w)
                n = KD * norm_place[r]

                def chunks(i, first):
                    for s in range(2):
                        j = i * 2 + s
                        if not first:
                            dve.wait_ge(h_lo_ready, j + (n - 1))
                        dve.tensor_tensor(tmp[:, s, 0:w], chunk(xres, j, w), wide[:, 0:w], ALU.mult).then_inc(normed, 1)
                        dve.wait_ge(normed, j + (KD * r + 1))
                        for o, (b, e) in enumerate(groups(w)):
                            last = dve.tensor_scalar(tmp[:, 2 + s, b:e], tmp[:, s, b:e], column(coef[:, l, which, o, :], j),
                                                     column(shift[:, l, which, o, :], j), ALU.mult, ALU.add)
                        last.then_inc(hf_ready, 1)

                chunks(0, True)
                with dve.Fori(1, KD // 2) as i:
                    chunks(i, False)

            def gate_rows(l):
                settle(dve.memset(rt[:, 0:2, :], 0.0))
                for k, first in ((0, 0), (1, 64)):
                    for d in range(2):
                        src = slice(first + 32 * d, first + 32 * d + H)
                        to = slice(32 * d, 32 * d + H)
                        if k == 0 and d == 0:
                            dve.wait_ge(gates_ready, l + 1)
                        for bank, b, e in ((4, 0, NC), (7, NC, T)):
                            got = ps[src, bank, 0:e - b]
                            settle(dve.tensor_scalar(rt[to, k, b:e], got if d == 0 else got[:, ::-1], gbias[src, l:l + 1],
                                                     None, ALU.add))
                dve.scalar_tensor_tensor(rt[:, 5, :], rt[:, 1, :], -1.0, rt[:, 1, :], ALU.mult, ALU.max).then_inc(rows_dve, 1)
                dve.wait_ge(rows_act, 3 * l + 2)
                settle(dve.memset(rt[:, 6, :], 1.0))
                settle(dve.memset(rt[:, 6, :].rearrange("r (c n) -> r c n", n=P)[:, :, 0:1], 0.0))
                settle(dve.scalar_tensor_tensor(rt[:, 2, :], rt[:, 1, :], 0.0, rt[:, 5, :], ALU.min, ALU.subtract))
                settle(dve.tensor_tensor_scan(rt[:, 3, :], rt[:, 6, :], rt[:, 2, :], 0.0, ALU.mult, ALU.add))
                settle(dve.tensor_tensor_scan(rt[:, 4, :], rt[:, 2, :], rt[:, 0, :], 0.0, ALU.add, ALU.max))
                settle(dve.tensor_tensor(rt[:, 8, :], rt[:, 3, :], rt[:, 4, :], ALU.subtract))
                settle(dve.tensor_tensor(rt[:, 7, :], rt[:, 0, :], rt[:, 3, :], ALU.subtract))

                def by_chunk(k):
                    return rt[:, k, :].rearrange("r (c n) -> r c n", n=P)

                def spread(k):
                    return rsm[:, k, :].rearrange("r (c o) -> r c o", o=1).to_broadcast([ROWS, NCH, P])

                settle(dve.memset(rsm[:, 0, 0:1], 0.0))
                settle(dve.tensor_copy(rsm[:, 0, 1:NCH], by_chunk(4)[:, 0:NCH - 1, P - 1]))
                settle(dve.tensor_copy(rsm[:, 1, :], by_chunk(8)[:, :, P - 1]))
                settle(dve.tensor_tensor(rsm[:, 2, :], rsm[:, 1, :], rsm[:, 0, :], ALU.add))
                settle(dve.tensor_tensor(by_chunk(5), by_chunk(8), spread(0), ALU.add))
                dve.tensor_tensor(by_chunk(1), by_chunk(7), spread(1), ALU.add).then_inc(rows_dve, 1)
                for k, to in ((8, r1_row[:]), (7, rq[:, R_CS, :, :])):
                    dve.tensor_copy(to[0:32], by_chunk(k)[0:32])
                    last = dve.tensor_copy(to[32:ROWS, :, ::-1], by_chunk(k)[32:ROWS])
                last.then_inc(rows_dve, 1)

            def gate_columns(l):
                dve.wait_ge(cols_turned, l + 1)
                for r in range(5):
                    got = ps[:, 5 + r // 2, r % 2 * NCH * ROWS:(r % 2 + 1) * NCH * ROWS].rearrange("p (c g) -> p c g", g=ROWS)
                    for d in range(2):
                        last = dve.tensor_copy(col[:, r, :, d, :], got[:, :, 32 * d:32 * d + H])
                last.then_inc(cols_ready, 1)

            conv_count = [0]

            def convolve(l, w):
                def tap(k, j, to, src, first=False, base=None, at_loop=None):
                    weight = column(tab_b[:, l, :], k + j * KC)
                    if first:
                        return dve.tensor_scalar(to, src, weight, column(tab_a[:, l, :], k + A_CB), ALU.mult, ALU.add)
                    return dve.scalar_tensor_tensor(to, src, weight, to, ALU.mult, ALU.add)

                mid = TAPS // 2
                order = [mid] + [j for j in range(TAPS) if j != mid]
                rows = NX // GRID_W
                zx = lambda t, k: t[:, k, 0:NX].rearrange("p (r c) -> p r c", c=GRID_W)
                for k0, along in ((0, "columns"), (KC // 2, "rows")):
                    for m, j in enumerate(j for j in order if along == "columns" or abs(j - mid) < rows):
                        o = j - mid
                        for k in (k0, k0 + 1):
                            if m:
                                dve.wait_ge(conv_step, conv_count[0] - 1)
                            n = GRID_W if along == "columns" else rows
                            b, e = max(0, -o), min(n, n - o)
                            if along == "columns":
                                to, src = zx(yc, k)[:, :, b:e], zx(z, k)[:, :, b + o:e + o]
                            else:
                                to, src = zx(yc, k)[:, b:e, :], zx(z, k)[:, b + o:e + o, :]
                            tap(k, j, to, src, m == 0).then_inc(conv_step, 1)
                            conv_count[0] += 1
                if w > NX:
                    base = conv_count[0]
                    with dve.Fori(0, KC // 2) as i:
                        for m, j in enumerate(order):
                            o = j - mid
                            b, e = max(0, -o), min(NC, NC - o)
                            for s in range(2):
                                if m:
                                    dve.wait_ge(conv_step, i * (2 * TAPS) + (base + 2 * m + s - 1))
                                k = i * 2 + s
                                part = lambda t, b, e: t[:, bass.ds(k, 1), NX + b:NX + e].rearrange("p k n -> p (k n)")
                                tap(k, j, part(yc, b, e), part(z, b + o, e + o), m == 0).then_inc(conv_step, 1)
                    conv_count[0] += KC * TAPS
                dve.wait_ge(conv_step, conv_count[0])

            def conv_norm(l, w):
                settle(dve.tensor_tensor(ssum[:, 0:w], yc[:, 0, 0:w], yc[:, 1, 0:w], ALU.add))
                settle(dve.tensor_tensor(ssum[:, 0:w], ssum[:, 0:w], yc[:, 2, 0:w], ALU.add))
                dve.tensor_tensor(ssum[:, 0:w], ssum[:, 0:w], yc[:, 3, 0:w], ALU.add).then_inc(yc_totalled, 1)
                chain = chain_of_conv(l, 0)
                dve.wait_ge(ss_summed, chain + 1)
                settle(dve.tensor_scalar(stat[:, 1, 0:w // P], ps[:, 4, 0:w // P], 1.0 / (KC * P), None, ALU.mult))
                diagonals(chain, w)
                for k in range(KC):
                    dve.tensor_tensor(yc[:, k, 0:w], yc[:, k, 0:w], wide[:, 0:w], ALU.subtract).then_inc(yc_dev, 1)
                reciprocals(chain_of_conv(l, 1), w)
                for k in range(KC):
                    dve.tensor_tensor(yc[:, k, 0:w], yc[:, k, 0:w], wide[:, 0:w], ALU.mult).then_inc(yc_norm, 1)

            def scan_steps(l):
                touched = set()
                for st in steps:
                    n, d, ch, t = st
                    o, kp = outs_before(l, n), count(kept, l, n)
                    if gives(l, st):
                        dve.wait_ge(mask_ready, o + 1)
                        dve.wait_ge(s_ready, o + 1)
                        if o >= 2:
                            dve.wait_ge(n_ready, o - 1)
                        dve.tensor_tensor(sw[n % 2][:].rearrange("p h t -> p (h t)"),
                                          ew[n % 2][:].rearrange("p h t -> p (h t)"), ps[:, 0, :], ALU.mult).then_inc(sw_ready, 1)
                    if keeps(st):
                        dve.wait_ge(dc_ready, kp + 1)
                        if inters(l, st):
                            dve.wait_ge(i_ready, count(inters, l, n) + 1)
                        if ch == 0:
                            dve.tensor_copy(flat2(state[d][:]), pair_banks(6)).then_inc(state_ready, 1)
                        else:
                            dve.wait_ge(state_ready, kp - 1)
                            for h in range(H):
                                last = dve.scalar_tensor_tensor(state[d][:, h, :], state[d][:, h, :], col[:, R_DEC, ch, d, h:h + 1],
                                                                head_ps(6, h), ALU.mult, ALU.add)
                            last.then_inc(state_ready, 1)
                    if gives(l, st):
                        dve.wait_ge(n_ready, o + 1)
                        if inters(l, st):
                            dve.wait_ge(isb_ready, count(inters, l, n) + 1)
                            total = dve.tensor_tensor(flat2(tot), pair_banks(2), flat2(isb[n % 2][:]), ALU.add)
                        else:
                            total = dve.tensor_copy(flat2(tot), pair_banks(2))
                        total.then_inc(tot_ready, 1)
                        dve.wait_ge(tot_ready, o + 1)
                        den = tot[:, :, P:E1].rearrange("p h o -> p (h o)")
                        settle(dve.scalar_tensor_tensor(stat[:, 2, 0:H], den, -1.0, den, ALU.mult, ALU.max))
                        settle(dve.tensor_tensor(stat[:, 2, 0:H], stat[:, 2, 0:H], col[:, R_EM, ch, d, :], ALU.max))
                        settle(dve.reciprocal(stat[:, 2, H:2 * H], stat[:, 2, 0:H]))
                        for h in range(H):
                            to = hm[:, t, h * P:(h + 1) * P]
                            by = stat[:, 2, H + h:H + h + 1]
                            if t in touched:
                                last = dve.scalar_tensor_tensor(to, tot[:, h, 0:P], by, to, ALU.mult, ALU.add)
                            else:
                                last = dve.tensor_scalar(to, tot[:, h, 0:P], by, None, ALU.mult)
                        settle(last)
                        touched.add(t)

            def mixer_out(l, w):
                nt = w // P
                heads = hm[:, 0:nt, :].rearrange("p t (h e) -> p (t h) e", e=P)
                squares = tmp[:].rearrange("p a n -> p (a n)")[:, 0:nt * DM].rearrange("p (g e) -> p g e", e=P)
                settle(dve.tensor_tensor(squares, heads, heads, ALU.mult))
                dve.tensor_reduce(stat[:, 1, 0:nt * H], squares, AX.X, ALU.add).then_inc(hm_squared, 1)
                dve.wait_ge(hm_root, l + 1)
                settle(dve.reciprocal(stat[:, 2, 0:nt * H], stat[:, 0, 0:nt * H]))
                dve.tensor_tensor(heads, heads, stat[:, 2, 0:nt * H].rearrange("p (g o) -> p g o", o=1).to_broadcast([P, nt * H, P]),
                                  ALU.mult).then_inc(hm_scaled, 1)
                for h in range(H):
                    dve.wait_ge(hm_turned, H * l + h + 1)
                    if h >= 2:
                        dve.wait_ge(h_lo_ready, KD * split_of(l, "y") + h - 1)
                    dve.scalar_tensor_tensor(tmp[:, 2 + h % 2, 0:w], slot_ps(2 + h % 2, w), tab_a[:, l, A_MG + h:A_MG + h + 1],
                                             qkvo[:, 3 * H + h, 0:w], ALU.mult, ALU.mult).then_inc(ym_ready, 1)

            dve.wait_ge(tab_turned, 1)
            dve.tensor_copy(tab_a[:], ps[:, 4, 0:DEPTH * P].rearrange("p (l n) -> p l n", l=DEPTH))
            for l in range(DEPTH):
                dve.tensor_copy(tab_b[:, l, :], ps[:, 4, (DEPTH + l) * P:(DEPTH + l) * P + TAPS * KC])
            settle(dve.tensor_copy(tab_c[:], ps[:, 5, 0:NCR]))
            dve.tensor_scalar(bq[:], tab_a[:, :, A_BIN:A_BIN + H], float(P) ** -0.5, None, ALU.mult).then_inc(tab_read, 1)
            for k in range(KD):
                dve.wait_ge(x_turned, k + 1)
                dve.tensor_copy(xres[:, k, :], slot_ps(k % 2, T)).then_inc(x_copied, 1)
            for l in range(DEPTH):
                dve.wait_ge(mod_used, NM * (l + 1))
                mod = tmp[:, 1, 0:2 * NM].rearrange("p (m o) -> p m o", o=2)
                settle(dve.tensor_tensor(mod, ps[:, 7 - l, 0:2 * NM].rearrange("p (m o) -> p m o", o=2),
                                         tab_a[:, l, 0:NM].rearrange("p (m o) -> p m o", o=1).to_broadcast([P, NM, 2]), ALU.add))
                for which, gain in enumerate((A_N1, A_NM, A_N2)):
                    for o in range(2):
                        part = lambda j: mod[:, (3 * which + j) * KD:(3 * which + j + 1) * KD, o]
                        dve.tensor_copy(shift[:, l, which, o, :], part(0))
                        dve.scalar_tensor_tensor(coef[:, l, which, o, :], part(1), 1.0, tab_a[:, l, gain:gain + KD], ALU.add, ALU.mult)
                        last = dve.tensor_scalar(gate[:, l, which, o, :], part(2), 1.0 if which == 1 else 0.5, None, ALU.mult)
                settle(last)

            for q in phases:
                l, w, name = q["l"], q["w"], q["name"]
                if name == "up" and q["half"] == 0:
                    norm(3 * l + (0 if q["up"] is ffn1_up else 2))
                if name == "glu":
                    norm(3 * l + 1)
                    gate_rows(l)
                if name == "q":
                    gate_columns(l)
                    convolve(l, w)
                if name == "out":
                    conv_norm(l, w)
                    scan_steps(l)
                    mixer_out(l, w)

                def pair(i, p, k_next, q=q, l=l, w=w, name=name):
                    if name == "up":
                        dve.wait_ge(slot_read[0], p + 1)
                        dve.wait_ge(unit_done, p * 2 + 2)
                        if q["ups"] or not isinstance(i, int) or i > 0:
                            dve.wait_ge(a_lo_ready, i + KF * q["ups"])
                        dve.tensor_tensor(tmp[:, 1, 0:w], tmp[:, 0, 0:w], slot_ps(1, w), ALU.mult).then_inc(slot_read[1], 1)
                        dve.wait_ge(a_hi_ready, i + (KF * q["ups"] + 1))
                        dve.tensor_tensor(chunk(a_lo, i, w), tmp[:, 1, 0:w], chunk(a_hi, i, w).bitcast(F32),
                                          ALU.subtract).then_inc(a_lo_ready, 1)
                    if name == "glu":
                        dve.wait_ge(slot_read[1], p + 1)
                        dve.scalar_tensor_tensor(chunk(z, i, w), slot_ps(0, w), column(tab_c, i + l * 2 * KC), tmp[:, 0, 0:w],
                                                 ALU.add, ALU.mult).then_inc(slot_read[0], 1)
                    if name in ("down", "out"):
                        for s in range(2):
                            dve.wait_ge(unit_done, p * 2 + (s + 1))
                            j = i * 2 + s
                            for o, (b, e) in enumerate(groups(w)):
                                to = xres[:, j, b:e] if isinstance(j, int) else xres[:, bass.ds(j, 1), b:e].rearrange("p k n -> p (k n)")
                                last = dve.scalar_tensor_tensor(to, slot_ps(s, w)[:, b:e], column(gate[:, l, q["gate"], o, :], j),
                                                                to, ALU.mult, ALU.add)
                            last.then_inc(slot_read[s], 1)

                if name not in ("q", "kv", "o"):
                    run_pairs(dve, q, pair)

            r = 3 * DEPTH
            reciprocals(chain_of_norm(r), NX)
            for k in range(KD):
                if k >= 2:
                    dve.wait_ge(o_turned, k - 1)
                settle(dve.tensor_tensor(tmp[:, k % 2, 0:NX], xres[:, k, 0:NX], wide[:, 0:NX], ALU.mult))
                dve.tensor_scalar(tmp[:, 2 + k % 2, 0:NX], tmp[:, k % 2, 0:NX], tab_c[:, C_FIN + k:C_FIN + k + 1], None,
                                  ALU.mult).then_inc(hf_ready, 1)

        @block.tensor
        def _(pe):
            def sums(chain, w, ready, value):
                pe.wait_ge(ready, value)
                for t in range(w // P):
                    last = pe.matmul(ps[:, 4, t:t + 1], ssum[:, t * P:(t + 1) * P], ones[:, 0:1], start=True, stop=True)
                last.then_inc(ss_summed, 1)
                pe.wait_ge(diag_ready, chain + 1)
                for b, e in groups(w):
                    last = pe.matmul(wide[:, b:e], ones[:], tmp[:, 0, b:e], start=True, stop=True)
                last.then_inc(wide_ready, 1)

            def unit(q, s, moving_hi, moving_lo, wait_k=None):
                w, k_all = q["w"], q["k"]
                for k in range(k_all):
                    if wait_k:
                        wait_k(k)
                    hi, lo = w_hi[s][:, k * P:(k + 1) * P], w_lo[s][:, k * P:(k + 1) * P]
                    for m, (wt, mv) in enumerate(((hi, moving_hi), (hi, moving_lo), (lo, moving_hi))):
                        for b, e in groups(w):
                            last = pe.matmul(slot_ps(s, w)[:, b:e], wt, mv[:, k, b:e],
                                             start=(k == 0 and m == 0), stop=(k == k_all - 1 and m == 2))
                last.then_inc(unit_done, 1)

            def gate_product(l):
                pe.wait_ge(gw_lo_ready, l + 1)
                pe.wait_ge(h_lo_ready, KD * (split_of(l, "mix") + 1))
                for k in range(KD):
                    for m, (wt, mv) in enumerate(((gw_hi, h_hi), (gw_hi, h_lo), (gw_lo, h_hi))):
                        for bank, b, e in ((7, 0, NX), (4, NX, T)):
                            last = pe.matmul(ps[0:GR, bank, 0:e - b], wt[:, k, :], mv[:, k, b:e],
                                             start=(k == 0 and m == 0), stop=(k == KD - 1 and m == 2))
                last.then_inc(gates_ready, 1)

            def gate_columns(l):
                pe.wait_ge(rows_act, 3 * (l + 1))
                pe.wait_ge(rows_dve, 3 * (l + 1))
                for r in range(5):
                    for ch in range(NCH):
                        first = r % 2 * NCH * ROWS + ch * ROWS
                        last = pe.transpose(ps[:, 5 + r // 2, first:first + ROWS], rq[:, r, ch, :], ident[0:ROWS, 0:ROWS])
                last.then_inc(cols_turned, 1)

            def turn_values(l):
                kv = phase("kv", l)
                for s in range(2):
                    pe.wait_ge(slot_read[s], phase("out", l)["p0"])
                pe.wait_ge(cols_ready, l + 1)
                for i in range(2 * TT):
                    if i >= 4:
                        pe.wait_ge(vk_read, 2 * TT * l + i - 3)
                    first, t = (2 * H, i) if i < TT else (H, i - TT)
                    for h in range(H):
                        last = pe.transpose(ps[:, 4 + i % 4, h * P:(h + 1) * P], qkvo[:, first + h, t * P:(t + 1) * P], ident[:])
                    last.then_inc(vk_turned, 1)
                pe.wait_ge(vk_read, 2 * TT * (l + 1))

            def scan_steps(l):
                def scores(st):
                    n, d, ch, t = st
                    o = outs_before(l, n)
                    tile = slice(t * P, (t + 1) * P)
                    if o:
                        pe.wait_ge(sw_ready, o)
                    for h in range(H):
                        last = pe.matmul(ps[:, 0, h * P:(h + 1) * P], qkvo[:, H + h, tile], qkvo[:, h, tile], start=True, stop=True)
                    last.then_inc(s_ready, 1)
                    if o:
                        pe.wait_ge(e_ready, o)
                    for h in range(H):
                        last = pe.matmul(ps[:, 1, h * P:(h + 1) * P], sel[:, d, h, :], r1_row[:, ch, :], start=True, stop=True)
                    last.then_inc(b_ready, 1)

                if gives(l, steps[0]):
                    scores(steps[0])
                for st in steps:
                    n, d, ch, t = st
                    o, kp = outs_before(l, n), count(kept, l, n)
                    tile = slice(t * P, (t + 1) * P)
                    if n + 1 < len(steps) and gives(l, steps[n + 1]):
                        scores(steps[n + 1])
                    if keeps(st):
                        pe.wait_ge(vw_ready, kp + 1)
                        if kp:
                            pe.wait_ge(state_ready, kp)
                        for h in range(H):
                            last = pe.matmul(head_ps(6, h), kt[:, t, h * P:(h + 1) * P], vw[n % 2][:, h, :], start=True, stop=True)
                        last.then_inc(dc_ready, 1)
                    if inters(l, st):
                        pe.wait_ge(state_ready, count(kept, l, n - 1))
                        it = count(inters, l, n)
                        if it:
                            pe.wait_ge(isb_ready, it)
                        for h in range(H):
                            last = pe.matmul(head_ps(4, h), qkvo[:, h, tile], state[d][:, h, :], start=True, stop=True)
                        last.then_inc(i_ready, 1)
                    if gives(l, st):
                        pe.wait_ge(sw_ready, o + 1)
                        if o:
                            pe.wait_ge(tot_ready, o)
                        for h in range(H):
                            last = pe.matmul(head_ps(2, h), sw[n % 2][:, h, :], vt[:, t, h, :], start=True, stop=True)
                        last.then_inc(n_ready, 1)

            def turn_mixer(l, w):
                pe.wait_ge(hm_scaled, l + 1)
                for h in range(H):
                    if h >= 2:
                        pe.wait_ge(ym_ready, H * l + h - 1)
                    for t in range(w // P):
                        last = pe.transpose(slot_ps(2 + h % 2, w)[:, t * P:(t + 1) * P], hm[:, t, h * P:(h + 1) * P], ident[:])
                    last.then_inc(hm_turned, 1)

            pe.wait_ge(const_ready, 4)
            pe.wait_ge(tab_loaded, 16 * TAB_DMAS)
            for l in range(DEPTH):
                pe.transpose(ps[:, 4, l * P:(l + 1) * P], tabs[:, l, :], ident[:])
                pe.transpose(ps[:, 4, (DEPTH + l) * P:(DEPTH + l) * P + TAPS * KC], tabs[0:TAPS * KC, DEPTH + l, :],
                             ident[0:TAPS * KC, 0:TAPS * KC])
            pe.transpose(ps[:, 5, 0:NCR], tabs[0:NCR, 2 * DEPTH, :], ident[0:NCR, 0:NCR]).then_inc(tab_turned, 1)
            pe.wait_ge(in_loaded, 32)
            for k in range(KD):
                if k >= 2:
                    pe.wait_ge(x_copied, k - 1)
                for t in range(TT):
                    last = pe.transpose(slot_ps(k % 2, T)[:, t * P:(t + 1) * P], tok[:, t, k * P:(k + 1) * P], ident[:])
                last.then_inc(x_turned, 1)
            pe.wait_ge(silu_ready, 1)
            for l in range(DEPTH):
                with pe.Fori(0, NM // 2) as i:
                    for s in range(2):
                        pe.wait_ge(mod_loaded[s], i * 16 + (16 * (NM // 2) * l + 16))
                        for k in range(KD):
                            last = pe.matmul(ps[:, 7 - l, bass.ds(i * 4 + 2 * s, 2)], mraw[s][:, k, :], silu_c[:, k, :],
                                             start=(k == 0), stop=(k == KD - 1))
                        last.then_inc(mod_used, 1)

            for s in range(2):
                pe.wait_ge(x_copied, KD)
            for q in phases:
                l, w, name = q["l"], q["w"], q["name"]
                moving = (a_hi, a_lo) if name == "down" else (h_hi, h_lo)
                wait_k = None
                if name == "up" and q["half"] == 0:
                    r = 3 * l + (0 if q["up"] is ffn1_up else 2)
                    sums(chain_of_norm(r), w, ss_added, KD * (r + 1))
                    n = KD * norm_place[r]
                    wait_k = lambda k, n=n: pe.wait_ge(h_lo_ready, n + k + 1)
                if name == "glu":
                    sums(chain_of_norm(3 * l + 1), T, ss_added, KD * (3 * l + 2))
                    gate_product(l)
                if name == "q":
                    gate_columns(l)
                if name == "out":
                    turn_values(l)
                    sums(chain_of_conv(l, 0), w, yc_totalled, l + 1)
                    sums(chain_of_conv(l, 1), w, yc_summed, KC * (l + 1))
                    scan_steps(l)
                    turn_mixer(l, w)
                    n = KD * split_of(l, "y")
                    wait_k = lambda k, n=n: pe.wait_ge(h_lo_ready, n + k + 1)
                if name == "down":
                    n = KF * q["ups"] - KF
                    wait_k = lambda k, n=n: pe.wait_ge(a_lo_ready, n + k + 1)

                def pair(i, p, wait_k=None, q=q, moving=moving):
                    for s in range(2):
                        pe.wait_ge(lo_ready, p * 2 + (s + 1))
                        if not isinstance(p, int) or p > 0:
                            pe.wait_ge(slot_read[s], p)
                        unit(q, s, *moving, wait_k=wait_k if s == 0 else None)

                pair(0, q["p0"], wait_k)
                with pe.Fori(1, q["pairs"]) as i:
                    pair(i, i + q["p0"])

            sums(chain_of_norm(3 * DEPTH), NX, ss_added, KD * (3 * DEPTH + 1))
            for k in range(KD):
                pe.wait_ge(hf_ready, KD * 3 * DEPTH + k + 1)
                if k >= 2:
                    pe.wait_ge(out_read, k - 1)
                for t in range(TX):
                    last = pe.transpose(ps[:, 2 * (k % 2), t * P:(t + 1) * P], tmp[:, 2 + k % 2, t * P:(t + 1) * P], ident[:])
                last.then_inc(o_turned, 1)


_INS = ["x", "c", "ctx", "c_ctx", "w_mod", "b_mod", "norm_ffn1", "ffn1_up", "ffn1_down", "norm_mix", "w_in", "b_in",
        "mlstm_norm", "conv_w", "conv_b", "conv_norm_g", "conv_norm_b", "w_out", "norm_ffn2", "ffn2_up", "ffn2_down",
        "norm_final"]


def kernel(**inputs):
    import numpy as _np
    import concourse.bacc as _bacc
    from concourse import mybir as _mybir
    from concourse.bass_utils import run_bass_kernel_spmd as _run

    nc = _bacc.Bacc("TRN2", target_bir_lowering=False, num_devices=1)
    arrays, args = {}, []
    for name in _INS:
        a = _np.ascontiguousarray(inputs[name])
        arrays[f"in_{name}_dram"] = a
        args.append(nc.dram_tensor(f"in_{name}_dram", a.shape, _mybir.dt.from_np(a.dtype), kind="ExternalInput").ap())
    shape = inputs["x"].shape
    args.append(nc.dram_tensor("out_0_dram", shape, _mybir.dt.float32, kind="ExternalOutput").ap())
    mixer_dit_kernel(nc, *args)
    r = _run(nc, [arrays], core_ids=[0])
    return r.results[0]["out_0_dram"]
```

```python
import concourse.bass as bass
from concourse import mybir
from contextlib import ExitStack

F32 = mybir.dt.float32
F32R = mybir.dt.float32r
ALU = mybir.AluOpType
ACT = mybir.ActivationFunctionType
AX = mybir.AxisListType

P = 128
EPS = 1e-6
GRID_W = 64


def mixer_dit_kernel(nc, x, c, ctx_in, c_ctx, w_mod, b_mod, norm_ffn1, ffn1_up, ffn1_down, norm_mix, w_in, b_in,
                     mlstm_norm, conv_w, conv_b, conv_norm_g, conv_norm_b, w_out, norm_ffn2, ffn2_up, ffn2_down,
                     norm_final, out):
    _, NX, D = x.shape
    NC = ctx_in.shape[1]
    T = NX + NC
    DEPTH = w_mod.shape[0]
    KD = D // P
    NM = w_mod.shape[2] // P
    FF = ffn1_down.shape[1]
    KF = FF // P // 2
    DM = mlstm_norm.shape[1]
    H = DM // P
    KC = conv_norm_g.shape[1] // P
    TAPS = conv_w.shape[1]
    G0 = 4 * DM
    U0 = G0 + 4 * H
    TX, TT = NX // P, T // P
    NCH = TT
    CCH = NC // P
    E1 = P + 1
    ROWS = 32 + H
    GR = 96 + H
    R_CS, R_WK, R_INTER, R_EM, R_DEC = range(5)
    assert D == 2 * DM and H == 4 and KC == 4 and T == 768 and FF % (2 * P) == 0

    phases = []

    def add_phase(name, l, k, pairs, width, **more):
        before = sum(q["pairs"] for q in phases)
        phases.append(dict(name=name, l=l, k=k, pairs=pairs, w=width, p0=before, **more))

    for l in range(DEPTH):
        last = l == DEPTH - 1
        WL = NX if last else T
        for half in range(2):
            add_phase("up", l, KD, KF, T, up=ffn1_up, half=half)
            add_phase("down", l, KF, KD // 2, T, down=ffn1_down, half=half, gate=0, norm=3 * l + 1 if half else None)
        add_phase("glu", l, KD, KC, WL)
        add_phase("q", l, KD, H // 2, WL)
        add_phase("kv", l, KD, H, T)
        add_phase("o", l, KD, H // 2, WL)
        add_phase("out", l, KD, KD // 2, WL, gate=1, norm=3 * l + 2)
        for half in range(2):
            add_phase("up", l, KD, KF, WL, up=ffn2_up, half=half)
            add_phase("down", l, KF, KD // 2, WL, down=ffn2_down, half=half, gate=2, norm=3 * l + 3 if half else None)

    M0 = 2 * KD
    rides = {}
    ffn1_0 = [q for q in phases if q["l"] == 0 and q["name"] in ("up", "down")][:4]
    for q, ride in zip(ffn1_0, ((2, 2, 2), (4, 2, 4), (2, 2, 2))):
        rides[id(q)] = (0, ride)
    for l in range(1, DEPTH):
        before = [q for q in phases if q["l"] == l - 1 and q["name"] in ("up", "down")][4:]
        for q, ride in zip(before, ((2, 2, 2), (4, 4, 4), (2, 2, 2), (2, 4, 2))):
            rides[id(q)] = (l, ride)
    made, ridden = {l: M0 if l == 0 else 0 for l in range(DEPTH)}, 0
    for q in phases:
        if id(q) in rides:
            l, ride = rides[id(q)]
            n = ride[0] + ride[1] * (q["pairs"] - 2) + ride[2]
            q["mods"] = (l, ride, made[l], ridden, made[l] + n == NM)
            q["mods_first"] = made[l] == (M0 if l == 0 else 0)
            made[l] += n
            ridden += n
    assert all(n == NM for n in made.values())
    for n, q in enumerate(phases):
        q["next"] = phases[n + 1] if n + 1 < len(phases) else None
        q["ups"] = sum(1 for r in phases[:n] if r["name"] == "up")

    def ridden_after(q):
        _, ride, _, ridden0, _ = q["mods"]
        return ridden0 + ride[0] + ride[1] * (q["pairs"] - 2) + ride[2]

    def phase(name, l, nth=0):
        return [q for q in phases if q["name"] == name and q["l"] == l][nth]

    def width_of_norm(r):
        return NX if r >= 3 * (DEPTH - 1) + 2 else T

    def split_of(l, what):
        return 4 * l + {"ffn1": 0, "mix": 1, "y": 2, "ffn2": 3}[what]

    norm_place = {}
    for l in range(DEPTH):
        norm_place[3 * l], norm_place[3 * l + 1], norm_place[3 * l + 2] = (
            split_of(l, "ffn1"), split_of(l, "mix"), split_of(l, "ffn2"))

    def lows_before(m):
        return m // 4 * (5 * KD // 2) + (0, KD // 2, KD, 2 * KD)[m % 4]

    def tile_of(d, ch):
        return (TX + ch if ch < CCH else ch - CCH) if d == 0 else TT - 1 - ch

    steps = [(2 * ch + d, d, ch, tile_of(d, ch)) for ch in range(NCH) for d in range(2)]

    def gives(l, step):
        return l < DEPTH - 1 or step[2] >= CCH

    def outs_before(l, n):
        return sum(gives(m, s) for m in range(l) for s in steps) + sum(gives(l, s) for s in steps[:n])

    def keeps(step):
        return step[2] < NCH - 1

    def kept(l, step):
        return keeps(step)

    def inters(l, step):
        return gives(l, step) and step[2] > 0

    def count(pred, l, n):
        return sum(pred(m, s) for m in range(l) for s in steps) + sum(pred(l, s) for s in steps[:n])

    with ExitStack() as stack:
        SB0 = 16512
        place = [SB0]

        def region(size):
            at = place[0]
            place[0] += (size + 31) // 32 * 32
            assert place[0] <= 229344, place[0]
            return at

        def at(name, shape, offset, dt=F32):
            return nc.alloc_sbuf_tensor_at(name, shape, dt, offset=offset)

        def sem(name):
            return stack.enter_context(nc.semaphore(name))

        r_x = region(KD * T * 4)
        r_h = region(2 * KD * T * 4)
        r_a = region(2 * KF * T * 4)
        UNIT = max(KD, KF) * P
        xres = at("xres", [P, KD, T], r_x)
        h_hi = at("h_hi", [P, KD, T], r_h, F32R)
        h_lo = at("h_lo", [P, KD, T], r_h + KD * T * 4, F32R)
        a_hi = at("a_hi", [P, KF, T], r_a, F32R)
        a_lo = at("a_lo", [P, KF, T], r_a + KF * T * 4, F32R)
        raw = [at(f"raw{s}", [P, UNIT], region(UNIT * 4)) for s in range(2)]
        w_hi = [at(f"w_hi{s}", [P, UNIT], region(UNIT * 4), F32R) for s in range(2)]
        w_lo = [at(f"w_lo{s}", [P, UNIT], region(UNIT * 4), F32R) for s in range(2)]
        r_m = region(KC * T * 4)
        tmp = at("tmp", [P, 4, T], region(4 * T * 4))
        ssum = at("ssum", [P, T], region(T * 4))
        ident = at("ident", [P, P], region(P * 4))
        ones = at("ones", [P, P], region(P * 4))
        sel = at("sel", [ROWS, 2, H, P], region(2 * H * P * 4))
        tab_a = at("tab_a", [P, DEPTH, P], region(DEPTH * P * 4))
        tab_b = at("tab_b", [P, DEPTH, TAPS * KC], region(DEPTH * TAPS * KC * 4))
        NCR = DEPTH * 2 * KC + 3 * KD
        tab_c = at("tab_c", [P, NCR], region(NCR * 4))
        coef = at("coef", [P, DEPTH, 3, 2, KD], region(DEPTH * 3 * 2 * KD * 4))
        shift = at("shift", [P, DEPTH, 3, 2, KD], region(DEPTH * 3 * 2 * KD * 4))
        gate = at("gate", [P, DEPTH, 3, 2, KD], region(DEPTH * 3 * 2 * KD * 4))
        silu_c = at("silu_c", [P, KD, 2], region(KD * 2 * 4))
        bq = at("bq", [P, DEPTH, H], region(DEPTH * H * 4))
        gbias = at("gbias", [P, DEPTH], region(DEPTH * 4))
        stat = at("stat", [P, 3, TT * H], region(3 * TT * H * 4))
        eps = at("eps", [P, 1], region(4))
        begun = at("begun", [P, 1], region(4))
        rsm = at("rsm", [ROWS, 3, NCH], region(3 * NCH * 4))
        qkvo = at("qkvo", [P, 4 * H, T], r_a)
        kt = at("kt", [P, TT, DM], r_a + 2 * H * T * 4)
        z = at("z", [P, KC, T], r_a + 4 * H * T * 4)
        r_left = r_a + (4 * H + KC) * T * 4
        r1_row = at("r1_row", [ROWS, NCH, P], r_left)
        col = at("col", [P, 5, NCH, 2, H], r_left + T * 4)
        rt = at("rt", [ROWS, 9, T], r_a)
        rq = at("rq", [ROWS, 5, NCH, P], r_a + 9 * T * 4)
        yc = at("yc", [P, KC, T], r_m)
        mraw = [at(f"mraw{s}", [P, KD, P], r_m + s * KD * P * 4) for s in range(2)]
        macc = [at(f"macc{s}", [P, 2, P], r_m + 2 * KD * P * 4 + s * 2 * P * 4) for s in range(2)]
        gw = at("gw", [P, KD, GR], r_m)
        gw_hi = at("gw_hi", [P, KD, GR], r_m + KD * GR * 4, F32R)
        gw_lo = at("gw_lo", [P, KD, GR], r_m + 2 * KD * GR * 4, F32R)
        gw16 = at("gw16", [P, KD, 4 * H], r_m + 3 * KD * GR * 4)
        HE = (H * E1 * 4 + 31) // 32 * 32
        vw = [at(f"vw{s}", [P, H, E1], r_h + s * HE) for s in range(2)]
        sw = [at(f"sw{s}", [P, H, P], r_h + 2 * HE + s * H * P * 4) for s in range(2)]
        r_h1 = r_h + KC * T * 4
        hm = at("hm", [P, TT, DM], r_h1)
        r_h2 = r_h + KD * T * 4
        vt = at("vt", [P, TT, H, E1], r_h2)
        state = [at(f"state{d}", [P, H, E1], r_h2 + (TT + d) * HE) for d in range(2)]
        isb = [at(f"isb{s}", [P, H, E1], r_h2 + (TT + 2 + s) * HE) for s in range(2)]
        r_h4 = r_h2 + (TT + 4) * HE
        ew = [at("ew0", [P, H, P], r_h + 2 * HE + 2 * H * P * 4), at("ew1", [P, H, P], r_h4)]
        assert r_h4 + H * P * 4 <= r_a
        tok = at("tok", [P, TT, D], r_a)
        tabs = at("tabs", [P, 2 * DEPTH + 1, P], r_a + TT * D * 4)
        m_first = [at("m_first0", [P, KD, KD * P], r_h),
                   at("m_first1", [P, KD, KD * P], r_a + TT * D * 4 + (2 * DEPTH + 1) * P * 4)]
        otok = at("otok", [P, TX, D], r_a)
        tot = tmp[:, 0, 0:H * E1].rearrange("p (h e) -> p h e", h=H)

        ps = stack.enter_context(nc.psum_tensor("ps", [P, 8, 512], F32))

        def slot_ps(s, w):
            return ps[:, 2 * s:2 * s + 2, :].rearrange("p b n -> p (b n)")[:, 0:w]

        wide = ps[:, 5:7, :].rearrange("p b n -> p (b n)")

        def groups(w):
            return [(0, NX)] + ([(NX, T)] if w > NX else [])

        def pair_banks(b):
            return ps[:, b:b + 2, 0:2 * E1]

        def head_ps(b, h):
            return ps[:, b + h // 2, h % 2 * E1:h % 2 * E1 + E1]

        def flat2(t):
            return t.rearrange("p (b h) e -> p b (h e)", b=2)

        def chunk(t, j, w):
            if isinstance(j, int):
                return t[:, j, 0:w]
            return t[:, bass.ds(j, 1), 0:w].rearrange("p k n -> p (k n)")

        def column(t, j):
            return t[:, j:j + 1] if isinstance(j, int) else t[:, bass.ds(j, 1)]

        in_loaded = sem("in_loaded")
        tab_loaded = sem("tab_loaded")
        bias_cleared = sem("bias_cleared")
        const_ready = sem("const_ready")
        const_cleared = sem("const_cleared")
        tab_turned = sem("tab_turned")
        tab_read = sem("tab_read")
        silu_ready = sem("silu_ready")
        mod_loaded = [sem(f"mod_loaded{s}") for s in range(2)]
        mod_step = sem("mod_step")
        mod_summed = sem("mod_summed")
        mod_read = sem("mod_read")
        first_mods = [sem(f"first_mods{j}") for j in range(2)]
        first_summed = sem("first_summed")
        x_turned = sem("x_turned")
        x_copied = sem("x_copied")
        raw_loaded = [sem(f"raw_loaded{s}") for s in range(2)]
        hi_ready = sem("hi_ready")
        lo_ready = sem("lo_ready")
        unit_done = sem("unit_done")
        slot_read = [sem(f"slot_read{s}") for s in range(2)]
        a_hi_ready = sem("a_hi_ready")
        a_lo_ready = sem("a_lo_ready")
        sq_ready = sem("sq_ready")
        ss_added = sem("ss_added")
        ss_summed = sem("ss_summed")
        root_begun = sem("root_begun")
        root_ready = sem("root_ready")
        factor_ready = sem("factor_ready")
        wide_ready = sem("wide_ready")
        hf_ready = sem("hf_ready")
        h_rounded = sem("h_rounded")
        h_hi_ready = sem("h_hi_ready")
        h_lo_ready = sem("h_lo_ready")
        h_even_ready = sem("h_even_ready")
        dve_self = sem("dve_self")
        gw_loaded = sem("gw_loaded")
        gw_cleared = sem("gw_cleared")
        gw_ready = sem("gw_ready")
        gw_hi_ready = sem("gw_hi_ready")
        gw_lo_ready = sem("gw_lo_ready")
        gates_ready = sem("gates_ready")
        rows_dve = sem("rows_dve")
        rows_act = sem("rows_act")
        cols_turned = sem("cols_turned")
        cols_ready = sem("cols_ready")
        conv_step = sem("conv_step")
        yc_totalled = sem("yc_totalled")
        yc_dev = sem("yc_dev")
        yc_sq = sem("yc_sq")
        yc_summed = sem("yc_summed")
        yc_norm = sem("yc_norm")
        yc_act = sem("yc_act")
        vk_turned = sem("vk_turned")
        vk_read = sem("vk_read")
        ones_ready = sem("ones_ready")
        s_ready = sem("s_ready")
        b_ready = sem("b_ready")
        e_ready = sem("e_ready")
        mask_ready = sem("mask_ready")
        sw_ready = sem("sw_ready")
        vw_ready = sem("vw_ready")
        n_ready = sem("n_ready")
        i_ready = sem("i_ready")
        isb_ready = sem("isb_ready")
        dc_ready = sem("dc_ready")
        state_ready = sem("state_ready")
        tot_ready = sem("tot_ready")
        hm_squared = sem("hm_squared")
        hm_root = sem("hm_root")
        hm_scaled = sem("hm_scaled")
        hm_turned = sem("hm_turned")
        ym_ready = sem("ym_ready")
        o_turned = sem("o_turned")
        out_read = sem("out_read")
        stored = sem("stored")

        A_N1 = NM
        A_NM, A_N2, A_MG = A_N1 + KD, A_N1 + 2 * KD, A_N1 + 3 * KD
        A_CB, A_CG, A_CN, A_BIN = A_MG + H, A_MG + H + KC, A_MG + H + 2 * KC, A_MG + H + 3 * KC
        assert A_BIN + 4 * H == P
        C_FIN = DEPTH * 2 * KC
        C_C = C_FIN + KD
        TAB_DMAS = DEPTH * 10 + DEPTH + 3 + DEPTH * 4
        GATE_ROWS = (0, 64, 32, 96)

        def as_rows(v):
            return v.rearrange("(r f) -> r f", f=P)

        def weights_of(q, i, s):
            l, name = q["l"], q["name"]
            if name == "up":
                w, at_col = q["up"][l], i * P + (s * FF + q["half"] * KF * P)
            elif name == "down":
                w, at_col = q["down"][l][q["half"] * KF * P:(q["half"] + 1) * KF * P], i * (2 * P) + s * P
            elif name == "glu":
                w, at_col = w_in[l], i * P + (U0 + s * KC * P)
            elif name == "out":
                w, at_col = w_out[l], i * (2 * P) + s * P
            else:
                w, at_col = w_in[l], i * (2 * P) + ({"q": 0, "kv": DM, "o": 3 * DM}[name] + s * P)
            return w.rearrange("(k p) n -> p k n", p=P)[:, :, bass.ds(at_col, P)]

        def chain_of_norm(r):
            return 5 * (r // 3) + (0, 1, 4)[r % 3]

        def chain_of_conv(l, which):
            return 5 * l + 2 + which

        def roots_before(chain):
            return chain - sum(chain_of_conv(l, 0) < chain for l in range(DEPTH))

        def wides_before(chain):
            def width(n):
                l, which = divmod(n, 5)
                if which in (2, 3):
                    return phase("out", l)["w"]
                return width_of_norm(3 * l + (0, 1, None, None, 2)[which])
            return sum(len(groups(width(n))) for n in range(chain))

        def run_pairs(engine, q, pair):
            n = q["pairs"]
            ml, ride, unit0, ridden0, _ = q.get("mods") or (0, (0, 0, 0), 0, 0, False)

            def riders(i, before, each):
                return [(ml, i * each + (unit0 + before + m), i * each + (ridden0 + before + m), (ridden0 + before + m) % 2)
                        for m in range(each)]

            pair(0, q["p0"], q["k"], riders(0, 0, ride[0]))
            if n > 2:
                with engine.Fori(1, n - 1) as i:
                    pair(i, i + q["p0"], q["k"], riders(i, ride[0] - ride[1], ride[1]))
            pair(n - 1, q["p0"] + n - 1, q["next"]["k"] if q["next"] else 0,
                 riders(0, ride[0] + ride[1] * (n - 2), ride[2]))

        block = stack.enter_context(nc.Block())

        @block.sync
        def _(sp):
            for j in range(2):
                sp.dma_start(m_first[j][:], w_mod[0].rearrange("(k p) n -> p k n", p=P)[:, :, j * D:(j + 1) * D]).then_inc(first_mods[j], 16)
            sp.dma_start(tok[:, 0:TX, :], x[0].rearrange("(t p) d -> p t d", p=P)).then_inc(in_loaded, 16)
            sp.dma_start(tok[:, TX:TT, :], ctx_in[0].rearrange("(t p) d -> p t d", p=P)).then_inc(in_loaded, 16)

            def load(q, i, s):
                sp.dma_start(raw[s][:, 0:q["k"] * P].rearrange("p (k n) -> p k n", n=P),
                             weights_of(q, i, s)).then_inc(raw_loaded[s], 16)

            for q in phases:
                first = 0
                if q["p0"] == 0:
                    load(q, 0, 0)
                    load(q, 0, 1)
                    first = 1
                if q["name"] == "glu":
                    before = [r for r in phases if r.get("mods") and r["p0"] < q["p0"]][-1]
                    sp.wait_ge(mod_summed, ridden_after(before))
                    sp.dma_start(gw16[:], w_in[q["l"]].rearrange("(k p) n -> p k n", p=P)[:, :, G0:U0]).then_inc(gw_loaded, 16)
                with sp.Fori(first, q["pairs"]) as i:
                    for s in range(2):
                        sp.wait_ge(lo_ready, i * 2 + (2 * q["p0"] + s - 1))
                        load(q, i, s)

            sp.wait_ge(out_read, KD)
            for t in range(TX):
                sp.dma_start(out[0, t * P:(t + 1) * P, :], otok[:, t, :]).then_inc(stored, 16)
            sp.wait_ge(stored, 16 * TX)

        @block.gpsimd
        def _(pool):
            pool.memset(gbias[:], 0.0).then_inc(bias_cleared, 1)
            pool.wait_ge(bias_cleared, 1)
            for l in range(DEPTH):
                for j, row in enumerate(GATE_ROWS):
                    pool.dma_start(gbias[row:row + H, l:l + 1],
                                   b_in[l, G0 + j * H:G0 + (j + 1) * H].rearrange("(h o) -> h o", o=1)).then_inc(tab_loaded, 16)
                r = 0
                for v in (b_mod[l], norm_ffn1[l], norm_mix[l], norm_ffn2[l], mlstm_norm[l], conv_b[l],
                          conv_norm_g[l], conv_norm_b[l], b_in[l, 0:G0]):
                    n = v.shape[0] // P
                    pool.dma_start(tabs[r:r + n, l, :], as_rows(v)).then_inc(tab_loaded, 16)
                    r += n
                pool.dma_start(tabs[0:TAPS * KC, DEPTH + l, :],
                               conv_w[l].rearrange("t (c f) -> (t c) f", f=P)).then_inc(tab_loaded, 16)
                pool.dma_start(tabs[l * 2 * KC:(l + 1) * 2 * KC, 2 * DEPTH, :],
                               as_rows(b_in[l, U0:U0 + 2 * KC * P])).then_inc(tab_loaded, 16)
            for v, r in ((norm_final, C_FIN), (c[0], C_C), (c_ctx, C_C + KD)):
                pool.dma_start(tabs[r:r + KD, 2 * DEPTH, :], as_rows(v)).then_inc(tab_loaded, 16)

            pool.memset(ident[:], 0.0).then_inc(const_cleared, 1)
            pool.memset(sel[:], 0.0).then_inc(const_cleared, 1)
            pool.memset(ones[:], 1.0).then_inc(const_ready, 1)
            pool.memset(eps[:], EPS).then_inc(const_ready, 1)
            pool.wait_ge(const_cleared, 2)
            pool.affine_select(out=ident[:], in_=ident[:], compare_op=ALU.not_equal, fill=1.0, base=0,
                               pattern=[[-1, P]], channel_multiplier=1).then_inc(const_ready, 1)
            pool.affine_select(out=sel[:], in_=sel[:], compare_op=ALU.not_equal, fill=1.0, base=0,
                               pattern=[[-32, 2], [-1, H], [0, P]], channel_multiplier=1).then_inc(const_ready, 1)

            def split_low(k, p, s):
                pool.wait_ge(hi_ready, p * 2 + (s + 1))
                pool.tensor_tensor(w_lo[s][:, 0:k * P], raw[s][:, 0:k * P], w_hi[s][:, 0:k * P].bitcast(F32),
                                   ALU.subtract).then_inc(lo_ready, 1)

            def add_square(r, j, s, w, first):
                pool.wait_ge(sq_ready, j + (KD * r + 1))
                if first:
                    if r:
                        pool.wait_ge(ss_summed, chain_of_norm(r))
                    pool.tensor_copy(ssum[:, 0:w], tmp[:, 2 + s, 0:w]).then_inc(ss_added, 1)
                else:
                    pool.wait_ge(ss_added, j + (KD - 1) * r)
                    pool.tensor_tensor(ssum[:, 0:w], ssum[:, 0:w], tmp[:, 2 + s, 0:w], ALU.add).then_inc(ss_added, 1)

            def norm_low(r):
                w, n = width_of_norm(r), KD * norm_place[r]
                with pool.Fori(0, KD // 4) as i:
                    for s in (1, 3):
                        pool.wait_ge(h_hi_ready, i * 4 + (n + s + 1))
                        j = i * 4 + s
                        pool.tensor_tensor(chunk(h_lo, j, w), tmp[:, s, 0:w], chunk(h_hi, j, w).bitcast(F32),
                                           ALU.subtract).then_inc(h_lo_ready, 1)

            def gate_weights(l):
                pool.wait_ge(gw_loaded, 16 * (l + 1))
                pool.memset(gw[:], 0.0).then_inc(gw_cleared, 1)
                pool.wait_ge(gw_cleared, l + 1)
                for j, row in enumerate(GATE_ROWS):
                    pool.tensor_copy(gw[:, :, row:row + H], gw16[:, :, j * H:(j + 1) * H]).then_inc(gw_ready, 1)
                pool.wait_ge(gw_hi_ready, l + 1)
                pool.tensor_tensor(gw_lo[:], gw[:], gw_hi[:].bitcast(F32), ALU.subtract).then_inc(gw_lo_ready, 1)

            def scan_steps(l):
                pool.wait_ge(vk_turned, 2 * TT * l + 1)
                pool.memset(vt[:, :, :, P:E1], 1.0).then_inc(ones_ready, 1)
                for st in steps:
                    n, d, ch, t = st
                    if keeps(st):
                        if n == 0:
                            pool.wait_ge(vk_read, 2 * TT * l + TT)
                            pool.wait_ge(ones_ready, l + 1)
                            pool.wait_ge(cols_ready, l + 1)
                        if n >= 2:
                            pool.wait_ge(dc_ready, count(kept, l, n - 1))
                        pool.tensor_tensor(vw[n % 2][:], vt[:, t, :, :],
                                           col[:, R_WK, ch, d, :].rearrange("p (h o) -> p h o", o=1).to_broadcast([P, H, E1]),
                                           ALU.mult).then_inc(vw_ready, 1)
                    if gives(l, st):
                        pool.wait_ge(e_ready, outs_before(l, n) + 1)
                        sign = 1 if d == 0 else -1
                        pool.affine_select(out=ew[n % 2][:], in_=ew[n % 2][:], compare_op=ALU.is_ge, fill=0.0, base=0,
                                           pattern=[[0, H], [sign, P]], channel_multiplier=-sign).then_inc(mask_ready, 1)

            def conv_squares(l, w):
                for k in range(KC):
                    pool.wait_ge(yc_sq, KC * l + k + 1)
                    if k == 0:
                        pool.wait_ge(ss_summed, chain_of_conv(l, 0) + 1)
                        pool.tensor_copy(ssum[:, 0:w], tmp[:, 2, 0:w]).then_inc(yc_summed, 1)
                    else:
                        pool.wait_ge(yc_summed, KC * l + k)
                        pool.tensor_tensor(ssum[:, 0:w], ssum[:, 0:w], tmp[:, 2 + k % 2, 0:w], ALU.add).then_inc(yc_summed, 1)

            def mixer_low(l, w):
                n = KD * split_of(l, "y")
                for k in range(KD):
                    pool.wait_ge(h_hi_ready, n + k + 1)
                    src = tmp[:, 2 + k % 2, 0:w] if k < H else yc[:, k - H, 0:w]
                    pool.tensor_tensor(h_lo[:, k, 0:w], src, h_hi[:, k, 0:w].bitcast(F32), ALU.subtract).then_inc(h_lo_ready, 1)

            def load_mod(l, unit, s):
                pool.dma_start(mraw[s][:], w_mod[l].rearrange("(k p) n -> p k n", p=P)[:, :, bass.ds(unit * P, P)]).then_inc(mod_loaded[s], 16)

            split_low(KD, 0, 0)
            split_low(KD, 0, 1)
            for j in range(KD - 1):
                add_square(0, j, j % 2, T, j == 0)
            for q in phases:
                l, w, name = q["l"], q["w"], q["name"]
                if q.get("mods_first"):
                    if q["p0"]:
                        pool.wait_ge(h_lo_ready, lows_before(split_of(l, "ffn2")))
                    for m in range(2):
                        load_mod(q["mods"][0], q["mods"][2] + m, m)
                if name == "up" and q["half"] == 0:
                    norm_low(3 * l + (0 if q["up"] is ffn1_up else 2))
                if name == "glu":
                    gate_weights(l)
                    norm_low(3 * l + 1)
                if name == "out":
                    conv_squares(l, w)
                    scan_steps(l)
                    mixer_low(l, w)

                def pair(i, p, k_next, riders, q=q, w=w):
                    last_riders = q.get("mods") and q["mods"][4] and isinstance(i, int) and i > 0

                    def reload(some):
                        for ml, unit, v, s in some:
                            pool.wait_ge(mod_step, v * (2 * KD) + 2 * KD)
                            load_mod(ml, unit + 2, s)

                    if last_riders:
                        riders = riders[:-2]
                    if k_next:
                        split_low(k_next, p + 1, 0)
                    reload(riders[:2])
                    if q.get("norm"):
                        add_square(q["norm"], i * 2, 0, w, isinstance(i, int) and i == 0)
                    if k_next:
                        split_low(k_next, p + 1, 1)
                    reload(riders[2:])
                    if q.get("norm") and not (isinstance(i, int) and i > 0):
                        add_square(q["norm"], i * 2 + 1, 1, w, False)

                run_pairs(pool, q, pair)

        @block.scalar
        def _(act):
            def split_high(k, p, s):
                act.wait_ge(raw_loaded[s], p * 16 + 16)
                if not isinstance(p, int) or p > 0:
                    act.wait_ge(unit_done, p * 2 + (s - 1))
                act.activation(w_hi[s][:, 0:k * P], raw[s][:, 0:k * P], ACT.Copy).then_inc(hi_ready, 1)

            def square(r, j, s, w):
                if not (isinstance(j, int) and j < 2):
                    act.wait_ge(ss_added, j + ((KD - 1) * r - 1))
                act.activation(tmp[:, 2 + s, 0:w], chunk(xres, j, w), ACT.Square).then_inc(sq_ready, 1)

            def root(chain, w, scale):
                n = roots_before(chain)
                if n:
                    act.wait_ge(root_begun, n)
                act.activation(begun[:], eps[:], ACT.Sqrt).then_inc(root_begun, 1)
                act.wait_ge(ss_summed, chain + 1)
                act.activation(stat[:, 0, 0:w // P], ps[:, 4, 0:w // P], ACT.Sqrt, scale=scale,
                               bias=eps[:]).then_inc(root_ready, 1)

            def norm_high(r):
                w = width_of_norm(r)
                l, which = divmod(r, 3)
                for j in range(KD):
                    act.wait_ge(hf_ready, KD * r + j + 1)
                    s = j % 4
                    for o, (b, e) in enumerate(groups(w)):
                        last = act.activation(h_hi[:, j, b:e], tmp[:, s, b:e], ACT.Identity, bias=shift[:, l, which, o, j:j + 1])
                    if s % 2:
                        last.then_inc(h_rounded, 1)
                        act.wait_ge(h_rounded, KD // 2 * r + j // 2 + 1)
                        for o, (b, e) in enumerate(groups(w)):
                            last = act.activation(tmp[:, s, b:e], tmp[:, s, b:e], ACT.Identity, bias=shift[:, l, which, o, j:j + 1])
                    last.then_inc(h_hi_ready, 1)

            def gate_rows(l):
                act.wait_ge(rows_dve, 3 * l + 1)
                act.activation(rt[:, 6, :], rt[:, 5, :], ACT.Exp, scale=-1.0).then_inc(rows_act, 1)
                act.wait_ge(rows_act, 3 * l + 1)
                act.activation(rt[:, 5, :], rt[:, 6, :], ACT.Ln, bias=ones[0:ROWS, 0:1]).then_inc(rows_act, 1)
                act.wait_ge(rows_dve, 3 * l + 2)
                for r, src, scale in ((R_WK, rt[:, 1, :], 1.0), (R_INTER, rt[:, 5, :], 1.0), (R_EM, rt[:, 4, :], -1.0),
                                      (R_DEC, None, 1.0)):
                    if src is None:
                        src = rsm[:, 2, :].rearrange("r (c o) -> r c o", o=1).to_broadcast([ROWS, NCH, P])
                    else:
                        src = src.rearrange("r (c n) -> r c n", n=P)
                    act.activation(rq[0:32, r, :, :], src[0:32], ACT.Exp, scale=scale)
                    last = act.activation(rq[32:ROWS, r, :, ::-1], src[32:ROWS], ACT.Exp, scale=scale)
                last.then_inc(rows_act, 1)

            def turned_values(l):
                for i in range(2 * TT):
                    act.wait_ge(vk_turned, 2 * TT * l + i + 1)
                    bank = ps[:, 4 + i % 4, :]
                    if i < TT:
                        act.activation(vt[:, i, :, 0:P], bank.rearrange("p (h e) -> p h e", h=H), ACT.Copy).then_inc(vk_read, 1)
                    else:
                        act.activation(kt[:, i - TT, :], bank, ACT.Copy).then_inc(vk_read, 1)

            def conv_norm(l, w):
                for k in range(KC):
                    act.wait_ge(yc_dev, KC * l + k + 1)
                    if k >= 2:
                        act.wait_ge(yc_summed, KC * l + k - 1)
                    act.activation(tmp[:, 2 + k % 2, 0:w], yc[:, k, 0:w], ACT.Square).then_inc(yc_sq, 1)
                root(chain_of_conv(l, 1), w, 1.0 / (KC * P))
                for k in range(KC):
                    act.wait_ge(yc_norm, KC * l + k + 1)
                    act.activation(yc[:, k, 0:w], yc[:, k, 0:w], ACT.Silu, scale=tab_a[:, l, A_CG + k:A_CG + k + 1],
                                   bias=tab_a[:, l, A_CN + k:A_CN + k + 1]).then_inc(yc_act, 1)

            def scan_steps(l):
                def weights(st):
                    n, d, ch, t = st
                    o = outs_before(l, n)
                    act.wait_ge(b_ready, o + 1)
                    if o >= 2:
                        act.wait_ge(sw_ready, o - 1)
                    for h in range(H):
                        last = act.activation(ew[n % 2][:, h, :], ps[:, 1, h * P:(h + 1) * P], ACT.Exp,
                                              bias=col[:, R_CS, ch, d, h:h + 1])
                    last.then_inc(e_ready, 1)

                act.wait_ge(cols_ready, l + 1)
                if gives(l, steps[0]):
                    weights(steps[0])
                for st in steps:
                    n, d, ch, t = st
                    if n + 1 < len(steps) and gives(l, steps[n + 1]):
                        weights(steps[n + 1])
                    if inters(l, st):
                        act.wait_ge(i_ready, count(inters, l, n) + 1)
                        if outs_before(l, n) >= 2:
                            act.wait_ge(tot_ready, outs_before(l, n) - 1)
                        for h in range(H):
                            last = act.activation(isb[n % 2][:, h, :], head_ps(4, h), ACT.Copy,
                                                  scale=col[:, R_INTER, ch, d, h:h + 1])
                        last.then_inc(isb_ready, 1)

            def mixer_high(l, w):
                act.wait_ge(hm_squared, l + 1)
                m = w // P * H
                act.activation(stat[:, 0, 0:m], stat[:, 1, 0:m], ACT.Sqrt, scale=1.0 / P, bias=eps[:]).then_inc(hm_root, 1)
                for k in range(KD):
                    if k < H:
                        act.wait_ge(ym_ready, H * l + k + 1)
                        src = tmp[:, 2 + k % 2, 0:w]
                    else:
                        act.wait_ge(hm_turned, H * (l + 1))
                        act.wait_ge(yc_act, KC * (l + 1))
                        src = yc[:, k - H, 0:w]
                    act.activation(h_hi[:, k, 0:w], src, ACT.Copy).then_inc(h_hi_ready, 1)

            act.wait_ge(const_ready, 4)
            act.wait_ge(tab_read, 1)
            act.activation(silu_c[:], tab_c[:, C_C:C_C + 2 * KD].rearrange("p (o k) -> p k o", o=2), ACT.Silu).then_inc(silu_ready, 1)
            split_high(KD, 0, 0)
            split_high(KD, 0, 1)
            for j in range(KD):
                act.wait_ge(x_copied, j + 1)
                square(0, j, j % 2, T)

            for q in phases:
                l, w, name = q["l"], q["w"], q["name"]
                if name == "up" and q["half"] == 0:
                    r = 3 * l + (0 if q["up"] is ffn1_up else 2)
                    root(chain_of_norm(r), w, 1.0 / D)
                    norm_high(r)
                if name == "glu":
                    act.wait_ge(gw_ready, 4 * (l + 1))
                    act.activation(gw_hi[:], gw[:], ACT.Copy).then_inc(gw_hi_ready, 1)
                    root(chain_of_norm(3 * l + 1), T, 1.0 / D)
                    norm_high(3 * l + 1)
                    gate_rows(l)
                if name == "out":
                    turned_values(l)
                    conv_norm(l, w)
                    scan_steps(l)
                    mixer_high(l, w)

                def evacuate(i, s, q=q, l=l, w=w, name=name):
                    if name == "q":
                        func, scale, bias, to = ACT.Identity, float(P) ** -0.5, column(bq[:, l, :], i * 2 + s), i * 2 + s
                    elif name == "kv":
                        func, scale, bias, to = ACT.Identity, 1.0, column(tab_a[:, l, :], i * 2 + (A_BIN + H + s)), i * 2 + (H + s)
                    else:
                        func, scale, bias, to = ACT.Sigmoid, 1.0, column(tab_a[:, l, :], i * 2 + (A_BIN + 3 * H + s)), i * 2 + (3 * H + s)
                    act.activation(chunk(qkvo, to, w), slot_ps(s, w), func, scale=scale, bias=bias).then_inc(slot_read[s], 1)

                def pair(i, p, k_next, riders, q=q, l=l, w=w, name=name, evacuate=evacuate):
                    act.wait_ge(unit_done, p * 2 + 1)
                    if name == "up":
                        act.activation(tmp[:, 0, 0:w], slot_ps(0, w), ACT.Silu).then_inc(slot_read[0], 1)
                    if name in ("q", "kv", "o"):
                        evacuate(i, 0)
                    if k_next:
                        split_high(k_next, p + 1, 0)
                    if q.get("norm"):
                        act.wait_ge(slot_read[0], p + 1)
                        square(q["norm"], i * 2, 0, w)
                    act.wait_ge(unit_done, p * 2 + 2)
                    if name == "glu":
                        if not isinstance(i, int) or i > 0:
                            act.wait_ge(slot_read[0], p)
                        act.activation(tmp[:, 0, 0:w], slot_ps(1, w), ACT.Sigmoid,
                                       bias=column(tab_c, i + (l * 2 * KC + KC))).then_inc(slot_read[1], 1)
                    if name in ("q", "kv", "o"):
                        evacuate(i, 1)
                    last_squares = q.get("norm") and isinstance(i, int) and i > 0
                    if last_squares:
                        act.wait_ge(slot_read[1], p + 1)
                        square(q["norm"], i * 2 + 1, 1, w)
                    if k_next:
                        split_high(k_next, p + 1, 1)
                    if name == "up":
                        act.wait_ge(slot_read[1], p + 1)
                        act.activation(chunk(a_hi, i, w), tmp[:, 1, 0:w], ACT.Copy).then_inc(a_hi_ready, 1)
                    if q.get("norm") and not last_squares:
                        act.wait_ge(slot_read[1], p + 1)
                        square(q["norm"], i * 2 + 1, 1, w)

                run_pairs(act, q, pair)

            root(chain_of_norm(3 * DEPTH), NX, 1.0 / D)
            for k in range(KD):
                act.wait_ge(o_turned, k + 1)
                act.activation(otok[:, :, k * P:(k + 1) * P], ps[:, 2 * (k % 2), :].rearrange("p (t f) -> p t f", t=TX),
                               ACT.Copy).then_inc(out_read, 1)

        @block.vector
        def _(dve):
            self_count = [0]

            def settle(ins):
                self_count[0] += 1
                ins.then_inc(dve_self, 1)
                dve.wait_ge(dve_self, self_count[0])

            def reciprocals(chain, w):
                dve.wait_ge(root_ready, roots_before(chain) + 1)
                dve.reciprocal(stat[:, 1, 0:w // P], stat[:, 0, 0:w // P]).then_inc(factor_ready, 1)

            def norm(r):
                w = width_of_norm(r)
                l, which = divmod(r, 3)
                reciprocals(chain_of_norm(r), w)
                q = [q for q in phases if q["name"] in ("up", "glu") and q["l"] == l and q.get("half", 0) == 0][which]
                if q["ups"]:
                    dve.wait_ge(a_lo_ready, KF * q["ups"])
                n = lows_before(norm_place[r])

                def scaled(i, s, first):
                    j = i * 4 + s
                    if not first:
                        if s % 2:
                            dve.wait_ge(h_lo_ready, i * 2 + (n + s // 2 - 1))
                        else:
                            dve.wait_ge(h_even_ready, i * 2 + (KD // 2 * r + s // 2 - 1))
                    for o, (b, e) in enumerate(groups(w)):
                        if first and s == 0:
                            dve.wait_ge(wide_ready, wides_before(chain_of_norm(r)) + o + 1)
                        last = dve.scalar_tensor_tensor(tmp[:, s, b:e], xres[:, bass.ds(j, 1), b:e].rearrange("p k n -> p (k n)"),
                                                        column(coef[:, l, which, o, :], j), wide[:, b:e], ALU.mult, ALU.mult)
                    last.then_inc(hf_ready, 1)

                def low(i, s):
                    j = i * 4 + s
                    dve.wait_ge(h_hi_ready, i * 4 + (KD * norm_place[r] + s + 1))
                    for o, (b, e) in enumerate(groups(w)):
                        last = dve.scalar_tensor_tensor(h_lo[:, bass.ds(j, 1), b:e].rearrange("p k n -> p (k n)"), tmp[:, s, b:e],
                                                        column(shift[:, l, which, o, :], j),
                                                        h_hi[:, bass.ds(j, 1), b:e].rearrange("p k n -> p (k n)").bitcast(F32),
                                                        ALU.add, ALU.subtract)
                    last.then_inc(h_even_ready, 1)

                def chunks(i, first):
                    scaled(i, 0, first)
                    scaled(i, 1, first)
                    low(i, 0)
                    scaled(i, 2, first)
                    scaled(i, 3, first)
                    low(i, 2)

                chunks(0, True)
                with dve.Fori(1, KD // 4) as i:
                    chunks(i, False)

            def gate_rows(l):
                settle(dve.memset(rt[:, 0:2, :], 0.0))
                for k, first in ((0, 0), (1, 64)):
                    for d in range(2):
                        src = slice(first + 32 * d, first + 32 * d + H)
                        to = slice(32 * d, 32 * d + H)
                        if k == 0 and d == 0:
                            dve.wait_ge(gates_ready, l + 1)
                        for bank, b, e in ((4, 0, NC), (7, NC, T)):
                            got = ps[src, bank, 0:e - b]
                            settle(dve.tensor_scalar(rt[to, k, b:e], got if d == 0 else got[:, ::-1], gbias[src, l:l + 1],
                                                     None, ALU.add))
                dve.scalar_tensor_tensor(rt[:, 5, :], rt[:, 1, :], -1.0, rt[:, 1, :], ALU.mult, ALU.max).then_inc(rows_dve, 1)
                dve.wait_ge(rows_act, 3 * l + 2)
                settle(dve.memset(rt[:, 6, :], 1.0))
                settle(dve.memset(rt[:, 6, :].rearrange("r (c n) -> r c n", n=P)[:, :, 0:1], 0.0))
                settle(dve.scalar_tensor_tensor(rt[:, 2, :], rt[:, 1, :], 0.0, rt[:, 5, :], ALU.min, ALU.subtract))
                settle(dve.tensor_tensor_scan(rt[:, 3, :], rt[:, 6, :], rt[:, 2, :], 0.0, ALU.mult, ALU.add))
                settle(dve.tensor_tensor_scan(rt[:, 4, :], rt[:, 2, :], rt[:, 0, :], 0.0, ALU.add, ALU.max))
                settle(dve.tensor_tensor(rt[:, 8, :], rt[:, 3, :], rt[:, 4, :], ALU.subtract))
                settle(dve.tensor_tensor(rt[:, 7, :], rt[:, 0, :], rt[:, 3, :], ALU.subtract))

                def by_chunk(k):
                    return rt[:, k, :].rearrange("r (c n) -> r c n", n=P)

                def spread(k):
                    return rsm[:, k, :].rearrange("r (c o) -> r c o", o=1).to_broadcast([ROWS, NCH, P])

                settle(dve.memset(rsm[:, 0, 0:1], 0.0))
                settle(dve.tensor_copy(rsm[:, 0, 1:NCH], by_chunk(4)[:, 0:NCH - 1, P - 1]))
                settle(dve.tensor_copy(rsm[:, 1, :], by_chunk(8)[:, :, P - 1]))
                settle(dve.tensor_tensor(rsm[:, 2, :], rsm[:, 1, :], rsm[:, 0, :], ALU.add))
                settle(dve.tensor_tensor(by_chunk(5), by_chunk(8), spread(0), ALU.add))
                dve.tensor_tensor(by_chunk(1), by_chunk(7), spread(1), ALU.add).then_inc(rows_dve, 1)
                for k, to in ((8, r1_row[:]), (7, rq[:, R_CS, :, :])):
                    dve.tensor_copy(to[0:32], by_chunk(k)[0:32])
                    last = dve.tensor_copy(to[32:ROWS, :, ::-1], by_chunk(k)[32:ROWS])
                last.then_inc(rows_dve, 1)

            def gate_columns(l):
                dve.wait_ge(cols_turned, l + 1)
                for r in range(5):
                    got = ps[:, 5 + r // 2, r % 2 * NCH * ROWS:(r % 2 + 1) * NCH * ROWS].rearrange("p (c g) -> p c g", g=ROWS)
                    for d in range(2):
                        last = dve.tensor_copy(col[:, r, :, d, :], got[:, :, 32 * d:32 * d + H])
                last.then_inc(cols_ready, 1)

            conv_count = [0]

            def convolve(l, w):
                def tap(k, j, to, src, first=False, base=None, at_loop=None):
                    weight = column(tab_b[:, l, :], k + j * KC)
                    if first:
                        return dve.tensor_scalar(to, src, weight, column(tab_a[:, l, :], k + A_CB), ALU.mult, ALU.add)
                    return dve.scalar_tensor_tensor(to, src, weight, to, ALU.mult, ALU.add)

                mid = TAPS // 2
                order = [mid] + [j for j in range(TAPS) if j != mid]
                rows = NX // GRID_W
                zx = lambda t, k: t[:, k, 0:NX].rearrange("p (r c) -> p r c", c=GRID_W)
                for k0, along in ((0, "columns"), (KC // 2, "rows")):
                    for m, j in enumerate(j for j in order if along == "columns" or abs(j - mid) < rows):
                        o = j - mid
                        for k in (k0, k0 + 1):
                            if m:
                                dve.wait_ge(conv_step, conv_count[0] - 1)
                            n = GRID_W if along == "columns" else rows
                            b, e = max(0, -o), min(n, n - o)
                            if along == "columns":
                                to, src = zx(yc, k)[:, :, b:e], zx(z, k)[:, :, b + o:e + o]
                            else:
                                to, src = zx(yc, k)[:, b:e, :], zx(z, k)[:, b + o:e + o, :]
                            tap(k, j, to, src, m == 0).then_inc(conv_step, 1)
                            conv_count[0] += 1
                if w > NX:
                    base = conv_count[0]
                    with dve.Fori(0, KC // 2) as i:
                        for m, j in enumerate(order):
                            o = j - mid
                            b, e = max(0, -o), min(NC, NC - o)
                            for s in range(2):
                                if m:
                                    dve.wait_ge(conv_step, i * (2 * TAPS) + (base + 2 * m + s - 1))
                                k = i * 2 + s
                                part = lambda t, b, e: t[:, bass.ds(k, 1), NX + b:NX + e].rearrange("p k n -> p (k n)")
                                tap(k, j, part(yc, b, e), part(z, b + o, e + o), m == 0).then_inc(conv_step, 1)
                    conv_count[0] += KC * TAPS
                dve.wait_ge(conv_step, conv_count[0])

            def conv_norm(l, w):
                settle(dve.tensor_tensor(ssum[:, 0:w], yc[:, 0, 0:w], yc[:, 1, 0:w], ALU.add))
                settle(dve.tensor_tensor(ssum[:, 0:w], ssum[:, 0:w], yc[:, 2, 0:w], ALU.add))
                dve.tensor_tensor(ssum[:, 0:w], ssum[:, 0:w], yc[:, 3, 0:w], ALU.add).then_inc(yc_totalled, 1)
                chain = chain_of_conv(l, 0)
                dve.wait_ge(ss_summed, chain + 1)
                dve.tensor_scalar(stat[:, 1, 0:w // P], ps[:, 4, 0:w // P], 1.0 / (KC * P), None, ALU.mult).then_inc(factor_ready, 1)
                dve.wait_ge(wide_ready, wides_before(chain) + len(groups(w)))
                for k in range(KC):
                    dve.tensor_tensor(yc[:, k, 0:w], yc[:, k, 0:w], wide[:, 0:w], ALU.subtract).then_inc(yc_dev, 1)
                reciprocals(chain_of_conv(l, 1), w)
                dve.wait_ge(wide_ready, wides_before(chain_of_conv(l, 1)) + len(groups(w)))
                for k in range(KC):
                    dve.tensor_tensor(yc[:, k, 0:w], yc[:, k, 0:w], wide[:, 0:w], ALU.mult).then_inc(yc_norm, 1)

            def scan_steps(l):
                touched = set()

                def weighted(st):
                    n, d, ch, t = st
                    o = outs_before(l, n)
                    dve.wait_ge(mask_ready, o + 1)
                    dve.wait_ge(s_ready, o + 1)
                    if o >= 2:
                        dve.wait_ge(n_ready, o - 1)
                    dve.tensor_tensor(sw[n % 2][:].rearrange("p h t -> p (h t)"),
                                      ew[n % 2][:].rearrange("p h t -> p (h t)"), ps[:, 0, :], ALU.mult).then_inc(sw_ready, 1)

                if gives(l, steps[0]):
                    weighted(steps[0])
                for st in steps:
                    n, d, ch, t = st
                    o, kp = outs_before(l, n), count(kept, l, n)
                    if keeps(st):
                        dve.wait_ge(dc_ready, kp + 1)
                        if inters(l, st):
                            dve.wait_ge(i_ready, count(inters, l, n) + 1)
                        if ch == 0:
                            dve.tensor_copy(flat2(state[d][:]), pair_banks(6)).then_inc(state_ready, 1)
                        else:
                            dve.wait_ge(state_ready, kp - 1)
                            for h in range(H):
                                last = dve.scalar_tensor_tensor(state[d][:, h, :], state[d][:, h, :], col[:, R_DEC, ch, d, h:h + 1],
                                                                head_ps(6, h), ALU.mult, ALU.add)
                            last.then_inc(state_ready, 1)
                    if n + 1 < len(steps) and gives(l, steps[n + 1]):
                        weighted(steps[n + 1])
                    if gives(l, st):
                        dve.wait_ge(n_ready, o + 1)
                        if inters(l, st):
                            dve.wait_ge(isb_ready, count(inters, l, n) + 1)
                            total = dve.tensor_tensor(flat2(tot), pair_banks(2), flat2(isb[n % 2][:]), ALU.add)
                        else:
                            total = dve.tensor_copy(flat2(tot), pair_banks(2))
                        total.then_inc(tot_ready, 1)
                        dve.wait_ge(tot_ready, o + 1)
                        den = tot[:, :, P:E1].rearrange("p h o -> p (h o)")
                        settle(dve.scalar_tensor_tensor(stat[:, 2, 0:H], den, -1.0, den, ALU.mult, ALU.max))
                        settle(dve.tensor_tensor(stat[:, 2, 0:H], stat[:, 2, 0:H], col[:, R_EM, ch, d, :], ALU.max))
                        settle(dve.reciprocal(stat[:, 2, H:2 * H], stat[:, 2, 0:H]))
                        for h in range(H):
                            to = hm[:, t, h * P:(h + 1) * P]
                            by = stat[:, 2, H + h:H + h + 1]
                            if t in touched:
                                last = dve.scalar_tensor_tensor(to, tot[:, h, 0:P], by, to, ALU.mult, ALU.add)
                            else:
                                last = dve.tensor_scalar(to, tot[:, h, 0:P], by, None, ALU.mult)
                        settle(last)
                        touched.add(t)

            def mixer_out(l, w):
                nt = w // P
                heads = hm[:, 0:nt, :].rearrange("p t (h e) -> p (t h) e", e=P)
                squares = tmp[:].rearrange("p a n -> p (a n)")[:, 0:nt * DM].rearrange("p (g e) -> p g e", e=P)
                settle(dve.tensor_tensor(squares, heads, heads, ALU.mult))
                dve.tensor_reduce(stat[:, 1, 0:nt * H], squares, AX.X, ALU.add).then_inc(hm_squared, 1)
                dve.wait_ge(hm_root, l + 1)
                settle(dve.reciprocal(stat[:, 2, 0:nt * H], stat[:, 0, 0:nt * H]))
                dve.tensor_tensor(heads, heads, stat[:, 2, 0:nt * H].rearrange("p (g o) -> p g o", o=1).to_broadcast([P, nt * H, P]),
                                  ALU.mult).then_inc(hm_scaled, 1)
                for h in range(H):
                    dve.wait_ge(hm_turned, H * l + h + 1)
                    if h >= 2:
                        dve.wait_ge(h_lo_ready, lows_before(split_of(l, "y")) + h - 1)
                    dve.scalar_tensor_tensor(tmp[:, 2 + h % 2, 0:w], slot_ps(2 + h % 2, w), tab_a[:, l, A_MG + h:A_MG + h + 1],
                                             qkvo[:, 3 * H + h, 0:w], ALU.mult, ALU.mult).then_inc(ym_ready, 1)

            dve.wait_ge(tab_turned, 1)
            dve.tensor_copy(tab_a[:], ps[:, 4, 0:DEPTH * P].rearrange("p (l n) -> p l n", l=DEPTH))
            for l in range(DEPTH):
                dve.tensor_copy(tab_b[:, l, :], ps[:, 4, (DEPTH + l) * P:(DEPTH + l) * P + TAPS * KC])
            settle(dve.tensor_copy(tab_c[:], ps[:, 5, 0:NCR]))
            dve.tensor_scalar(bq[:], tab_a[:, :, A_BIN:A_BIN + H], float(P) ** -0.5, None, ALU.mult).then_inc(tab_read, 1)
            for k in range(KD):
                dve.wait_ge(x_turned, k + 1)
                dve.tensor_copy(xres[:, k, :], slot_ps(k % 2, T)).then_inc(x_copied, 1)
            def modulation(l, vectors):
                first, end = min(vectors) * KD, (max(vectors) + 1) * KD
                mod = tmp[:, 1, 0:2 * NM].rearrange("p (m o) -> p m o", o=2)
                settle(dve.tensor_tensor(mod[:, first:end, :], ps[:, 7, 2 * first:2 * end].rearrange("p (m o) -> p m o", o=2),
                                         tab_a[:, l, first:end].rearrange("p (m o) -> p m o", o=1).to_broadcast([P, end - first, 2]),
                                         ALU.add))
                for j in vectors:
                    which, kind = divmod(j, 3)
                    gain = (A_N1, A_NM, A_N2)[which]
                    for o in range(2):
                        part = mod[:, j * KD:(j + 1) * KD, o]
                        if kind == 0:
                            last = dve.tensor_copy(shift[:, l, which, o, :], part)
                        elif kind == 1:
                            last = dve.scalar_tensor_tensor(coef[:, l, which, o, :], part, 1.0, tab_a[:, l, gain:gain + KD],
                                                            ALU.add, ALU.mult)
                        else:
                            last = dve.tensor_scalar(gate[:, l, which, o, :], part, 1.0 if which == 1 else 0.5, None, ALU.mult)
                last.then_inc(mod_read, 1)
                mod_reads[0] += 1
                dve.wait_ge(mod_read, mod_reads[0])

            mod_reads = [0]

            def mod_units(riders):
                for ml, unit, v, s in riders:
                    dve.wait_ge(mod_loaded[s], (v - s) * 8 + 16)
                    if not isinstance(v, int) or v >= 2:
                        dve.wait_ge(mod_summed, v - 1)
                    for k in range(KD):
                        for o in range(2):
                            to, by = macc[s][:, o, :], silu_c[:, k, o:o + 1]
                            if k == 0:
                                step = dve.tensor_scalar(to, mraw[s][:, k, :], by, None, ALU.mult)
                            else:
                                dve.wait_ge(mod_step, v * (2 * KD) + (2 * k + o - 1))
                                step = dve.scalar_tensor_tensor(to, mraw[s][:, k, :], by, to, ALU.mult, ALU.add)
                            step.then_inc(mod_step, 1)

            dve.wait_ge(first_summed, 1)
            modulation(0, (0, 1))

            for q in phases:
                l, w, name = q["l"], q["w"], q["name"]
                if name == "up" and q["half"] == 0:
                    norm(3 * l + (0 if q["up"] is ffn1_up else 2))
                if name == "glu":
                    norm(3 * l + 1)
                    gate_rows(l)
                if name == "q":
                    gate_columns(l)
                    convolve(l, w)
                if name == "out":
                    conv_norm(l, w)
                    scan_steps(l)
                    mixer_out(l, w)

                def pair(i, p, k_next, riders, q=q, l=l, w=w, name=name):
                    mod_units(riders[:2])
                    if name == "up":
                        dve.wait_ge(slot_read[0], p + 1)
                        dve.wait_ge(unit_done, p * 2 + 2)
                        if q["ups"] or not isinstance(i, int) or i > 0:
                            dve.wait_ge(a_lo_ready, i + KF * q["ups"])
                        dve.tensor_tensor(tmp[:, 1, 0:w], tmp[:, 0, 0:w], slot_ps(1, w), ALU.mult).then_inc(slot_read[1], 1)
                        dve.wait_ge(a_hi_ready, i + (KF * q["ups"] + 1))
                        dve.tensor_tensor(chunk(a_lo, i, w), tmp[:, 1, 0:w], chunk(a_hi, i, w).bitcast(F32),
                                          ALU.subtract).then_inc(a_lo_ready, 1)
                    if name == "glu":
                        dve.wait_ge(slot_read[1], p + 1)
                        dve.scalar_tensor_tensor(chunk(z, i, w), slot_ps(0, w), column(tab_c, i + l * 2 * KC), tmp[:, 0, 0:w],
                                                 ALU.add, ALU.mult).then_inc(slot_read[0], 1)
                    if name in ("down", "out"):
                        for s in range(2):
                            if s == 1:
                                mod_units(riders[2:])
                            dve.wait_ge(unit_done, p * 2 + (s + 1))
                            j = i * 2 + s
                            for o, (b, e) in enumerate(groups(w)):
                                to = xres[:, j, b:e] if isinstance(j, int) else xres[:, bass.ds(j, 1), b:e].rearrange("p k n -> p (k n)")
                                last = dve.scalar_tensor_tensor(to, slot_ps(s, w)[:, b:e], column(gate[:, l, q["gate"], o, :], j),
                                                                to, ALU.mult, ALU.add)
                            last.then_inc(slot_read[s], 1)

                if name not in ("q", "kv", "o"):
                    run_pairs(dve, q, pair)
                if q.get("mods"):
                    ml, _, _, _, ends = q["mods"]
                    dve.wait_ge(mod_summed, ridden_after(q))
                    if ends or q is phases[0]:
                        dve.wait_ge(a_lo_ready, KF * (q["ups"] + (name == "up")))
                    if q is phases[0]:
                        modulation(0, (2,))
                    elif ends:
                        modulation(ml, tuple(range(3, 9)) if ml == 0 else tuple(range(9)))

            r = 3 * DEPTH
            reciprocals(chain_of_norm(r), NX)
            dve.wait_ge(a_lo_ready, KF * (phases[-1]["ups"]))
            dve.wait_ge(wide_ready, wides_before(chain_of_norm(r)) + 1)
            for k in range(KD):
                if k >= 4:
                    dve.wait_ge(o_turned, k - 3)
                dve.scalar_tensor_tensor(tmp[:, k % 4, 0:NX], xres[:, k, 0:NX], tab_c[:, C_FIN + k:C_FIN + k + 1],
                                         wide[:, 0:NX], ALU.mult, ALU.mult).then_inc(hf_ready, 1)

        @block.tensor
        def _(pe):
            def sums(chain, w, parts=(ssum[:],)):
                for t in range(w // P):
                    for n, part in enumerate(parts):
                        last = pe.matmul(ps[:, 4, t:t + 1], part[:, t * P:(t + 1) * P], ones[:, 0:1],
                                         start=(n == 0), stop=(n == len(parts) - 1))
                last.then_inc(ss_summed, 1)
                pe.wait_ge(factor_ready, chain + 1)
                for b, e in groups(w):
                    for t in range(b // P, e // P):
                        last = pe.matmul(wide[:, t * P:(t + 1) * P], stat[:, 1, t:t + 1].to_broadcast([P, P]), ident[:],
                                         start=True, stop=True)
                    last.then_inc(wide_ready, 1)

            def norm_sums(r, w):
                pe.wait_ge(ss_added, (KD - 1) * (r + 1))
                pe.wait_ge(sq_ready, KD * (r + 1))
                sums(chain_of_norm(r), w, (ssum[:], tmp[:, 3, :]))

            def chunk_split(r, k):
                if k % 2:
                    pe.wait_ge(h_lo_ready, lows_before(norm_place[r]) + (k + 1) // 2)
                else:
                    pe.wait_ge(h_even_ready, KD // 2 * r + k // 2 + 1)

            def unit(q, s, moving_hi, moving_lo, wait_k=None):
                w, k_all = q["w"], q["k"]
                for k in range(k_all):
                    if wait_k:
                        wait_k(k)
                    hi, lo = w_hi[s][:, k * P:(k + 1) * P], w_lo[s][:, k * P:(k + 1) * P]
                    for m, (wt, mv) in enumerate(((hi, moving_hi), (hi, moving_lo), (lo, moving_hi))):
                        for b, e in groups(w):
                            last = pe.matmul(slot_ps(s, w)[:, b:e], wt, mv[:, k, b:e],
                                             start=(k == 0 and m == 0), stop=(k == k_all - 1 and m == 2))
                last.then_inc(unit_done, 1)

            def gate_product(l):
                pe.wait_ge(gw_lo_ready, l + 1)
                for k in range(KD):
                    chunk_split(3 * l + 1, k)
                    for m, (wt, mv) in enumerate(((gw_hi, h_hi), (gw_hi, h_lo), (gw_lo, h_hi))):
                        for bank, b, e in ((7, 0, NX), (4, NX, T)):
                            last = pe.matmul(ps[0:GR, bank, 0:e - b], wt[:, k, :], mv[:, k, b:e],
                                             start=(k == 0 and m == 0), stop=(k == KD - 1 and m == 2))
                last.then_inc(gates_ready, 1)

            def gate_columns(l):
                pe.wait_ge(rows_act, 3 * (l + 1))
                pe.wait_ge(rows_dve, 3 * (l + 1))
                for r in range(5):
                    for ch in range(NCH):
                        first = r % 2 * NCH * ROWS + ch * ROWS
                        last = pe.transpose(ps[:, 5 + r // 2, first:first + ROWS], rq[:, r, ch, :], ident[0:ROWS, 0:ROWS])
                last.then_inc(cols_turned, 1)

            def turn_values(l):
                kv = phase("kv", l)
                for s in range(2):
                    pe.wait_ge(slot_read[s], phase("out", l)["p0"])
                pe.wait_ge(cols_ready, l + 1)
                for i in range(2 * TT):
                    if i >= 4:
                        pe.wait_ge(vk_read, 2 * TT * l + i - 3)
                    first, t = (2 * H, i) if i < TT else (H, i - TT)
                    for h in range(H):
                        last = pe.transpose(ps[:, 4 + i % 4, h * P:(h + 1) * P], qkvo[:, first + h, t * P:(t + 1) * P], ident[:])
                    last.then_inc(vk_turned, 1)
                pe.wait_ge(vk_read, 2 * TT * (l + 1))

            def scan_steps(l):
                def scores(st):
                    n, d, ch, t = st
                    o = outs_before(l, n)
                    tile = slice(t * P, (t + 1) * P)
                    if o:
                        pe.wait_ge(sw_ready, o)
                    for h in range(H):
                        last = pe.matmul(ps[:, 0, h * P:(h + 1) * P], qkvo[:, H + h, tile], qkvo[:, h, tile], start=True, stop=True)
                    last.then_inc(s_ready, 1)
                    if o:
                        pe.wait_ge(e_ready, o)
                    for h in range(H):
                        last = pe.matmul(ps[:, 1, h * P:(h + 1) * P], sel[:, d, h, :], r1_row[:, ch, :], start=True, stop=True)
                    last.then_inc(b_ready, 1)

                if gives(l, steps[0]):
                    scores(steps[0])
                for st in steps:
                    n, d, ch, t = st
                    o, kp = outs_before(l, n), count(kept, l, n)
                    tile = slice(t * P, (t + 1) * P)
                    if n + 1 < len(steps) and gives(l, steps[n + 1]):
                        scores(steps[n + 1])
                    if keeps(st):
                        pe.wait_ge(vw_ready, kp + 1)
                        if kp:
                            pe.wait_ge(state_ready, kp)
                        for h in range(H):
                            last = pe.matmul(head_ps(6, h), kt[:, t, h * P:(h + 1) * P], vw[n % 2][:, h, :], start=True, stop=True)
                        last.then_inc(dc_ready, 1)
                    if inters(l, st):
                        pe.wait_ge(state_ready, count(kept, l, n - 1))
                        it = count(inters, l, n)
                        if it:
                            pe.wait_ge(isb_ready, it)
                        for h in range(H):
                            last = pe.matmul(head_ps(4, h), qkvo[:, h, tile], state[d][:, h, :], start=True, stop=True)
                        last.then_inc(i_ready, 1)
                    if gives(l, st):
                        pe.wait_ge(sw_ready, o + 1)
                        if o:
                            pe.wait_ge(tot_ready, o)
                        for h in range(H):
                            last = pe.matmul(head_ps(2, h), sw[n % 2][:, h, :], vt[:, t, h, :], start=True, stop=True)
                        last.then_inc(n_ready, 1)

            def turn_mixer(l, w):
                pe.wait_ge(hm_scaled, l + 1)
                for h in range(H):
                    if h >= 2:
                        pe.wait_ge(ym_ready, H * l + h - 1)
                    for t in range(w // P):
                        last = pe.transpose(slot_ps(2 + h % 2, w)[:, t * P:(t + 1) * P], hm[:, t, h * P:(h + 1) * P], ident[:])
                    last.then_inc(hm_turned, 1)

            pe.wait_ge(const_ready, 4)
            pe.wait_ge(tab_loaded, 16 * TAB_DMAS)
            for l in range(DEPTH):
                pe.transpose(ps[:, 4, l * P:(l + 1) * P], tabs[:, l, :], ident[:])
                pe.transpose(ps[:, 4, (DEPTH + l) * P:(DEPTH + l) * P + TAPS * KC], tabs[0:TAPS * KC, DEPTH + l, :],
                             ident[0:TAPS * KC, 0:TAPS * KC])
            pe.transpose(ps[:, 5, 0:NCR], tabs[0:NCR, 2 * DEPTH, :], ident[0:NCR, 0:NCR]).then_inc(tab_turned, 1)
            pe.wait_ge(in_loaded, 32)
            for k in range(KD):
                if k >= 2:
                    pe.wait_ge(x_copied, k - 1)
                for t in range(TT):
                    last = pe.transpose(slot_ps(k % 2, T)[:, t * P:(t + 1) * P], tok[:, t, k * P:(k + 1) * P], ident[:])
                last.then_inc(x_turned, 1)
            pe.wait_ge(silu_ready, 1)
            for j in range(2):
                pe.wait_ge(first_mods[j], 16)
                for m in range(KD):
                    for k in range(KD):
                        last = pe.matmul(ps[:, 7, 2 * (j * KD + m):2 * (j * KD + m) + 2], m_first[j][:, k, m * P:(m + 1) * P],
                                         silu_c[:, k, :], start=(k == 0), stop=(k == KD - 1))
            last.then_inc(first_summed, 1)

            for q in phases:
                l, w, name = q["l"], q["w"], q["name"]
                moving = (a_hi, a_lo) if name == "down" else (h_hi, h_lo)
                wait_k = None
                if name == "up" and q["half"] == 0:
                    r = 3 * l + (0 if q["up"] is ffn1_up else 2)
                    norm_sums(r, w)
                    wait_k = lambda k, r=r: chunk_split(r, k)
                if name == "glu":
                    norm_sums(3 * l + 1, T)
                    gate_product(l)
                if name == "q":
                    gate_columns(l)
                if name == "out":
                    turn_values(l)
                    pe.wait_ge(yc_totalled, l + 1)
                    sums(chain_of_conv(l, 0), w)
                    pe.wait_ge(yc_summed, KC * (l + 1))
                    sums(chain_of_conv(l, 1), w)
                    scan_steps(l)
                    turn_mixer(l, w)
                    n = lows_before(split_of(l, "y"))
                    wait_k = lambda k, n=n: pe.wait_ge(h_lo_ready, n + k + 1)
                if name == "down":
                    n = KF * q["ups"] - KF
                    wait_k = lambda k, n=n: pe.wait_ge(a_lo_ready, n + k + 1)

                def pair(i, p, k_next, riders, wait_all=wait_k, q=q, moving=moving):
                    wait_k = wait_all if isinstance(i, int) and i == 0 else None
                    if riders and isinstance(i, int) and i == 0:
                        pe.wait_ge(mod_read, 1 + (q["p0"] > 0) + (q["mods"][0] > 0))
                    for s in range(2):
                        pe.wait_ge(lo_ready, p * 2 + (s + 1))
                        if not isinstance(p, int) or p > 0:
                            pe.wait_ge(slot_read[s], p)
                        unit(q, s, *moving, wait_k=wait_k if s == 0 else None)
                    for ml, mu, v, s in riders:
                        pe.wait_ge(mod_step, v * (2 * KD) + 2 * KD)
                        for o in range(2):
                            last = pe.matmul(ps[:, 7, bass.ds(mu * 2 + o, 1)], macc[s][:, o, :], ones[:, 0:1], start=True, stop=True)
                        last.then_inc(mod_summed, 1)

                run_pairs(pe, q, pair)

            norm_sums(3 * DEPTH, NX)
            for k in range(KD):
                pe.wait_ge(hf_ready, KD * 3 * DEPTH + k + 1)
                if k >= 2:
                    pe.wait_ge(out_read, k - 1)
                for t in range(TX):
                    last = pe.transpose(ps[:, 2 * (k % 2), t * P:(t + 1) * P], tmp[:, k % 4, t * P:(t + 1) * P], ident[:])
                last.then_inc(o_turned, 1)


_INS = ["x", "c", "ctx", "c_ctx", "w_mod", "b_mod", "norm_ffn1", "ffn1_up", "ffn1_down", "norm_mix", "w_in", "b_in",
        "mlstm_norm", "conv_w", "conv_b", "conv_norm_g", "conv_norm_b", "w_out", "norm_ffn2", "ffn2_up", "ffn2_down",
        "norm_final"]


def kernel(**inputs):
    import numpy as _np
    import concourse.bacc as _bacc
    from concourse import mybir as _mybir
    from concourse.bass_utils import run_bass_kernel_spmd as _run

    nc = _bacc.Bacc("TRN2", target_bir_lowering=False, num_devices=1)
    arrays, args = {}, []
    for name in _INS:
        a = _np.ascontiguousarray(inputs[name])
        arrays[f"in_{name}_dram"] = a
        args.append(nc.dram_tensor(f"in_{name}_dram", a.shape, _mybir.dt.from_np(a.dtype), kind="ExternalInput").ap())
    shape = inputs["x"].shape
    args.append(nc.dram_tensor("out_0_dram", shape, _mybir.dt.float32, kind="ExternalOutput").ap())
    mixer_dit_kernel(nc, *args)
    r = _run(nc, [arrays], core_ids=[0])
    return r.results[0]["out_0_dram"]
```

```python
import concourse.bass as bass
from concourse import mybir
from contextlib import ExitStack

F32 = mybir.dt.float32
F32R = mybir.dt.float32r
ALU = mybir.AluOpType
ACT = mybir.ActivationFunctionType
AX = mybir.AxisListType

P = 128
EPS = 1e-6
GRID_W = 64


def mixer_dit_kernel(nc, x, c, ctx_in, c_ctx, w_mod, b_mod, norm_ffn1, ffn1_up, ffn1_down, norm_mix, w_in, b_in,
                     mlstm_norm, conv_w, conv_b, conv_norm_g, conv_norm_b, w_out, norm_ffn2, ffn2_up, ffn2_down,
                     norm_final, out):
    _, NX, D = x.shape
    NC = ctx_in.shape[1]
    T = NX + NC
    DEPTH = w_mod.shape[0]
    KD = D // P
    NM = w_mod.shape[2] // P
    FF = ffn1_down.shape[1]
    KF = FF // P // 2
    DM = mlstm_norm.shape[1]
    H = DM // P
    KC = conv_norm_g.shape[1] // P
    TAPS = conv_w.shape[1]
    G0 = 4 * DM
    U0 = G0 + 4 * H
    TX, TT = NX // P, T // P
    NCH = TT
    CCH = NC // P
    E1 = P + 1
    ROWS = 32 + H
    GR = 96 + H
    R_CS, R_WK, R_INTER, R_EM, R_DEC = range(5)
    assert D == 2 * DM and H == 4 and KC == 4 and T == 768 and FF % (2 * P) == 0

    phases = []

    def add_phase(name, l, k, pairs, width, **more):
        before = sum(q["pairs"] for q in phases)
        phases.append(dict(name=name, l=l, k=k, pairs=pairs, w=width, p0=before, **more))

    for l in range(DEPTH):
        last = l == DEPTH - 1
        WL = NX if last else T
        for half in range(2):
            add_phase("up", l, KD, KF, T, up=ffn1_up, half=half)
            add_phase("down", l, KF, KD // 2, T, down=ffn1_down, half=half, gate=0, norm=3 * l + 1 if half else None)
        add_phase("q", l, KD, H // 2, WL)
        add_phase("glu", l, KD, KC, WL)
        add_phase("kv", l, KD, H, T)
        add_phase("o", l, KD, H // 2, WL)
        add_phase("out", l, KD, KD // 2, WL, gate=1, norm=3 * l + 2)
        for half in range(2):
            add_phase("up", l, KD, KF, WL, up=ffn2_up, half=half)
            add_phase("down", l, KF, KD // 2, WL, down=ffn2_down, half=half, gate=2, norm=3 * l + 3 if half else None)

    M0 = 2 * KD
    rides = {}
    ffn1_0 = [q for q in phases if q["l"] == 0 and q["name"] in ("up", "down")][:4]
    for q, ride in zip(ffn1_0, ((2, 2, 2), (4, 2, 4), (2, 2, 2))):
        rides[id(q)] = (0, ride)
    for l in range(1, DEPTH):
        before = [q for q in phases if q["l"] == l - 1 and q["name"] in ("up", "down")][4:]
        for q, ride in zip(before, ((2, 2, 2), (4, 4, 4), (2, 2, 2), (2, 4, 2))):
            rides[id(q)] = (l, ride)
    made, ridden = {l: M0 if l == 0 else 0 for l in range(DEPTH)}, 0
    for q in phases:
        if id(q) in rides:
            l, ride = rides[id(q)]
            n = ride[0] + ride[1] * (q["pairs"] - 2) + ride[2]
            q["mods"] = (l, ride, made[l], ridden, made[l] + n == NM)
            q["mods_first"] = made[l] == (M0 if l == 0 else 0)
            made[l] += n
            ridden += n
    assert all(n == NM for n in made.values())
    for n, q in enumerate(phases):
        q["next"] = phases[n + 1] if n + 1 < len(phases) else None
        q["ups"] = sum(1 for r in phases[:n] if r["name"] == "up")

    def ridden_after(q):
        _, ride, _, ridden0, _ = q["mods"]
        return ridden0 + ride[0] + ride[1] * (q["pairs"] - 2) + ride[2]

    def phase(name, l, nth=0):
        return [q for q in phases if q["name"] == name and q["l"] == l][nth]

    def width_of_norm(r):
        return NX if r >= 3 * (DEPTH - 1) + 2 else T

    def split_of(l, what):
        return 4 * l + {"ffn1": 0, "mix": 1, "y": 2, "ffn2": 3}[what]

    norm_place = {}
    for l in range(DEPTH):
        norm_place[3 * l], norm_place[3 * l + 1], norm_place[3 * l + 2] = (
            split_of(l, "ffn1"), split_of(l, "mix"), split_of(l, "ffn2"))

    def lows_before(m):
        return m * (KD // 2)

    def tile_of(d, ch):
        return (TX + ch if ch < CCH else ch - CCH) if d == 0 else TT - 1 - ch

    steps = [(2 * ch + d, d, ch, tile_of(d, ch)) for ch in range(NCH) for d in range(2)]

    def gives(l, step):
        return l < DEPTH - 1 or step[2] >= CCH

    def outs_before(l, n):
        return sum(gives(m, s) for m in range(l) for s in steps) + sum(gives(l, s) for s in steps[:n])

    def whole_at(l, n):
        return gives(l, steps[n]) and any(s[3] == steps[n][3] and gives(l, s) for s in steps[:n])

    def wholes_before(l, n):
        return sum(whole_at(m, k) for m in range(l) for k in range(len(steps))) + sum(whole_at(l, k) for k in range(n))

    def keeps(step):
        return step[2] < NCH - 1

    def kept(l, step):
        return keeps(step)

    def inters(l, step):
        return gives(l, step) and step[2] > 0

    def count(pred, l, n):
        return sum(pred(m, s) for m in range(l) for s in steps) + sum(pred(l, s) for s in steps[:n])

    with ExitStack() as stack:
        SB0 = 16512
        place = [SB0]

        def region(size):
            at = place[0]
            place[0] += (size + 31) // 32 * 32
            assert place[0] <= 229344, place[0]
            return at

        def at(name, shape, offset, dt=F32):
            return nc.alloc_sbuf_tensor_at(name, shape, dt, offset=offset)

        def sem(name):
            return stack.enter_context(nc.semaphore(name))

        r_x = region(KD * T * 4)
        r_h = region(2 * KD * T * 4)
        r_a = region(2 * KF * T * 4)
        UNIT = max(KD, KF) * P
        xres = at("xres", [P, KD, T], r_x)
        h_hi = at("h_hi", [P, KD, T], r_h, F32R)
        h_lo = at("h_lo", [P, KD, T], r_h + KD * T * 4, F32R)
        a_hi = at("a_hi", [P, KF, T], r_a, F32R)
        a_lo = at("a_lo", [P, KF, T], r_a + KF * T * 4, F32R)
        raw = [at(f"raw{s}", [P, UNIT], region(UNIT * 4)) for s in range(2)]
        w_hi = [at(f"w_hi{s}", [P, UNIT], region(UNIT * 4), F32R) for s in range(2)]
        w_lo = [at(f"w_lo{s}", [P, UNIT], region(UNIT * 4), F32R) for s in range(2)]
        r_m = region(KC * T * 4)
        tmp = at("tmp", [P, 4, T], region(4 * T * 4))
        ssum = at("ssum", [P, T], region(T * 4))
        ident = at("ident", [P, P], region(P * 4))
        ones = at("ones", [P, P], region(P * 4))
        sel = at("sel", [ROWS, 2, H, P], region(2 * H * P * 4))
        tab_a = at("tab_a", [P, DEPTH, P], region(DEPTH * P * 4))
        tab_b = at("tab_b", [P, DEPTH, TAPS * KC], region(DEPTH * TAPS * KC * 4))
        NCR = DEPTH * 2 * KC + 3 * KD
        tab_c = at("tab_c", [P, NCR], region(NCR * 4))
        coef = at("coef", [P, DEPTH, 3, 2, KD], region(DEPTH * 3 * 2 * KD * 4))
        shift = at("shift", [P, DEPTH, 3, 2, KD], region(DEPTH * 3 * 2 * KD * 4))
        gate = at("gate", [P, DEPTH, 3, 2, KD], region(DEPTH * 3 * 2 * KD * 4))
        silu_c = at("silu_c", [P, KD, 2], region(KD * 2 * 4))
        bq = at("bq", [P, DEPTH, H], region(DEPTH * H * 4))
        gbias = at("gbias", [P, DEPTH], region(DEPTH * 4))
        stat = at("stat", [P, 3, TT * H], region(3 * TT * H * 4))
        eps = at("eps", [P, 1], region(4))
        begun = at("begun", [P, 1], region(4))
        rsm = at("rsm", [ROWS, 3, NCH], region(3 * NCH * 4))
        qkvo = at("qkvo", [P, 4 * H, T], r_a)
        kt = at("kt", [P, TT, DM], r_a + 2 * H * T * 4)
        z = at("z", [P, KC, T], r_a + 4 * H * T * 4)
        r_left = r_a + (4 * H + KC) * T * 4
        r1_row = at("r1_row", [ROWS, NCH, P], r_left)
        col = at("col", [P, 5, NCH, 2, H], r_left + T * 4)
        rt = at("rt", [ROWS, 7, T], r_a + H * T * 4)
        rq = at("rq", [ROWS, 5, NCH, P], r_a + (H + 7) * T * 4)
        yc = at("yc", [P, KC, T], r_m)
        mraw = [at(f"mraw{s}", [P, KD, P], r_m + s * KD * P * 4) for s in range(2)]
        macc = [at(f"macc{s}", [P, 2, P], r_m + 2 * KD * P * 4 + s * 2 * P * 4) for s in range(2)]
        gw = at("gw", [P, KD, GR], r_m)
        gw_hi = at("gw_hi", [P, KD, GR], r_m + KD * GR * 4, F32R)
        gw_lo = at("gw_lo", [P, KD, GR], r_m + 2 * KD * GR * 4, F32R)
        gw16 = at("gw16", [P, KD, 4 * H], r_m + 3 * KD * GR * 4)
        HE = (H * E1 * 4 + 31) // 32 * 32
        vw = [at(f"vw{s}", [P, H, E1], r_h + s * HE) for s in range(2)]
        sw = [at(f"sw{s}", [P, H, P], r_h + 2 * HE + s * H * P * 4) for s in range(2)]
        r_h1 = r_h + KC * T * 4
        hm = at("hm", [P, TT, DM], r_h1)
        r_h2 = r_h + KD * T * 4
        vt = at("vt", [P, TT, H, E1], r_h2)
        state = [at(f"state{d}", [P, H, E1], r_h2 + (TT + d) * HE) for d in range(2)]
        isb = [at(f"isb{s}", [P, H, E1], r_h2 + (TT + 2 + s) * HE) for s in range(2)]
        r_h4 = r_h2 + (TT + 4) * HE
        ew = [at("ew0", [P, H, P], r_h + 2 * HE + 2 * H * P * 4), at("ew1", [P, H, P], r_h4)]
        assert r_h4 + H * P * 4 <= r_a
        tok = at("tok", [P, TT, D], r_a)
        tabs = at("tabs", [P, 2 * DEPTH + 1, P], r_a + TT * D * 4)
        m_first = [at("m_first0", [P, KD, KD * P], r_h),
                   at("m_first1", [P, KD, KD * P], r_a + TT * D * 4 + (2 * DEPTH + 1) * P * 4)]
        ACC = 3 * KD // 4
        m_acc = at("m_acc", [P, 2, ACC * P], r_h + KD * KD * P * 4)
        otok = at("otok", [P, TX, D], r_a)
        squares = tmp[:, 2, 0:H * P].rearrange("p (h e) -> p h e", h=H)
        tot = tmp[:, 0, 0:H * E1].rearrange("p (h e) -> p h e", h=H)

        ps = stack.enter_context(nc.psum_tensor("ps", [P, 8, 512], F32))

        def slot_ps(s, w):
            return ps[:, 2 * s:2 * s + 2, :].rearrange("p b n -> p (b n)")[:, 0:w]

        wide = ps[:, 5:7, :].rearrange("p b n -> p (b n)")

        def row(k):
            return rt[:, k, :] if k < 7 else tmp[0:ROWS, k - 5, :]

        def groups(w):
            return [(0, NX)] + ([(NX, T)] if w > NX else [])

        def pair_banks(b):
            return ps[:, b:b + 2, 0:2 * E1]

        def head_ps(b, h):
            return ps[:, b + h // 2, h % 2 * E1:h % 2 * E1 + E1]

        def flat2(t):
            return t.rearrange("p (b h) e -> p b (h e)", b=2)

        def chunk(t, j, w):
            if isinstance(j, int):
                return t[:, j, 0:w]
            return t[:, bass.ds(j, 1), 0:w].rearrange("p k n -> p (k n)")

        def column(t, j):
            return t[:, j:j + 1] if isinstance(j, int) else t[:, bass.ds(j, 1)]

        in_loaded = sem("in_loaded")
        cond_loaded = sem("cond_loaded")
        tab_loaded = sem("tab_loaded")
        bias_cleared = sem("bias_cleared")
        const_ready = sem("const_ready")
        const_cleared = sem("const_cleared")
        tab_turned = sem("tab_turned")
        tab_read = sem("tab_read")
        bq_ready = sem("bq_ready")
        silu_ready = sem("silu_ready")
        mod_loaded = [sem(f"mod_loaded{s}") for s in range(2)]
        mod_step = sem("mod_step")
        mod_summed = sem("mod_summed")
        mod_read = sem("mod_read")
        first_mods = [sem(f"first_mods{j}") for j in range(2)]
        first_chunks = [sem(f"first_chunks{j}") for j in range(KD // 2)]
        first_step = sem("first_step")
        first_summed = sem("first_summed")
        x_turned = sem("x_turned")
        x_copied = sem("x_copied")
        raw_loaded = [sem(f"raw_loaded{s}") for s in range(2)]
        hi_ready = sem("hi_ready")
        lo_ready = sem("lo_ready")
        unit_done = sem("unit_done")
        slot_read = [sem(f"slot_read{s}") for s in range(2)]
        a_hi_ready = sem("a_hi_ready")
        a_lo_ready = sem("a_lo_ready")
        latent_done = sem("latent_done")
        latent_read = sem("latent_read")
        latent_squared = sem("latent_squared")
        sq_ready = sem("sq_ready")
        ss_added = sem("ss_added")
        ss_summed = sem("ss_summed")
        root_begun = sem("root_begun")
        root_ready = sem("root_ready")
        inv_ready = sem("inv_ready")
        hf_ready = sem("hf_ready")
        h_rounded = sem("h_rounded")
        h_hi_ready = sem("h_hi_ready")
        h_lo_ready = sem("h_lo_ready")
        h_low_dve = sem("h_low_dve")
        dve_self = sem("dve_self")
        gw_loaded = sem("gw_loaded")
        gw_cleared = sem("gw_cleared")
        gw_ready = sem("gw_ready")
        gw_hi_ready = sem("gw_hi_ready")
        gw_lo_ready = sem("gw_lo_ready")
        gates_ready = sem("gates_ready")
        rows_dve = sem("rows_dve")
        rows_act = sem("rows_act")
        cols_turned = sem("cols_turned")
        cols_ready = sem("cols_ready")
        conv_step = sem("conv_step")
        yc_totalled = sem("yc_totalled")
        yc_dev = sem("yc_dev")
        yc_sq = sem("yc_sq")
        yc_summed = sem("yc_summed")
        yc_norm = sem("yc_norm")
        yc_act = sem("yc_act")
        vk_turned = sem("vk_turned")
        vk_read = sem("vk_read")
        ones_ready = sem("ones_ready")
        s_ready = sem("s_ready")
        b_ready = sem("b_ready")
        e_ready = sem("e_ready")
        mask_ready = sem("mask_ready")
        sw_ready = sem("sw_ready")
        vw_ready = sem("vw_ready")
        n_ready = sem("n_ready")
        i_ready = sem("i_ready")
        isb_ready = sem("isb_ready")
        dc_ready = sem("dc_ready")
        state_ready = sem("state_ready")
        tot_ready = sem("tot_ready")
        hm_whole = sem("hm_whole")
        hm_squared = sem("hm_squared")
        hm_root = sem("hm_root")
        hm_inverse = sem("hm_inverse")
        hm_scaled = sem("hm_scaled")
        hm_scaled_pool = sem("hm_scaled_pool")
        hm_turned = sem("hm_turned")
        ym_ready = sem("ym_ready")
        o_turned = sem("o_turned")
        out_read = sem("out_read")
        stored = sem("stored")

        A_N1 = NM
        A_NM, A_N2, A_MG = A_N1 + KD, A_N1 + 2 * KD, A_N1 + 3 * KD
        A_CB, A_CG, A_CN, A_BIN = A_MG + H, A_MG + H + KC, A_MG + H + 2 * KC, A_MG + H + 3 * KC
        assert A_BIN + 4 * H == P
        LAST_CHUNKS = KD // 2
        C_FIN = DEPTH * 2 * KC
        C_C = C_FIN + KD
        COND_DMAS = DEPTH + 3
        TAB_DMAS = DEPTH * (10 + 4)
        GATE_ROWS = (0, 64, 32, 96)

        def as_rows(v):
            return v.rearrange("(r f) -> r f", f=P)

        def weights_of(q, i, s):
            l, name = q["l"], q["name"]
            if name == "up":
                w, at_col = q["up"][l], i * P + (s * FF + q["half"] * KF * P)
            elif name == "down":
                w, at_col = q["down"][l][q["half"] * KF * P:(q["half"] + 1) * KF * P], i * (2 * P) + s * P
            elif name == "glu":
                w, at_col = w_in[l], i * P + (U0 + s * KC * P)
            elif name == "out":
                w, at_col = w_out[l], i * (2 * P) + s * P
            else:
                w, at_col = w_in[l], i * (2 * P) + ({"q": 0, "kv": DM, "o": 3 * DM}[name] + s * P)
            return w.rearrange("(k p) n -> p k n", p=P)[:, :, bass.ds(at_col, P)]

        def chain_of_norm(r):
            return 5 * (r // 3) + (0, 1, 4)[r % 3]

        def chain_of_conv(l, which):
            return 5 * l + 2 + which

        def groups_of(chain):
            l, which = divmod(chain, 5)
            w = phase("out", l)["w"] if which in (2, 3) else width_of_norm(3 * l + (0, 1, None, None, 2)[which])
            return len(groups(w))

        def sums_before(chain):
            return sum(groups_of(n) for n in range(chain))

        def roots_before(chain):
            return sum(groups_of(n) for n in range(chain) if n % 5 != 2)

        def ahead(q, i):
            return bool(q.get("norm")) and q["w"] > NX and isinstance(i, int) and i == q["pairs"] - 1

        def aheads_before(r):
            return sum(1 for q in phases if q.get("norm") and q["norm"] < r and q["w"] > NX)

        def run_pairs(engine, q, pair):
            n = q["pairs"]
            ml, ride, unit0, ridden0, _ = q.get("mods") or (0, (0, 0, 0), 0, 0, False)

            def riders(i, before, each):
                return [(ml, i * each + (unit0 + before + m), i * each + (ridden0 + before + m), (ridden0 + before + m) % 2)
                        for m in range(each)]

            pair(0, q["p0"], q["k"], riders(0, 0, ride[0]))
            if n > 2:
                with engine.Fori(1, n - 1) as i:
                    pair(i, i + q["p0"], q["k"], riders(i, ride[0] - ride[1], ride[1]))
            pair(n - 1, q["p0"] + n - 1, q["next"]["k"] if q["next"] else 0,
                 riders(0, ride[0] + ride[1] * (n - 2), ride[2]))

        def scale_head(engine, h, nt):
            head = hm[:, 0:nt, h * P:(h + 1) * P]
            by = stat[:, 2, 0:nt * H].rearrange("p (t h) -> p t h", h=H)[:, :, h:h + 1].to_broadcast([P, nt, P])
            return engine.tensor_tensor(head, head, by, ALU.mult)

        block = stack.enter_context(nc.Block())

        @block.sync
        def _(sp):
            for v, r in ((c[0], C_C), (c_ctx, C_C + KD), (norm_final, C_FIN)):
                sp.dma_start(tabs[r:r + KD, 2 * DEPTH, :], as_rows(v)).then_inc(cond_loaded, 16)
            for l in range(DEPTH):
                sp.dma_start(tabs[l * 2 * KC:(l + 1) * 2 * KC, 2 * DEPTH, :],
                             as_rows(b_in[l, U0:U0 + 2 * KC * P])).then_inc(cond_loaded, 16)
            mods = w_mod[0].rearrange("(k p) n -> p k n", p=P)
            sp.dma_start(m_first[0][:, :, 0:D // 2], mods[:, :, 0:D // 2]).then_inc(first_mods[0], 16)
            sp.dma_start(tok[:, 0:TX, :], x[0].rearrange("(t p) d -> p t d", p=P)).then_inc(in_loaded, 16)
            sp.dma_start(tok[:, TX:TT, :], ctx_in[0].rearrange("(t p) d -> p t d", p=P)).then_inc(in_loaded, 16)

            sp.dma_start(m_first[0][:, :, D // 2:D], mods[:, :, D // 2:D]).then_inc(first_mods[1], 16)
            for k in range(0, KD, 2):
                sp.dma_start(m_first[1][:, k:k + 2, :], mods[:, k:k + 2, D:2 * D]).then_inc(first_chunks[k // 2], 16)

            def load(q, i, s):
                sp.dma_start(raw[s][:, 0:q["k"] * P].rearrange("p (k n) -> p k n", n=P),
                             weights_of(q, i, s)).then_inc(raw_loaded[s], 16)

            for q in phases:
                first = 0
                if q["p0"] == 0:
                    load(q, 0, 0)
                    load(q, 0, 1)
                    first = 1
                if q["next"] and q["next"]["name"] == "q":
                    if first == 0:
                        for s in range(2):
                            sp.wait_ge(lo_ready, 2 * q["p0"] + s - 1)
                            load(q, 0, s)
                        first = 1
                    before = [r for r in phases if r.get("mods") and r["p0"] < q["p0"]][-1]
                    sp.wait_ge(mod_summed, ridden_after(before))
                    sp.dma_start(gw16[:], w_in[q["l"]].rearrange("(k p) n -> p k n", p=P)[:, :, G0:U0]).then_inc(gw_loaded, 16)
                with sp.Fori(first, q["pairs"]) as i:
                    for s in range(2):
                        sp.wait_ge(lo_ready, i * 2 + (2 * q["p0"] + s - 1))
                        load(q, i, s)

            sp.wait_ge(out_read, KD)
            for t in range(TX):
                sp.dma_start(out[0, t * P:(t + 1) * P, :], otok[:, t, :]).then_inc(stored, 16)
            sp.wait_ge(stored, 16 * TX)

        @block.gpsimd
        def _(pool):
            pool.memset(gbias[:], 0.0).then_inc(bias_cleared, 1)
            pool.memset(ident[:], 0.0).then_inc(const_cleared, 1)
            pool.memset(sel[:], 0.0).then_inc(const_cleared, 1)
            pool.memset(ones[:], 1.0).then_inc(const_ready, 1)
            pool.memset(eps[:], EPS).then_inc(const_ready, 1)
            pool.wait_ge(const_cleared, 2)
            pool.affine_select(out=ident[:], in_=ident[:], compare_op=ALU.not_equal, fill=1.0, base=0,
                               pattern=[[-1, P]], channel_multiplier=1).then_inc(const_ready, 1)
            pool.affine_select(out=sel[:], in_=sel[:], compare_op=ALU.not_equal, fill=1.0, base=0,
                               pattern=[[-32, 2], [-1, H], [0, P]], channel_multiplier=1).then_inc(const_ready, 1)

            def split_low(k, p, s):
                pool.wait_ge(hi_ready, p * 2 + (s + 1))
                pool.tensor_tensor(w_lo[s][:, 0:k * P], raw[s][:, 0:k * P], w_hi[s][:, 0:k * P].bitcast(F32),
                                   ALU.subtract).then_inc(lo_ready, 1)

            def add_square(r, j, s, w, first):
                pool.wait_ge(sq_ready, j + (KD * r + 1))
                if first:
                    if r:
                        if r % 3 == 2:
                            pool.wait_ge(yc_norm, KC * (r // 3 + 1))
                        else:
                            pool.wait_ge(hf_ready, KD * r)
                    pool.tensor_copy(ssum[:, 0:w], tmp[:, 2 + s, 0:w]).then_inc(ss_added, 1)
                else:
                    pool.wait_ge(ss_added, j + (KD - 2) * r)
                    pool.tensor_tensor(ssum[:, 0:w], ssum[:, 0:w], tmp[:, 2 + s, 0:w], ALU.add).then_inc(ss_added, 1)

            def norm_low(r):
                w, n = width_of_norm(r), KD * norm_place[r]
                with pool.Fori(0, KD // 4) as i:
                    for s in (1, 3):
                        pool.wait_ge(h_hi_ready, i * 4 + (n + s + 1))
                        j = i * 4 + s
                        pool.tensor_tensor(chunk(h_lo, j, w), tmp[:, s, 0:w], chunk(h_hi, j, w).bitcast(F32),
                                           ALU.subtract).then_inc(h_lo_ready, 1)

            def gate_weights(l):
                pool.wait_ge(gw_loaded, 16 * (l + 1))
                pool.memset(gw[:], 0.0).then_inc(gw_cleared, 1)
                pool.wait_ge(gw_cleared, l + 1)
                for j, row in enumerate(GATE_ROWS):
                    pool.tensor_copy(gw[:, :, row:row + H], gw16[:, :, j * H:(j + 1) * H]).then_inc(gw_ready, 1)
                pool.wait_ge(gw_hi_ready, l + 1)
                pool.tensor_tensor(gw_lo[:], gw[:], gw_hi[:].bitcast(F32), ALU.subtract).then_inc(gw_lo_ready, 1)

            def scan_steps(l):
                pool.wait_ge(vk_turned, 2 * TT * l + 1)
                pool.memset(vt[:, :, :, P:E1], 1.0).then_inc(ones_ready, 1)
                for st in steps:
                    n, d, ch, t = st
                    if keeps(st):
                        if n == 0:
                            pool.wait_ge(vk_read, 2 * TT * l + TT)
                            pool.wait_ge(ones_ready, l + 1)
                            pool.wait_ge(cols_ready, l + 1)
                        if n >= 2:
                            pool.wait_ge(dc_ready, count(kept, l, n - 1))
                        pool.tensor_tensor(vw[n % 2][:], vt[:, t, :, :],
                                           col[:, R_WK, ch, d, :].rearrange("p (h o) -> p h o", o=1).to_broadcast([P, H, E1]),
                                           ALU.mult).then_inc(vw_ready, 1)
                    if gives(l, st):
                        pool.wait_ge(e_ready, outs_before(l, n) + 1)
                        sign = 1 if d == 0 else -1
                        pool.affine_select(out=ew[n % 2][:], in_=ew[n % 2][:], compare_op=ALU.is_ge, fill=0.0, base=0,
                                           pattern=[[0, H], [sign, P]], channel_multiplier=-sign).then_inc(mask_ready, 1)

            def conv_squares(l, w):
                for k in range(KC):
                    pool.wait_ge(yc_sq, KC * l + k + 1)
                    if k == 0:
                        pool.wait_ge(ss_summed, sums_before(chain_of_conv(l, 1)))
                        pool.tensor_copy(ssum[:, 0:w], tmp[:, 2, 0:w]).then_inc(yc_summed, 1)
                    else:
                        pool.wait_ge(yc_summed, KC * l + k)
                        pool.tensor_tensor(ssum[:, 0:w], ssum[:, 0:w], tmp[:, 2 + k % 2, 0:w], ALU.add).then_inc(yc_summed, 1)

            def mixer_low(l, w):
                n = KD * split_of(l, "y")
                pool.wait_ge(hm_inverse, l + 1)
                for h in range(H // 2, H):
                    scale_head(pool, h, w // P).then_inc(hm_scaled_pool, 1)
                for k in range(H):
                    pool.wait_ge(h_hi_ready, n + k + 1)
                    pool.tensor_tensor(h_lo[:, k, 0:w], tmp[:, 2 + k % 2, 0:w], h_hi[:, k, 0:w].bitcast(F32), ALU.subtract).then_inc(h_lo_ready, 1)

            def load_mod(l, unit, s):
                pool.dma_start(mraw[s][:], w_mod[l].rearrange("(k p) n -> p k n", p=P)[:, :, bass.ds(unit * P, P)]).then_inc(mod_loaded[s], 16)

            for j in range(KD - 2):
                add_square(0, j, j % 2, T, j == 0)
            split_low(KD, 0, 0)
            split_low(KD, 0, 1)
            for q in phases:
                l, w, name = q["l"], q["w"], q["name"]
                if q.get("mods_first"):
                    if q["p0"]:
                        pool.wait_ge(h_low_dve, lows_before(split_of(l, "ffn2")))
                    for m in range(2):
                        load_mod(q["mods"][0], q["mods"][2] + m, m)
                if name == "up" and q["half"] == 0:
                    norm_low(3 * l + (0 if q["up"] is ffn1_up else 2))
                if name == "q":
                    norm_low(3 * l + 1)
                if name == "out":
                    scan_steps(l)
                    mixer_low(l, w)

                def pair(i, p, k_next, riders, q=q, l=l, w=w, name=name):
                    last_riders = q.get("mods") and q["mods"][4] and isinstance(i, int) and i > 0

                    def reload(some):
                        for ml, unit, v, s in some:
                            pool.wait_ge(mod_step, v * (2 * KD) + 2 * KD)
                            load_mod(ml, unit + 2, s)

                    if last_riders:
                        riders = riders[:-2]
                    if name == "o" and i == 1:
                        conv_squares(l, w)
                    late = name == "up" and isinstance(i, int) and i == 0
                    if not late:
                        reload(riders[:2])
                    if k_next:
                        split_low(k_next, p + 1, 0)
                    if late:
                        reload(riders[:2])
                    ends = isinstance(i, int) and i > 0
                    if q.get("norm") and not ends:
                        add_square(q["norm"], i * 2, 0, w, isinstance(i, int) and i == 0)
                    reload(riders[2:])
                    if k_next:
                        split_low(k_next, p + 1, 1)
                    if q.get("norm") and not ends:
                        add_square(q["norm"], i * 2 + 1, 1, w, False)
                    if isinstance(i, int) and i == 0 and q["next"] and q["next"]["name"] == "q":
                        gate_weights(l)

                run_pairs(pool, q, pair)

        @block.scalar
        def _(act):
            def split_high(k, p, s):
                act.wait_ge(raw_loaded[s], p * 16 + 16)
                if not isinstance(p, int) or p > 0:
                    act.wait_ge(unit_done, p * 2 + (s - 1))
                act.activation(w_hi[s][:, 0:k * P], raw[s][:, 0:k * P], ACT.Copy).then_inc(hi_ready, 1)

            def square(r, j, s, w):
                if not (isinstance(j, int) and j < 2):
                    act.wait_ge(ss_added, j + ((KD - 2) * r - 1))
                act.activation(tmp[:, 2 + s, 0:w], chunk(xres, j, w), ACT.Square).then_inc(sq_ready, 1)

            roots_begun = [0]

            def begin_root():
                if roots_begun[0]:
                    act.wait_ge(root_begun, roots_begun[0])
                act.activation(begun[:], eps[:], ACT.Sqrt).then_inc(root_begun, 1)
                roots_begun[0] += 1

            def root(chain, w, scale, sums=wide, which=(0, 1)):
                for o, (b, e) in enumerate(groups(w)):
                    if o in which:
                        act.wait_ge(ss_summed, sums_before(chain) + o + 1)
                        act.activation(ssum[:, b:e], sums[:, b:e], ACT.Sqrt, scale=scale, bias=eps[:]).then_inc(root_ready, 1)

            def norm_root(r):
                w = width_of_norm(r)
                root(chain_of_norm(r), w, 1.0 / D, which=(1,) if r and w > NX else (0, 1))

            def norm_high(r):
                w = width_of_norm(r)
                l, which = divmod(r, 3)
                for j in range(KD):
                    act.wait_ge(hf_ready, KD * r + j + 1)
                    s = j % 4
                    for o, (b, e) in enumerate(groups(w)):
                        last = act.activation(h_hi[:, j, b:e], tmp[:, s, b:e], ACT.Identity, bias=shift[:, l, which, o, j:j + 1])
                    if s % 2:
                        last.then_inc(h_rounded, 1)
                        act.wait_ge(h_rounded, KD // 2 * r + j // 2 + 1)
                        for o, (b, e) in enumerate(groups(w)):
                            last = act.activation(tmp[:, s, b:e], tmp[:, s, b:e], ACT.Identity, bias=shift[:, l, which, o, j:j + 1])
                    last.then_inc(h_hi_ready, 1)

            def forget_rows(l):
                act.wait_ge(rows_dve, 3 * l + 1)
                act.activation(rt[:, 6, :], rt[:, 5, :], ACT.Exp, scale=-1.0).then_inc(rows_act, 1)
                act.wait_ge(rows_act, 3 * l + 1)
                act.activation(rt[:, 5, :], rt[:, 6, :], ACT.Ln, bias=ones[0:ROWS, 0:1]).then_inc(rows_act, 1)

            def exponential_rows(l):
                act.wait_ge(rows_dve, 3 * l + 2)
                for r, src, scale in ((R_WK, rt[:, 1, :], 1.0), (R_INTER, rt[:, 5, :], 1.0), (R_EM, rt[:, 4, :], -1.0),
                                      (R_DEC, None, 1.0)):
                    if src is None:
                        src = rsm[:, 2, :].rearrange("r (c o) -> r c o", o=1).to_broadcast([ROWS, NCH, P])
                    else:
                        src = src.rearrange("r (c n) -> r c n", n=P)
                    act.activation(rq[0:32, r, :, :], src[0:32], ACT.Exp, scale=scale)
                    last = act.activation(rq[32:ROWS, r, :, ::-1], src[32:ROWS], ACT.Exp, scale=scale)
                last.then_inc(rows_act, 1)

            def turned_values(l):
                for i in range(2 * TT):
                    act.wait_ge(vk_turned, 2 * TT * l + i + 1)
                    bank = ps[:, 4 + (i + 1) % 4, :]
                    if i < TT:
                        act.activation(vt[:, i, :, 0:P], bank.rearrange("p (h e) -> p h e", h=H), ACT.Copy).then_inc(vk_read, 1)
                    else:
                        act.activation(kt[:, i - TT, :], bank, ACT.Copy).then_inc(vk_read, 1)

            def conv_squares(l, w):
                for k in range(KC):
                    act.wait_ge(yc_dev, KC * l + k + 1)
                    if k >= 2:
                        act.wait_ge(yc_summed, KC * l + k - 1)
                    act.activation(tmp[:, 2 + k % 2, 0:w], yc[:, k, 0:w], ACT.Square).then_inc(yc_sq, 1)

            def head_squares(l, n):
                t = steps[n][3]
                if not whole_at(l, n):
                    return
                act.wait_ge(hm_whole, wholes_before(l, n) + 1)
                if wholes_before(l, n):
                    act.wait_ge(hm_squared, wholes_before(l, n))
                for h in range(H):
                    last = act.activation(squares[:, h, :], hm[:, t, h * P:(h + 1) * P], ACT.Square,
                                          accum_out=stat[:, 1, t * H + h:t * H + h + 1])
                last.then_inc(hm_squared, 1)

            def conv_out(l, w):
                for k in range(KC):
                    act.wait_ge(yc_norm, KC * l + k + 1)
                    act.activation(yc[:, k, 0:w], yc[:, k, 0:w], ACT.Silu, scale=tab_a[:, l, A_CG + k:A_CG + k + 1],
                                   bias=tab_a[:, l, A_CN + k:A_CN + k + 1]).then_inc(yc_act, 1)

            def scan_steps(l):
                def weights(st):
                    n, d, ch, t = st
                    o = outs_before(l, n)
                    act.wait_ge(b_ready, o + 1)
                    if o >= 2:
                        act.wait_ge(sw_ready, o - 1)
                    for h in range(H):
                        last = act.activation(ew[n % 2][:, h, :], ps[:, 1, h * P:(h + 1) * P], ACT.Exp,
                                              bias=col[:, R_CS, ch, d, h:h + 1])
                    last.then_inc(e_ready, 1)

                act.wait_ge(cols_ready, l + 1)
                if gives(l, steps[0]):
                    weights(steps[0])
                for st in steps:
                    n, d, ch, t = st
                    if n + 1 < len(steps) and gives(l, steps[n + 1]):
                        weights(steps[n + 1])
                    if n == len(steps) - 1:
                        begin_root()
                    if inters(l, st):
                        act.wait_ge(i_ready, count(inters, l, n) + 1)
                        if outs_before(l, n) >= 2:
                            act.wait_ge(tot_ready, outs_before(l, n) - 1)
                        for h in range(H):
                            last = act.activation(isb[n % 2][:, h, :], head_ps(4, h), ACT.Copy,
                                                  scale=col[:, R_INTER, ch, d, h:h + 1])
                        last.then_inc(isb_ready, 1)
                    if n:
                        head_squares(l, n - 1)
                head_squares(l, len(steps) - 1)

            def mixer_high(l, w):
                act.wait_ge(hm_squared, wholes_before(l + 1, 0))
                m = w // P * H
                act.activation(stat[:, 0, 0:m], stat[:, 1, 0:m], ACT.Sqrt, scale=1.0 / P, bias=eps[:]).then_inc(hm_root, 1)
                conv_out(l, w)
                for k in range(KD):
                    if k < H:
                        act.wait_ge(ym_ready, H * l + k + 1)
                        src = tmp[:, 2 + k % 2, 0:w]
                    else:
                        act.wait_ge(hm_turned, H * (l + 1))
                        act.wait_ge(yc_act, KC * (l + 1))
                        src = yc[:, k - H, 0:w]
                    act.activation(h_hi[:, k, 0:w], src, ACT.Copy).then_inc(h_hi_ready, 1)

            act.wait_ge(const_ready, 4)
            act.wait_ge(tab_read, 1)
            act.activation(silu_c[:], tab_c[:, C_C:C_C + 2 * KD].rearrange("p (o k) -> p k o", o=2), ACT.Silu).then_inc(silu_ready, 1)
            act.wait_ge(bias_cleared, 1)
            for l in range(DEPTH):
                for j, row in enumerate(GATE_ROWS):
                    act.dma_start(gbias[row:row + H, l:l + 1],
                                   b_in[l, G0 + j * H:G0 + (j + 1) * H].rearrange("(h o) -> h o", o=1)).then_inc(tab_loaded, 16)
                r = 0
                for v in (b_mod[l], norm_ffn1[l], norm_mix[l], norm_ffn2[l], mlstm_norm[l], conv_b[l],
                          conv_norm_g[l], conv_norm_b[l], b_in[l, 0:G0]):
                    n = v.shape[0] // P
                    act.dma_start(tabs[r:r + n, l, :], as_rows(v)).then_inc(tab_loaded, 16)
                    r += n
                act.dma_start(tabs[0:TAPS * KC, DEPTH + l, :],
                               conv_w[l].rearrange("t (c f) -> (t c) f", f=P)).then_inc(tab_loaded, 16)

            for j in range(KD):
                act.wait_ge(x_copied, j + 1)
                square(0, j, j % 2, T)
            begin_root()
            split_high(KD, 0, 0)
            split_high(KD, 0, 1)

            for q in phases:
                l, w, name = q["l"], q["w"], q["name"]
                if name == "up" and q["half"] == 0:
                    r = 3 * l + (0 if q["up"] is ffn1_up else 2)
                    norm_root(r)
                    norm_high(r)
                if name == "q":
                    norm_root(3 * l + 1)
                    norm_high(3 * l + 1)
                if name == "glu":
                    exponential_rows(l)
                if name == "out":
                    begin_root()
                    root(chain_of_conv(l, 1), w, 1.0 / (KC * P), slot_ps(1, w))
                    turned_values(l)
                    scan_steps(l)
                    mixer_high(l, w)

                def evacuate(i, s, q=q, l=l, w=w, name=name):
                    if name == "q":
                        func, scale, bias, to = ACT.Identity, float(P) ** -0.5, column(bq[:, l, :], i * 2 + s), i * 2 + s
                    elif name == "kv":
                        func, scale, bias, to = ACT.Identity, 1.0, column(tab_a[:, l, :], i * 2 + (A_BIN + H + s)), i * 2 + (H + s)
                    else:
                        func, scale, bias, to = ACT.Sigmoid, 1.0, column(tab_a[:, l, :], i * 2 + (A_BIN + 3 * H + s)), i * 2 + (3 * H + s)
                    act.activation(chunk(qkvo, to, w), slot_ps(s, w), func, scale=scale, bias=bias).then_inc(slot_read[s], 1)

                def last_before_norm(p, k_next, q=q, w=w):
                    r = q["norm"]
                    n = 2 * aheads_before(r)
                    for s in range(2):
                        act.wait_ge(latent_read, n + s + 1)
                        act.wait_ge(ss_added, KD - 2 + s + ((KD - 2) * r - 1))
                        act.activation(tmp[:, 2 + s, 0:NX], xres[:, KD - 2 + s, 0:NX], ACT.Square).then_inc(latent_squared, 1)
                    begin_root()
                    for s in range(2):
                        act.wait_ge(unit_done, p * 2 + 1 + s)
                        if s == 0 and k_next:
                            split_high(k_next, p + 1, 0)
                        act.wait_ge(slot_read[s], p + 1)
                        act.activation(tmp[:, 2 + s, NX:T], xres[:, KD - 2 + s, NX:T], ACT.Square).then_inc(sq_ready, 1)
                        if s == 0:
                            root(chain_of_norm(r), w, 1.0 / D, which=(0,))
                    split_high(k_next, p + 1, 1)

                def pair(i, p, k_next, riders, q=q, l=l, w=w, name=name, evacuate=evacuate):
                    if ahead(q, i):
                        last_before_norm(p, k_next)
                        return
                    if name == "o" and i == 1:
                        conv_squares(l, w)
                    act.wait_ge(unit_done, p * 2 + 1)
                    early = name == "up" and isinstance(i, int) and i == 0
                    if early:
                        split_high(k_next, p + 1, 0)
                    if name == "up":
                        act.activation(tmp[:, 0, 0:w], slot_ps(0, w), ACT.Silu).then_inc(slot_read[0], 1)
                    if name in ("q", "kv", "o"):
                        evacuate(i, 0)
                    if k_next and not early:
                        split_high(k_next, p + 1, 0)
                    if q.get("norm"):
                        act.wait_ge(slot_read[0], p + 1)
                        square(q["norm"], i * 2, 0, w)
                    last_squares = q.get("norm") and isinstance(i, int) and i > 0
                    if last_squares:
                        begin_root()
                    act.wait_ge(unit_done, p * 2 + 2)
                    if name == "glu":
                        if not isinstance(i, int) or i > 0:
                            act.wait_ge(slot_read[0], p)
                        act.activation(tmp[:, 0, 0:w], slot_ps(1, w), ACT.Sigmoid,
                                       bias=column(tab_c, i + (l * 2 * KC + KC))).then_inc(slot_read[1], 1)
                    if name in ("q", "kv", "o"):
                        evacuate(i, 1)
                    if last_squares:
                        act.wait_ge(slot_read[1], p + 1)
                        square(q["norm"], i * 2 + 1, 1, w)
                    if k_next:
                        split_high(k_next, p + 1, 1)
                    if name == "up":
                        act.wait_ge(slot_read[1], p + 1)
                        act.activation(chunk(a_hi, i, w), tmp[:, 1, 0:w], ACT.Copy).then_inc(a_hi_ready, 1)
                    if q.get("norm") and not last_squares:
                        act.wait_ge(slot_read[1], p + 1)
                        square(q["norm"], i * 2 + 1, 1, w)
                    if name == "q" and i == 0:
                        forget_rows(l)
                    if isinstance(i, int) and i == 0 and q["next"] and q["next"]["name"] == "q":
                        act.wait_ge(gw_ready, 4 * (l + 1))
                        act.activation(gw_hi[:], gw[:], ACT.Copy).then_inc(gw_hi_ready, 1)

                run_pairs(act, q, pair)

            norm_root(3 * DEPTH)
            for k in range(KD):
                act.wait_ge(o_turned, k + 1)
                act.activation(otok[:, :, k * P:(k + 1) * P], ps[:, 2 * (k % 2), :].rearrange("p (t f) -> p t f", t=TX),
                               ACT.Copy).then_inc(out_read, 1)

        @block.vector
        def _(dve):
            self_count = [0]

            def settle(ins):
                self_count[0] += 1
                ins.then_inc(dve_self, 1)
                dve.wait_ge(dve_self, self_count[0])

            def reciprocals(chain, w, which=(0, 1)):
                for o, (b, e) in enumerate(groups(w)):
                    if o in which:
                        dve.wait_ge(root_ready, roots_before(chain) + o + 1)
                        dve.reciprocal(ssum[:, b:e], ssum[:, b:e]).then_inc(inv_ready, 1)

            def norm(r):
                w = width_of_norm(r)
                l, which = divmod(r, 3)
                if w == NX:
                    reciprocals(chain_of_norm(r), w)
                q = [q for q in phases if q["name"] in ("up", "q") and q["l"] == l and q.get("half", 0) == 0][which]
                if q["ups"]:
                    dve.wait_ge(a_lo_ready, KF * q["ups"])
                n = lows_before(norm_place[r])

                def scaled(i, s, first, which_groups=(0, 1)):
                    j = i * 4 + s
                    if not first:
                        if s % 2:
                            dve.wait_ge(h_lo_ready, i * 2 + (n + s // 2 - 1))
                        else:
                            dve.wait_ge(h_low_dve, i * 2 + (n + s // 2 - 1))
                    for o, (b, e) in enumerate(groups(w)):
                        if o not in which_groups:
                            continue
                        if first and s == 0:
                            dve.wait_ge(inv_ready, roots_before(chain_of_norm(r)) + o + 1)
                        last = dve.scalar_tensor_tensor(tmp[:, s, b:e], xres[:, bass.ds(j, 1), b:e].rearrange("p k n -> p (k n)"),
                                                        column(coef[:, l, which, o, :], j), ssum[:, b:e], ALU.mult, ALU.mult)
                        if o == len(groups(w)) - 1:
                            last.then_inc(hf_ready, 1)

                def low(i, s):
                    j = i * 4 + s
                    dve.wait_ge(h_hi_ready, i * 4 + (KD * norm_place[r] + s + 1))
                    for o, (b, e) in enumerate(groups(w)):
                        last = dve.scalar_tensor_tensor(h_lo[:, bass.ds(j, 1), b:e].rearrange("p k n -> p (k n)"), tmp[:, s, b:e],
                                                        column(shift[:, l, which, o, :], j),
                                                        h_hi[:, bass.ds(j, 1), b:e].rearrange("p k n -> p (k n)").bitcast(F32),
                                                        ALU.add, ALU.subtract)
                    last.then_inc(h_low_dve, 1)

                def chunks(i, first):
                    if first:
                        scaled(i, 0, first, (0,))
                        scaled(i, 1, first, (0,))
                        if r and w > NX:
                            reciprocals(chain_of_norm(r), w, (1,))
                        if w > NX:
                            scaled(i, 0, first, (1,))
                            scaled(i, 1, first, (1,))
                    else:
                        scaled(i, 0, first)
                        scaled(i, 1, first)
                    low(i, 0)
                    scaled(i, 2, first)
                    scaled(i, 3, first)
                    low(i, 2)

                chunks(0, True)
                with dve.Fori(1, KD // 4) as i:
                    chunks(i, False)

            def gate_rows(l):
                settle(dve.memset(rt[:, 0:2, :], 0.0))
                for k, first in ((0, 0), (1, 64)):
                    for d in range(2):
                        src = slice(first + 32 * d, first + 32 * d + H)
                        to = slice(32 * d, 32 * d + H)
                        if k == 0 and d == 0:
                            dve.wait_ge(gates_ready, l + 1)
                        for bank, b, e in ((4, 0, NC), (7, NC, T)):
                            got = ps[src, bank, 0:e - b]
                            settle(dve.tensor_scalar(rt[to, k, b:e], got if d == 0 else got[:, ::-1], gbias[src, l:l + 1],
                                                     None, ALU.add))
                dve.scalar_tensor_tensor(rt[:, 5, :], rt[:, 1, :], -1.0, rt[:, 1, :], ALU.mult, ALU.max).then_inc(rows_dve, 1)
                dve.wait_ge(rows_act, 3 * l + 2)
                settle(dve.memset(rt[:, 6, :], 1.0))
                settle(dve.memset(rt[:, 6, :].rearrange("r (c n) -> r c n", n=P)[:, :, 0:1], 0.0))
                settle(dve.scalar_tensor_tensor(rt[:, 2, :], rt[:, 1, :], 0.0, rt[:, 5, :], ALU.min, ALU.subtract))
                settle(dve.tensor_tensor_scan(rt[:, 3, :], rt[:, 6, :], rt[:, 2, :], 0.0, ALU.mult, ALU.add))
                settle(dve.tensor_tensor_scan(rt[:, 4, :], rt[:, 2, :], rt[:, 0, :], 0.0, ALU.add, ALU.max))
                settle(dve.tensor_tensor(row(8), rt[:, 3, :], rt[:, 4, :], ALU.subtract))
                settle(dve.tensor_tensor(row(7), rt[:, 0, :], rt[:, 3, :], ALU.subtract))

                def by_chunk(k):
                    return row(k).rearrange("r (c n) -> r c n", n=P)

                def spread(k):
                    return rsm[:, k, :].rearrange("r (c o) -> r c o", o=1).to_broadcast([ROWS, NCH, P])

                settle(dve.memset(rsm[:, 0, 0:1], 0.0))
                settle(dve.tensor_copy(rsm[:, 0, 1:NCH], by_chunk(4)[:, 0:NCH - 1, P - 1]))
                settle(dve.tensor_copy(rsm[:, 1, :], by_chunk(8)[:, :, P - 1]))
                settle(dve.tensor_tensor(rsm[:, 2, :], rsm[:, 1, :], rsm[:, 0, :], ALU.add))
                settle(dve.tensor_tensor(by_chunk(5), by_chunk(8), spread(0), ALU.add))
                dve.tensor_tensor(by_chunk(1), by_chunk(7), spread(1), ALU.add).then_inc(rows_dve, 1)
                for k, to in ((8, r1_row[:]), (7, rq[:, R_CS, :, :])):
                    dve.tensor_copy(to[0:32], by_chunk(k)[0:32])
                    last = dve.tensor_copy(to[32:ROWS, :, ::-1], by_chunk(k)[32:ROWS])
                last.then_inc(rows_dve, 1)

            def gate_columns(l):
                dve.wait_ge(cols_turned, l + 1)
                for r in range(5):
                    got = ps[:, 5 + r // 2, r % 2 * NCH * ROWS:(r % 2 + 1) * NCH * ROWS].rearrange("p (c g) -> p c g", g=ROWS)
                    for d in range(2):
                        last = dve.tensor_copy(col[:, r, :, d, :], got[:, :, 32 * d:32 * d + H])
                last.then_inc(cols_ready, 1)

            conv_count = [0]
            mid = TAPS // 2
            tap_order = [mid] + [j for j in range(TAPS) if j != mid]
            grid_rows = NX // GRID_W

            def tap(l, k, j, to, src, first):
                weight = column(tab_b[:, l, :], k + j * KC)
                if first:
                    return dve.tensor_scalar(to, src, weight, column(tab_a[:, l, :], k + A_CB), ALU.mult, ALU.add)
                return dve.scalar_tensor_tensor(to, src, weight, to, ALU.mult, ALU.add)

            def convolve_latent(l, along, taps):
                zx = lambda t, k: t[:, k, 0:NX].rearrange("p (r c) -> p r c", c=GRID_W)
                k0 = 0 if along == "columns" else KC // 2
                n = GRID_W if along == "columns" else grid_rows
                for j in taps:
                    o = j - mid
                    b, e = max(0, -o), min(n, n - o)
                    for k in (k0, k0 + 1):
                        if j != mid:
                            dve.wait_ge(conv_step, conv_count[0] - 1)
                        if along == "columns":
                            to, src = zx(yc, k)[:, :, b:e], zx(z, k)[:, :, b + o:e + o]
                        else:
                            to, src = zx(yc, k)[:, b:e, :], zx(z, k)[:, b + o:e + o, :]
                        tap(l, k, j, to, src, j == mid).then_inc(conv_step, 1)
                        conv_count[0] += 1

            def convolve_context(l):
                base = conv_count[0]
                with dve.Fori(0, KC // 2) as i:
                    for m, j in enumerate(tap_order):
                        o = j - mid
                        b, e = max(0, -o), min(NC, NC - o)
                        for s in range(2):
                            if m:
                                dve.wait_ge(conv_step, i * (2 * TAPS) + (base + 2 * m + s - 1))
                            k = i * 2 + s
                            part = lambda t, b, e: t[:, bass.ds(k, 1), NX + b:NX + e].rearrange("p k n -> p (k n)")
                            tap(l, k, j, part(yc, b, e), part(z, b + o, e + o), m == 0).then_inc(conv_step, 1)
                conv_count[0] += KC * TAPS

            def conv_mean(l, w):
                dve.wait_ge(conv_step, conv_count[0])
                dve.wait_ge(hf_ready, KD * (3 * l + 2))
                settle(dve.tensor_tensor(ssum[:, 0:w], yc[:, 0, 0:w], yc[:, 1, 0:w], ALU.add))
                settle(dve.tensor_tensor(ssum[:, 0:w], ssum[:, 0:w], yc[:, 2, 0:w], ALU.add))
                dve.tensor_tensor(ssum[:, 0:w], ssum[:, 0:w], yc[:, 3, 0:w], ALU.add).then_inc(yc_totalled, 1)
                chain = chain_of_conv(l, 0)
                dve.wait_ge(ss_summed, sums_before(chain + 1))
                for k in range(KC):
                    dve.scalar_tensor_tensor(yc[:, k, 0:w], wide[:, 0:w], -1.0 / (KC * P), yc[:, k, 0:w],
                                             ALU.mult, ALU.add).then_inc(yc_dev, 1)

            def conv_scale(l, w):
                chain = chain_of_conv(l, 1)
                reciprocals(chain, w)
                dve.wait_ge(inv_ready, roots_before(chain + 1))
                for k in range(KC):
                    dve.tensor_tensor(yc[:, k, 0:w], yc[:, k, 0:w], ssum[:, 0:w], ALU.mult).then_inc(yc_norm, 1)

            def scan_steps(l):
                touched = set()

                def weighted(st):
                    n, d, ch, t = st
                    o = outs_before(l, n)
                    dve.wait_ge(mask_ready, o + 1)
                    dve.wait_ge(s_ready, o + 1)
                    if o >= 2:
                        dve.wait_ge(n_ready, o - 1)
                    dve.tensor_tensor(sw[n % 2][:].rearrange("p h t -> p (h t)"),
                                      ew[n % 2][:].rearrange("p h t -> p (h t)"), ps[:, 0, :], ALU.mult).then_inc(sw_ready, 1)

                if gives(l, steps[0]):
                    weighted(steps[0])
                for st in steps:
                    n, d, ch, t = st
                    o, kp = outs_before(l, n), count(kept, l, n)
                    if keeps(st):
                        dve.wait_ge(dc_ready, kp + 1)
                        if inters(l, st):
                            dve.wait_ge(i_ready, count(inters, l, n) + 1)
                        if ch == 0:
                            dve.tensor_copy(flat2(state[d][:]), pair_banks(6)).then_inc(state_ready, 1)
                        else:
                            dve.wait_ge(state_ready, kp - 1)
                            for h in range(H):
                                last = dve.scalar_tensor_tensor(state[d][:, h, :], state[d][:, h, :], col[:, R_DEC, ch, d, h:h + 1],
                                                                head_ps(6, h), ALU.mult, ALU.add)
                            last.then_inc(state_ready, 1)
                    if n + 1 < len(steps) and gives(l, steps[n + 1]):
                        weighted(steps[n + 1])
                    if gives(l, st):
                        dve.wait_ge(n_ready, o + 1)
                        if inters(l, st):
                            dve.wait_ge(isb_ready, count(inters, l, n) + 1)
                            total = dve.tensor_tensor(flat2(tot), pair_banks(2), flat2(isb[n % 2][:]), ALU.add)
                        else:
                            total = dve.tensor_copy(flat2(tot), pair_banks(2))
                        total.then_inc(tot_ready, 1)
                        dve.wait_ge(tot_ready, o + 1)
                        den = tot[:, :, P:E1].rearrange("p h o -> p (h o)")
                        settle(dve.scalar_tensor_tensor(stat[:, 2, 0:H], den, -1.0, den, ALU.mult, ALU.max))
                        settle(dve.tensor_tensor(stat[:, 2, 0:H], stat[:, 2, 0:H], col[:, R_EM, ch, d, :], ALU.max))
                        settle(dve.reciprocal(stat[:, 2, H:2 * H], stat[:, 2, 0:H]))
                        for h in range(H):
                            to = hm[:, t, h * P:(h + 1) * P]
                            by = stat[:, 2, H + h:H + h + 1]
                            if t in touched:
                                last = dve.scalar_tensor_tensor(to, tot[:, h, 0:P], by, to, ALU.mult, ALU.add)
                            else:
                                last = dve.tensor_scalar(to, tot[:, h, 0:P], by, None, ALU.mult)
                        settle(last)
                        if whole_at(l, n):
                            dve.sem_inc(hm_whole, 1)
                        touched.add(t)

            def mixer_out(l, w):
                nt = w // P
                dve.wait_ge(hm_root, l + 1)
                dve.reciprocal(stat[:, 2, 0:nt * H], stat[:, 0, 0:nt * H]).then_inc(hm_inverse, 1)
                dve.wait_ge(hm_inverse, l + 1)
                for h in range(H // 2):
                    scale_head(dve, h, nt).then_inc(hm_scaled, 1)
                for h in range(H):
                    dve.wait_ge(hm_turned, H * l + h + 1)
                    if h >= 2:
                        dve.wait_ge(h_lo_ready, lows_before(split_of(l, "y")) + h - 1)
                    dve.scalar_tensor_tensor(tmp[:, 2 + h % 2, 0:w], slot_ps(2 + h % 2, w), tab_a[:, l, A_MG + h:A_MG + h + 1],
                                             qkvo[:, 3 * H + h, 0:w], ALU.mult, ALU.mult).then_inc(ym_ready, 1)
                for k in range(H, KD):
                    dve.wait_ge(h_hi_ready, KD * split_of(l, "y") + k + 1)
                    dve.tensor_tensor(h_lo[:, k, 0:w], yc[:, k - H, 0:w], h_hi[:, k, 0:w].bitcast(F32), ALU.subtract).then_inc(h_low_dve, 1)

            dve.wait_ge(tab_turned, 1)
            dve.tensor_copy(tab_c[:], ps[:, 5, 0:NCR]).then_inc(tab_read, 1)
            for k in range(KD):
                dve.wait_ge(x_turned, k + 1)
                dve.tensor_copy(xres[:, k, :], slot_ps(k % 2, T)).then_inc(x_copied, 1)
            dve.wait_ge(silu_ready, 1)
            for k in range(KD):
                if k % 2 == 0:
                    dve.wait_ge(first_chunks[k // 2], 16)
                for o in range(2):
                    if k == 0:
                        step = dve.tensor_scalar(m_acc[:, o, :], m_first[1][:, k, 0:ACC * P], silu_c[:, k, o:o + 1], None, ALU.mult)
                    else:
                        dve.wait_ge(first_step, 2 * k + o - 1)
                        step = dve.scalar_tensor_tensor(m_acc[:, o, :], m_first[1][:, k, 0:ACC * P], silu_c[:, k, o:o + 1],
                                                        m_acc[:, o, :], ALU.mult, ALU.add)
                    step.then_inc(first_step, 1)
            def modulation(l, vectors):
                first, end = min(vectors) * KD, (max(vectors) + 1) * KD
                mod = tmp[:, 1, 0:2 * NM].rearrange("p (m o) -> p m o", o=2)
                settle(dve.tensor_tensor(mod[:, first:end, :], ps[:, 7, 2 * first:2 * end].rearrange("p (m o) -> p m o", o=2),
                                         tab_a[:, l, first:end].rearrange("p (m o) -> p m o", o=1).to_broadcast([P, end - first, 2]),
                                         ALU.add))
                for j in vectors:
                    which, kind = divmod(j, 3)
                    gain = (A_N1, A_NM, A_N2)[which]
                    for o in range(2):
                        part = mod[:, j * KD:(j + 1) * KD, o]
                        if kind == 0:
                            last = dve.tensor_copy(shift[:, l, which, o, :], part)
                        elif kind == 1:
                            last = dve.scalar_tensor_tensor(coef[:, l, which, o, :], part, 1.0, tab_a[:, l, gain:gain + KD],
                                                            ALU.add, ALU.mult)
                        else:
                            last = dve.tensor_scalar(gate[:, l, which, o, :], part, 1.0 if which == 1 else 0.5, None, ALU.mult)
                last.then_inc(mod_read, 1)
                mod_reads[0] += 1
                dve.wait_ge(mod_read, mod_reads[0])

            mod_reads = [0]

            def mod_units(riders):
                for ml, unit, v, s in riders:
                    dve.wait_ge(mod_loaded[s], (v - s) * 8 + 16)
                    if not isinstance(v, int) or v >= 2:
                        dve.wait_ge(mod_summed, v - 1)
                    for k in range(KD):
                        for o in range(2):
                            to, by = macc[s][:, o, :], silu_c[:, k, o:o + 1]
                            if k == 0:
                                step = dve.tensor_scalar(to, mraw[s][:, k, :], by, None, ALU.mult)
                            else:
                                dve.wait_ge(mod_step, v * (2 * KD) + (2 * k + o - 1))
                                step = dve.scalar_tensor_tensor(to, mraw[s][:, k, :], by, to, ALU.mult, ALU.add)
                            step.then_inc(mod_step, 1)

            dve.wait_ge(tab_turned, 2)
            dve.tensor_copy(tab_a[:], ps[:, 4, 0:DEPTH * P].rearrange("p (l n) -> p l n", l=DEPTH)).then_inc(tab_read, 1)
            for l in range(DEPTH):
                last = dve.tensor_copy(tab_b[:, l, :], ps[:, 4, (DEPTH + l) * P:(DEPTH + l) * P + TAPS * KC])
            last.then_inc(tab_read, 1)
            dve.wait_ge(tab_read, 3)
            dve.tensor_scalar(bq[:], tab_a[:, :, A_BIN:A_BIN + H], float(P) ** -0.5, None, ALU.mult).then_inc(bq_ready, 1)

            reciprocals(0, T)
            dve.wait_ge(first_summed, 1)
            modulation(0, (0, 1))

            for q in phases:
                l, w, name = q["l"], q["w"], q["name"]
                if name == "up" and q["half"] == 0:
                    norm(3 * l + (0 if q["up"] is ffn1_up else 2))
                if name == "q":
                    norm(3 * l + 1)
                    gate_rows(l)
                if name == "kv":
                    convolve_latent(l, "columns", tap_order[2 * (TAPS // 3):])
                    convolve_latent(l, "rows", [j for j in tap_order if abs(j - mid) < grid_rows])
                    if phase("glu", l)["w"] > NX:
                        convolve_context(l)
                if name == "o":
                    conv_mean(l, w)
                if name == "out":
                    conv_scale(l, w)
                    scan_steps(l)
                    mixer_out(l, w)

                def residual(q, s, j, o, b, e):
                    to = xres[:, j, b:e] if isinstance(j, int) else xres[:, bass.ds(j, 1), b:e].rearrange("p k n -> p (k n)")
                    return dve.scalar_tensor_tensor(to, slot_ps(s, q["w"])[:, b:e], column(gate[:, q["l"], q["gate"], o, :], j),
                                                    to, ALU.mult, ALU.add)

                def last_before_norm(p, q=q, w=w):
                    r = q["norm"]
                    for s in range(2):
                        dve.wait_ge(latent_done, 2 * aheads_before(r) + s + 1)
                        residual(q, s, KD - 2 + s, 0, 0, NX).then_inc(latent_read, 1)
                    for s in range(2):
                        dve.wait_ge(unit_done, p * 2 + 1 + s)
                        residual(q, s, KD - 2 + s, 1, NX, T).then_inc(slot_read[s], 1)
                        if s == 0:
                            reciprocals(chain_of_norm(r), w, (0,))

                def pair(i, p, k_next, riders, q=q, l=l, w=w, name=name):
                    mod_units(riders[:2])
                    if ahead(q, i):
                        last_before_norm(p)
                        return
                    if name == "up":
                        dve.wait_ge(slot_read[0], p + 1)
                        dve.wait_ge(unit_done, p * 2 + 2)
                        if q["ups"] or not isinstance(i, int) or i > 0:
                            dve.wait_ge(a_lo_ready, i + KF * q["ups"])
                        dve.tensor_tensor(tmp[:, 1, 0:w], tmp[:, 0, 0:w], slot_ps(1, w), ALU.mult).then_inc(slot_read[1], 1)
                        dve.wait_ge(a_hi_ready, i + (KF * q["ups"] + 1))
                        dve.tensor_tensor(chunk(a_lo, i, w), tmp[:, 1, 0:w], chunk(a_hi, i, w).bitcast(F32),
                                          ALU.subtract).then_inc(a_lo_ready, 1)
                    if name == "glu":
                        dve.wait_ge(slot_read[1], p + 1)
                        dve.scalar_tensor_tensor(chunk(z, i, w), slot_ps(0, w), column(tab_c, i + l * 2 * KC), tmp[:, 0, 0:w],
                                                 ALU.add, ALU.mult).then_inc(slot_read[0], 1)
                    if name in ("down", "out"):
                        for s in range(2):
                            if s == 1:
                                mod_units(riders[2:])
                            dve.wait_ge(unit_done, p * 2 + (s + 1))
                            j = i * 2 + s
                            for o, (b, e) in enumerate(groups(w)):
                                last = residual(q, s, j, o, b, e)
                            last.then_inc(slot_read[s], 1)

                if name == "glu":
                    for i in range(q["pairs"]):
                        pair(i, q["p0"] + i, 0, [])
                        if i == 0:
                            gate_columns(l)
                        if i >= q["pairs"] - 3 and i < q["pairs"] - 1:
                            part = i - (q["pairs"] - 3)
                            dve.wait_ge(slot_read[0], q["p0"] + i + 1)
                            convolve_latent(l, "columns", tap_order[part * (TAPS // 3):(part + 1) * (TAPS // 3)])
                elif name not in ("q", "kv", "o"):
                    run_pairs(dve, q, pair)
                if q.get("mods"):
                    ml, _, _, _, ends = q["mods"]
                    dve.wait_ge(mod_summed, ridden_after(q))
                    if ends or q is phases[0]:
                        dve.wait_ge(a_lo_ready, KF * (q["ups"] + (name == "up")))
                    if q is phases[0]:
                        modulation(0, (2,))
                    elif ends:
                        modulation(ml, tuple(range(3, 9)) if ml == 0 else tuple(range(9)))

            r = 3 * DEPTH
            reciprocals(chain_of_norm(r), NX)
            dve.wait_ge(a_lo_ready, KF * (phases[-1]["ups"]))
            dve.wait_ge(inv_ready, roots_before(chain_of_norm(r)) + 1)
            for k in range(KD):
                if k >= 4:
                    dve.wait_ge(o_turned, k - 3)
                dve.scalar_tensor_tensor(tmp[:, k % 4, 0:NX], xres[:, k, 0:NX], tab_c[:, C_FIN + k:C_FIN + k + 1],
                                         ssum[:, 0:NX], ALU.mult, ALU.mult).then_inc(hf_ready, 1)

        @block.tensor
        def _(pe):
            def add_part(w, part, to=wide, first=True, last=True, which=(0, 1)):
                for o, (b, e) in enumerate(groups(w)):
                    if o in which:
                        step = pe.matmul(to[:, b:e], ones[:], part[:, b:e], start=first, stop=last)
                        if last:
                            step.then_inc(ss_summed, 1)

            def norm_sums(r, w, which=(0, 1)):
                pe.wait_ge(ss_added, (KD - 2) * (r + 1))
                add_part(w, ssum[:], last=False, which=which)
                if which == (0,):
                    pe.wait_ge(latent_squared, 2 * (aheads_before(r) + 1))
                else:
                    pe.wait_ge(sq_ready, KD * (r + 1))
                add_part(w, tmp[:, 2, :], first=False, last=False, which=which)
                add_part(w, tmp[:, 3, :], first=False, which=which)

            def chunk_split(r, k):
                if k % 2:
                    pe.wait_ge(h_lo_ready, lows_before(norm_place[r]) + (k + 1) // 2)
                else:
                    pe.wait_ge(h_low_dve, lows_before(norm_place[r]) + k // 2 + 1)

            def units(q, slots, moving_hi, moving_lo, wait_k=None, which=(0, 1)):
                w, k_all = q["w"], q["k"]
                turns = k_all - LAST_CHUNKS
                order = [(k, (s,)) for k in range(turns) for s in slots] + [(k, (s,)) for s in slots for k in range(turns, k_all)]
                for k, ss in order:
                    if wait_k and ss[0] == slots[0]:
                        wait_k(k)
                    for s in ss:
                        hi, lo = w_hi[s][:, k * P:(k + 1) * P], w_lo[s][:, k * P:(k + 1) * P]
                        for m, (wt, mv) in enumerate(((hi, moving_hi), (hi, moving_lo), (lo, moving_hi))):
                            for o, (b, e) in enumerate(groups(w)):
                                if o in which:
                                    last = pe.matmul(slot_ps(s, w)[:, b:e], wt, mv[:, k, b:e],
                                                     start=(k == 0 and m == 0), stop=(k == k_all - 1 and m == 2))
                        if k == k_all - 1:
                            last.then_inc(latent_done if which == (0,) else unit_done, 1)

            def gate_product(l, k):
                if k == 0:
                    pe.wait_ge(gw_lo_ready, l + 1)
                for m, (wt, mv) in enumerate(((gw_hi, h_hi), (gw_hi, h_lo), (gw_lo, h_hi))):
                    for bank, b, e in ((7, 0, NX), (4, NX, T)):
                        last = pe.matmul(ps[0:GR, bank, 0:e - b], wt[:, k, :], mv[:, k, b:e],
                                         start=(k == 0 and m == 0), stop=(k == KD - 1 and m == 2))
                if k == KD - 1:
                    last.then_inc(gates_ready, 1)

            def gate_columns(l):
                pe.wait_ge(rows_act, 3 * (l + 1))
                pe.wait_ge(rows_dve, 3 * (l + 1))
                for r in range(5):
                    for ch in range(NCH):
                        first = r % 2 * NCH * ROWS + ch * ROWS
                        last = pe.transpose(ps[:, 5 + r // 2, first:first + ROWS], rq[:, r, ch, :], ident[0:ROWS, 0:ROWS])
                last.then_inc(cols_turned, 1)

            def turn_values(l):
                for s in range(2):
                    pe.wait_ge(slot_read[s], phase("out", l)["p0"])
                pe.wait_ge(cols_ready, l + 1)
                for i in range(2 * TT):
                    if i >= 4:
                        pe.wait_ge(vk_read, 2 * TT * l + i - 3)
                    first, t = (2 * H, i) if i < TT else (H, i - TT)
                    for h in range(H):
                        last = pe.transpose(ps[:, 4 + (i + 1) % 4, h * P:(h + 1) * P], qkvo[:, first + h, t * P:(t + 1) * P], ident[:])
                    last.then_inc(vk_turned, 1)
                pe.wait_ge(vk_read, 2 * TT * (l + 1))

            def scan_steps(l):
                def scores(st):
                    n, d, ch, t = st
                    o = outs_before(l, n)
                    tile = slice(t * P, (t + 1) * P)
                    if o:
                        pe.wait_ge(e_ready, o)
                    for h in range(H):
                        last = pe.matmul(ps[:, 1, h * P:(h + 1) * P], sel[:, d, h, :], r1_row[:, ch, :], start=True, stop=True)
                    last.then_inc(b_ready, 1)
                    if o:
                        pe.wait_ge(sw_ready, o)
                    for h in range(H):
                        last = pe.matmul(ps[:, 0, h * P:(h + 1) * P], qkvo[:, H + h, tile], qkvo[:, h, tile], start=True, stop=True)
                    last.then_inc(s_ready, 1)

                if gives(l, steps[0]):
                    scores(steps[0])
                for st in steps:
                    n, d, ch, t = st
                    o, kp = outs_before(l, n), count(kept, l, n)
                    tile = slice(t * P, (t + 1) * P)
                    if n + 1 < len(steps) and gives(l, steps[n + 1]):
                        scores(steps[n + 1])
                    if keeps(st):
                        pe.wait_ge(vw_ready, kp + 1)
                        if kp:
                            pe.wait_ge(state_ready, kp)
                        for h in range(H):
                            last = pe.matmul(head_ps(6, h), kt[:, t, h * P:(h + 1) * P], vw[n % 2][:, h, :], start=True, stop=True)
                        last.then_inc(dc_ready, 1)
                    if inters(l, st):
                        pe.wait_ge(state_ready, count(kept, l, n - 1))
                        it = count(inters, l, n)
                        if it:
                            pe.wait_ge(isb_ready, it)
                        for h in range(H):
                            last = pe.matmul(head_ps(4, h), qkvo[:, h, tile], state[d][:, h, :], start=True, stop=True)
                        last.then_inc(i_ready, 1)
                    if gives(l, st):
                        pe.wait_ge(sw_ready, o + 1)
                        if o:
                            pe.wait_ge(tot_ready, o)
                        for h in range(H):
                            last = pe.matmul(head_ps(2, h), sw[n % 2][:, h, :], vt[:, t, h, :], start=True, stop=True)
                        last.then_inc(n_ready, 1)

            def turn_mixer(l, w):
                for h in range(H):
                    pe.wait_ge(hm_scaled if h < H // 2 else hm_scaled_pool, H // 2 * l + h % (H // 2) + 1)
                    if h >= 2:
                        pe.wait_ge(ym_ready, H * l + h - 1)
                    for t in range(w // P):
                        last = pe.transpose(slot_ps(2 + h % 2, w)[:, t * P:(t + 1) * P], hm[:, t, h * P:(h + 1) * P], ident[:])
                    last.then_inc(hm_turned, 1)

            pe.wait_ge(const_ready, 4)
            pe.wait_ge(cond_loaded, 16 * COND_DMAS)
            pe.transpose(ps[:, 5, 0:NCR], tabs[0:NCR, 2 * DEPTH, :], ident[0:NCR, 0:NCR]).then_inc(tab_turned, 1)

            def first_vector(half):
                pe.wait_ge(first_mods[half], 16)
                for m in range(half * KD // 2, (half + 1) * KD // 2):
                    for k in range(KD):
                        pe.matmul(ps[:, 7, 2 * m:2 * m + 2], m_first[0][:, k, m * P:(m + 1) * P], silu_c[:, k, :],
                                  start=(k == 0), stop=(k == KD - 1))

            pe.wait_ge(silu_ready, 1)
            first_vector(0)
            pe.wait_ge(in_loaded, 32)
            for k in range(KD):
                if k >= 2:
                    pe.wait_ge(x_copied, k - 1)
                for t in range(TT):
                    last = pe.transpose(slot_ps(k % 2, T)[:, t * P:(t + 1) * P], tok[:, t, k * P:(k + 1) * P], ident[:])
                last.then_inc(x_turned, 1)
            first_vector(1)
            pe.wait_ge(tab_loaded, 16 * TAB_DMAS)
            for l in range(DEPTH):
                pe.transpose(ps[:, 4, l * P:(l + 1) * P], tabs[:, l, :], ident[:])
                last = pe.transpose(ps[:, 4, (DEPTH + l) * P:(DEPTH + l) * P + TAPS * KC], tabs[0:TAPS * KC, DEPTH + l, :],
                                    ident[0:TAPS * KC, 0:TAPS * KC])
            last.then_inc(tab_turned, 1)
            norm_sums(0, T)
            for done in first_chunks:
                pe.wait_ge(done, 16)
            for m in range(ACC, KD):
                for k in range(KD):
                    pe.matmul(ps[:, 7, 2 * (KD + m):2 * (KD + m) + 2], m_first[1][:, k, m * P:(m + 1) * P], silu_c[:, k, :],
                              start=(k == 0), stop=(k == KD - 1))
            pe.wait_ge(first_step, 2 * KD)
            for m in range(ACC):
                for o in range(2):
                    last = pe.matmul(ps[:, 7, 2 * (KD + m) + o:2 * (KD + m) + o + 1], m_acc[:, o, m * P:(m + 1) * P], ones[:, 0:1],
                                     start=True, stop=True)
            last.then_inc(first_summed, 1)

            pe.wait_ge(tab_read, 3)
            for q in phases:
                l, w, name = q["l"], q["w"], q["name"]
                moving = (a_hi, a_lo) if name == "down" else (h_hi, h_lo)
                wait_k = None
                if name == "up" and q["half"] == 0:
                    r = 3 * l + (0 if q["up"] is ffn1_up else 2)
                    if r:
                        norm_sums(r, w, (1,) if w > NX else (0, 1))
                    wait_k = lambda k, r=r: chunk_split(r, k)
                if name == "q":
                    norm_sums(3 * l + 1, T, (1,))

                    def wait_k(k, l=l):
                        chunk_split(3 * l + 1, k)
                        gate_product(l, k)
                if name == "out":
                    pe.wait_ge(yc_summed, KC * (l + 1))
                    pe.wait_ge(slot_read[1], q["p0"])
                    add_part(w, ssum[:], to=slot_ps(1, T))
                    turn_values(l)
                    pe.wait_ge(root_ready, roots_before(chain_of_conv(l, 1) + 1))
                    scan_steps(l)
                    turn_mixer(l, w)
                    n = lows_before(split_of(l, "y"))
                    wait_k = lambda k, n=n: pe.wait_ge(h_lo_ready if k < H else h_low_dve, n + k % H + 1)
                if name == "down":
                    n = KF * q["ups"] - KF
                    wait_k = lambda k, n=n: pe.wait_ge(a_lo_ready, n + k + 1)

                def pair(i, p, k_next, riders, wait_all=wait_k, q=q, moving=moving):
                    wait_k = wait_all if isinstance(i, int) and i == 0 else None
                    if riders and isinstance(i, int) and i == 0:
                        pe.wait_ge(mod_read, 1 + (q["p0"] > 0) + (q["mods"][0] > 0))
                    if q["name"] == "o" and i == 1:
                        pe.wait_ge(yc_totalled, q["l"] + 1)
                        add_part(q["w"], ssum[:])
                    def sum_riders(some):
                        for ml, mu, v, s in some:
                            pe.wait_ge(mod_step, v * (2 * KD) + 2 * KD)
                            for o in range(2):
                                last = pe.matmul(ps[:, 7, bass.ds(mu * 2 + o, 1)], macc[s][:, o, :], ones[:, 0:1], start=True, stop=True)
                            last.then_inc(mod_summed, 1)

                    together = wait_k and q["name"] in ("up", "out")
                    for s in range(2):
                        pe.wait_ge(lo_ready, p * 2 + (s + 1))
                        if not isinstance(p, int) or p > 0:
                            pe.wait_ge(slot_read[s], p)
                        if ahead(q, i):
                            units(q, (s,), *moving, which=(0,))
                        elif not together:
                            units(q, (s,), *moving, wait_k=wait_k if s == 0 else None)
                            if s == 0:
                                sum_riders(riders[:-2])
                    if together:
                        units(q, (0, 1), *moving, wait_k=wait_k)
                    if ahead(q, i):
                        units(q, (0,), *moving, which=(1,))
                        norm_sums(q["norm"], q["w"], (0,))
                        units(q, (1,), *moving, which=(1,))
                    sum_riders(riders[:-2] if together else [])
                    sum_riders(riders[-2:])
                    if q["name"] == "glu" and isinstance(i, int) and i == 0:
                        gate_columns(q["l"])

                run_pairs(pe, q, pair)

            norm_sums(3 * DEPTH, NX)
            for k in range(KD):
                pe.wait_ge(hf_ready, KD * 3 * DEPTH + k + 1)
                if k >= 2:
                    pe.wait_ge(out_read, k - 1)
                for t in range(TX):
                    last = pe.transpose(ps[:, 2 * (k % 2), t * P:(t + 1) * P], tmp[:, k % 4, t * P:(t + 1) * P], ident[:])
                last.then_inc(o_turned, 1)


_INS = ["x", "c", "ctx", "c_ctx", "w_mod", "b_mod", "norm_ffn1", "ffn1_up", "ffn1_down", "norm_mix", "w_in", "b_in",
        "mlstm_norm", "conv_w", "conv_b", "conv_norm_g", "conv_norm_b", "w_out", "norm_ffn2", "ffn2_up", "ffn2_down",
        "norm_final"]


def kernel(**inputs):
    import numpy as _np
    import concourse.bacc as _bacc
    from concourse import mybir as _mybir
    from concourse.bass_utils import run_bass_kernel_spmd as _run

    nc = _bacc.Bacc("TRN2", target_bir_lowering=False, num_devices=1)
    arrays, args = {}, []
    for name in _INS:
        a = _np.ascontiguousarray(inputs[name])
        arrays[f"in_{name}_dram"] = a
        args.append(nc.dram_tensor(f"in_{name}_dram", a.shape, _mybir.dt.from_np(a.dtype), kind="ExternalInput").ap())
    shape = inputs["x"].shape
    args.append(nc.dram_tensor("out_0_dram", shape, _mybir.dt.float32, kind="ExternalOutput").ap())
    mixer_dit_kernel(nc, *args)
    r = _run(nc, [arrays], core_ids=[0])
    return r.results[0]["out_0_dram"]
```
